# Optimizing a Trainium2 kernel written in Bass

```python
import math
import jax, jax.numpy as jnp
from jax import lax
import numpy as np

D_MODEL = 1024
BATCH = 1
SEQ = 256
DEPTH = 4

HEAD_DIM = 64
N_HEADS = D_MODEL // HEAD_DIM
SWA_KV_HEADS = max(1, N_HEADS // 8)
N_MIXERS = 3
SB_BLOCK = 128
MOBA_BLOCK = 256
MOBA_TOPK = 3
MOBA_QCHUNK = 16
SWA_WINDOW = 128
ROPE_THETA = 10000.0
D_FF = -(-8 * D_MODEL // (3 * 256)) * 256
EPS = 1e-6


def rms_norm(x, gain):
    xf = x.astype(jnp.float32)
    var = jnp.mean(xf * xf, axis=-1, keepdims=True)
    return (xf * lax.rsqrt(var + EPS)).astype(x.dtype) * gain

def modulate(h, shift, scale):
    return h * (1.0 + scale) + shift

def split_heads(t, n):
    b, s, _ = t.shape
    return t.reshape(b, s, n, HEAD_DIM).transpose(0, 2, 1, 3)

def merge_heads(t):
    b, n, s, d = t.shape
    return t.transpose(0, 2, 1, 3).reshape(b, s, n * d)

def rope_tables(seq_len):
    inv_freq = 1.0 / (ROPE_THETA ** (jnp.arange(0, HEAD_DIM, 2, dtype=jnp.float32) / HEAD_DIM))
    ang = jnp.arange(seq_len, dtype=jnp.float32)[:, None] * inv_freq[None, :]
    return jnp.cos(ang), jnp.sin(ang)

def apply_rope(x, cos, sin):
    cos = cos.astype(x.dtype)
    sin = sin.astype(x.dtype)
    x1, x2 = jnp.split(x, 2, axis=-1)
    return jnp.concatenate([x1 * cos - x2 * sin, x2 * cos + x1 * sin], axis=-1)

def stick_breaking_attention(h, w_in, w_out):
    b, s_len, _ = h.shape
    q, k, v = jnp.split(h @ w_in, 3, axis=-1)
    q, k, v = split_heads(q, N_HEADS), split_heads(k, N_HEADS), split_heads(v, N_HEADS)
    nblk = s_len // SB_BLOCK
    q_blocks = q.reshape(b, N_HEADS, nblk, SB_BLOCK, HEAD_DIM).transpose(2, 0, 1, 3, 4)
    k_pos = jnp.arange(s_len)
    scale = HEAD_DIM ** -0.5

    def block(args):
        qb, bi = args
        q_pos = bi * SB_BLOCK + jnp.arange(SB_BLOCK)
        z = jnp.einsum('bhqd,bhkd->bhqk', qb, k).astype(jnp.float32) * scale
        past = k_pos[None, :] < q_pos[:, None]
        log_beta = jax.nn.log_sigmoid(z)
        log_keep = jnp.where(past, jax.nn.log_sigmoid(-z), 0.0)
        later = lax.cumsum(log_keep, axis=3, reverse=True) - log_keep
        a = jnp.where(past, jnp.exp(log_beta + later), 0.0)
        return jnp.einsum('bhqk,bhkd->bhqd', a.astype(v.dtype), v)

    o = lax.map(block, (q_blocks, jnp.arange(nblk)))
    o = o.transpose(1, 2, 0, 3, 4).reshape(b, N_HEADS, s_len, HEAD_DIM)
    return merge_heads(o) @ w_out

def moba_attention(h, w_in, qk_gain, w_out, cos, sin):
    b, s_len, _ = h.shape
    q, k, v = jnp.split(h @ w_in, 3, axis=-1)
    q, k, v = split_heads(q, N_HEADS), split_heads(k, N_HEADS), split_heads(v, N_HEADS)
    q = apply_rope(rms_norm(q, qk_gain[0]), cos, sin)
    k = apply_rope(rms_norm(k, qk_gain[1]), cos, sin)
    pad = (-s_len) % MOBA_BLOCK
    padw = ((0, 0), (0, 0), (0, pad), (0, 0))
    q, k, v = jnp.pad(q, padw), jnp.pad(k, padw), jnp.pad(v, padw)
    s_pad = s_len + pad
    nb = s_pad // MOBA_BLOCK
    topk = min(MOBA_TOPK, nb)
    k_blk = k.reshape(b, N_HEADS, nb, MOBA_BLOCK, HEAD_DIM)
    v_blk = v.reshape(b, N_HEADS, nb, MOBA_BLOCK, HEAD_DIM)
    k_mean = jnp.mean(k_blk.astype(jnp.float32), axis=3).astype(k.dtype)
    n_chunks = s_pad // MOBA_QCHUNK
    q_chunks = q.reshape(b, N_HEADS, n_chunks, MOBA_QCHUNK, HEAD_DIM).transpose(2, 0, 1, 3, 4)
    b_idx = jnp.arange(b)[:, None, None, None]
    h_idx = jnp.arange(N_HEADS)[None, :, None, None]
    blk_ids = jnp.arange(nb)
    in_blk = jnp.arange(MOBA_BLOCK)
    scale = HEAD_DIM ** -0.5

    def chunk(args):
        qc, ci = args
        q_pos = ci * MOBA_QCHUNK + jnp.arange(MOBA_QCHUNK)
        own = (ci * MOBA_QCHUNK) // MOBA_BLOCK
        gate = jnp.einsum('bhqd,bhnd->bhqn', qc, k_mean).astype(jnp.float32)
        gate = jnp.where(blk_ids < own, gate, -jnp.inf)
        top_val, top_idx = lax.top_k(gate, topk)
        sel_ok = jnp.isfinite(top_val)
        kg = k_blk[b_idx, h_idx, top_idx]
        vg = v_blk[b_idx, h_idx, top_idx]
        s_sel = jnp.einsum('bhqd,bhqnkd->bhqnk', qc, kg).astype(jnp.float32) * scale
        s_sel = jnp.where(sel_ok[..., None], s_sel, -jnp.inf)
        k_own = lax.dynamic_slice_in_dim(k, own * MOBA_BLOCK, MOBA_BLOCK, axis=2)
        v_own = lax.dynamic_slice_in_dim(v, own * MOBA_BLOCK, MOBA_BLOCK, axis=2)
        s_own = jnp.einsum('bhqd,bhkd->bhqk', qc, k_own).astype(jnp.float32) * scale
        own_pos = own * MOBA_BLOCK + in_blk
        s_own = jnp.where(own_pos[None, :] <= q_pos[:, None], s_own, -jnp.inf)
        qn = qc.shape[2]
        logits = jnp.concatenate([s_sel.reshape(b, N_HEADS, qn, topk * MOBA_BLOCK), s_own], axis=-1)
        p = jax.nn.softmax(logits, axis=-1).astype(v.dtype)
        p_sel = p[..., :topk * MOBA_BLOCK].reshape(b, N_HEADS, qn, topk, MOBA_BLOCK)
        p_own = p[..., topk * MOBA_BLOCK:]
        return (jnp.einsum('bhqnk,bhqnkd->bhqd', p_sel, vg)
                + jnp.einsum('bhqk,bhkd->bhqd', p_own, v_own))

    o = lax.map(chunk, (q_chunks, jnp.arange(n_chunks)))
    o = o.transpose(1, 2, 0, 3, 4).reshape(b, N_HEADS, s_pad, HEAD_DIM)[:, :, :s_len]
    return merge_heads(o) @ w_out

def swa_sink_attention(h, w_in, qk_gain, sinks, w_out, cos, sin):
    b, s_len, _ = h.shape
    qd, kvd = N_HEADS * HEAD_DIM, SWA_KV_HEADS * HEAD_DIM
    q, k, v = jnp.split(h @ w_in, [qd, qd + kvd], axis=-1)
    q, k, v = split_heads(q, N_HEADS), split_heads(k, SWA_KV_HEADS), split_heads(v, SWA_KV_HEADS)
    q = apply_rope(rms_norm(q, qk_gain[0]), cos, sin)
    k = apply_rope(rms_norm(k, qk_gain[1]), cos, sin)
    w = SWA_WINDOW
    nb = s_len // w
    g = N_HEADS // SWA_KV_HEADS
    qb = q.reshape(b, SWA_KV_HEADS, g, nb, w, HEAD_DIM)

    def band(t):
        tb = t.reshape(b, SWA_KV_HEADS, nb, w, HEAD_DIM)
        prev = jnp.pad(tb, ((0, 0), (0, 0), (1, 0), (0, 0), (0, 0)))[:, :, :-1]
        return jnp.concatenate([prev, tb], axis=3)

    kb, vb = band(k), band(v)
    s = jnp.einsum('bkgnqd,bknsd->bkgnqs', qb, kb).astype(jnp.float32) * (HEAD_DIM ** -0.5)
    q_off = jnp.arange(w)[:, None] + w
    k_off = jnp.arange(2 * w)[None, :]
    rel = q_off - k_off
    in_win = (rel >= 0) & (rel < SWA_WINDOW)
    valid = in_win[None] & ((jnp.arange(nb)[:, None, None] > 0) | (k_off >= w)[None])
    s = jnp.where(valid, s, -jnp.inf)
    sink = sinks.astype(jnp.float32).reshape(SWA_KV_HEADS, g)[None, :, :, None, None, None]
    m = jnp.maximum(jnp.max(s, axis=-1, keepdims=True), sink)
    e = jnp.exp(s - m)
    p = e / (jnp.sum(e, axis=-1, keepdims=True) + jnp.exp(sink - m))
    o = jnp.einsum('bkgnqs,bknsd->bkgnqd', p.astype(v.dtype), vb)
    o = o.reshape(b, N_HEADS, s_len, HEAD_DIM)
    return merge_heads(o) @ w_out

def swiglu(h, w_gate, w_up, w_down):
    return (jax.nn.silu(h @ w_gate) * (h @ w_up)) @ w_down

def first_inputs(seed: int = 0) -> dict:
    key = jax.random.key(seed)
    ks = jax.random.split(key, 20)
    d = D_MODEL
    hd = N_HEADS * HEAD_DIM
    n_sb, n_moba, n_swa = (DEPTH + 2) // 3, (DEPTH + 1) // 3, DEPTH // 3

    def nrm(k, shape, scale):
        return jax.random.normal(k, shape, jnp.float32) * scale

    return {
        "x": nrm(ks[0], (BATCH, SEQ, d), 1.0),
        "c": nrm(ks[1], (BATCH, d), 1.0),
        "ada_w": nrm(ks[2], (DEPTH, d, 6 * d), 0.5 * d ** -0.5),
        "ada_b": nrm(ks[3], (DEPTH, 6 * d), 0.02),
        "norm_gain": 1.0 + nrm(ks[4], (DEPTH, 2, d), 0.02),
        "ffn_w_gate": nrm(ks[5], (DEPTH, d, D_FF), d ** -0.5),
        "ffn_w_up": nrm(ks[6], (DEPTH, d, D_FF), d ** -0.5),
        "ffn_w_down": nrm(ks[7], (DEPTH, D_FF, d), D_FF ** -0.5),
        "sb_w_in": nrm(ks[8], (n_sb, d, 3 * hd), d ** -0.5),
        "sb_w_out": nrm(ks[9], (n_sb, hd, d), hd ** -0.5),
        "moba_w_in": nrm(ks[10], (n_moba, d, 3 * hd), d ** -0.5),
        "moba_qk_gain": 1.0 + nrm(ks[11], (n_moba, 2, HEAD_DIM), 0.02),
        "moba_w_out": nrm(ks[12], (n_moba, hd, d), hd ** -0.5),
        "swa_w_in": nrm(ks[13], (n_swa, d, (N_HEADS + 2 * SWA_KV_HEADS) * HEAD_DIM), d ** -0.5),
        "swa_qk_gain": 1.0 + nrm(ks[14], (n_swa, 2, HEAD_DIM), 0.02),
        "swa_sinks": nrm(ks[15], (n_swa, N_HEADS), 0.5),
        "swa_w_out": nrm(ks[16], (n_swa, hd, d), hd ** -0.5),
    }

def first_block(x, c, ada_w, ada_b, norm_gain, ffn_w_gate, ffn_w_up, ffn_w_down,
              sb_w_in, sb_w_out, moba_w_in, moba_qk_gain, moba_w_out,
              swa_w_in, swa_qk_gain, swa_sinks, swa_w_out):
    s_len = x.shape[1]
    cos, sin = rope_tables(s_len)
    c_act = jax.nn.silu(c)
    for i in range(DEPTH):
        mod = c_act @ ada_w[i] + ada_b[i]
        sh1, sc1, g1, sh2, sc2, g2 = [m[:, None, :] for m in jnp.split(mod, 6, axis=-1)]
        h = modulate(rms_norm(x, norm_gain[i, 0]), sh1, sc1)
        kind, j = i % N_MIXERS, i // N_MIXERS
        if kind == 0:
            y = stick_breaking_attention(h, sb_w_in[j], sb_w_out[j])
        elif kind == 1:
            y = moba_attention(h, moba_w_in[j], moba_qk_gain[j], moba_w_out[j], cos, sin)
        else:
            y = swa_sink_attention(h, swa_w_in[j], swa_qk_gain[j], swa_sinks[j], swa_w_out[j], cos, sin)
        x = x + g1 * y
        h = modulate(rms_norm(x, norm_gain[i, 1]), sh2, sc2)
        x = x + g2 * swiglu(h, ffn_w_gate[i], ffn_w_up[i], ffn_w_down[i])
    return x


DEPTH_2 = 1

GRID_W = 64
CTX_LEN = 256
ATTN_Q_HEADS = 8
ATTN_KV_HEADS = 2
ATTN_GROUP = ATTN_Q_HEADS // ATTN_KV_HEADS
WINDOW = 128
ATTN_BLOCK = 128
ROPE_BASE = 10000.0
DN_HEADS = 8
DN_HEAD_DIM = 64
CONV_W = 3
CHUNK = 64
N_DIR = 2
D_FF_2 = 4 * D_MODEL
NEG_INF = -1e30

ATTN_WIDTH = ATTN_Q_HEADS * HEAD_DIM
KV_WIDTH = ATTN_KV_HEADS * HEAD_DIM
DN_WIDTH = DN_HEADS * DN_HEAD_DIM
IN_SPLITS = (ATTN_WIDTH, KV_WIDTH, KV_WIDTH, DN_WIDTH, DN_WIDTH, DN_WIDTH, DN_WIDTH,
             N_DIR * DN_HEADS, N_DIR * DN_HEADS, D_MODEL, D_MODEL)
IN_WIDTH = 4 * DN_WIDTH + ATTN_WIDTH + 2 * KV_WIDTH + 2 * N_DIR * DN_HEADS + 2 * D_MODEL


def rms_norm_2(x, g):
    xf = x.astype(jnp.float32)
    return xf * lax.rsqrt(jnp.mean(xf * xf, axis=-1, keepdims=True) + EPS) * g.astype(jnp.float32)

def l2_normalize(x):
    return x * lax.rsqrt(jnp.sum(x * x, axis=-1, keepdims=True) + EPS)

def split_cols(p):
    offsets = [int(o) for o in np.cumsum(IN_SPLITS)[:-1]]
    return jnp.split(p, offsets, axis=-1)

def axial_rope(x, row, col):
    half = HEAD_DIM // 2
    n_freq = half // 2
    freqs = ROPE_BASE ** (-jnp.arange(n_freq, dtype=jnp.float32) / n_freq)

    def rot(xh, pos):
        ang = pos.astype(jnp.float32)[:, None] * freqs
        cos = jnp.cos(ang)[None, :, None, :]
        sin = jnp.sin(ang)[None, :, None, :]
        x1, x2 = xh[..., :n_freq], xh[..., n_freq:]
        return jnp.concatenate([x1 * cos - x2 * sin, x1 * sin + x2 * cos], axis=-1)

    return jnp.concatenate([rot(x[..., :half], row), rot(x[..., half:], col)], axis=-1)

def centred_short_conv(x, w):
    pad = CONV_W // 2
    T = x.shape[1]
    xp = jnp.pad(x, ((0, 0), (pad, CONV_W - 1 - pad), (0, 0)))
    y = sum(xp[:, tap:tap + T] * w[tap] for tap in range(CONV_W))
    return jax.nn.silu(y)

def gated_delta_chunked(q, k, v, g_log, beta, s0):
    B, T, H, dk = q.shape
    n = T // CHUNK

    def chunks(a):
        return jnp.moveaxis(a.reshape((B, n, CHUNK, H) + a.shape[3:]), 3, 1)

    qc, kc, vc = chunks(q), chunks(k), chunks(v)
    gc, bc = chunks(g_log), chunks(beta)
    G = jnp.cumsum(gc, axis=-1)
    idx = jnp.arange(CHUNK)
    strict = idx[:, None] > idx[None, :]
    incl = idx[:, None] >= idx[None, :]
    diff = G[..., :, None] - G[..., None, :]
    dec_strict = jnp.where(strict, jnp.exp(jnp.where(strict, diff, 0.0)), 0.0)
    dec_incl = jnp.where(incl, jnp.exp(jnp.where(incl, diff, 0.0)), 0.0)
    kk = jnp.einsum('bhnid,bhnjd->bhnij', kc, kc)
    t_mat = jnp.eye(CHUNK, dtype=jnp.float32) + bc[..., :, None] * dec_strict * kk
    eG = jnp.exp(G)
    w_mat = lax.linalg.triangular_solve(t_mat, (bc * eG)[..., None] * kc, left_side=True, lower=True,
                                        unit_diagonal=True)
    u_v = lax.linalg.triangular_solve(t_mat, bc[..., None] * vc, left_side=True, lower=True,
                                      unit_diagonal=True)
    intra = dec_incl * jnp.einsum('bhnid,bhnjd->bhnij', qc, kc)
    q_dec = eG[..., None] * qc
    g_last = G[..., -1]
    k_tail = jnp.exp(g_last[..., None] - G)[..., None] * kc

    def step(S, xs):
        w_c, uv_c, qd_c, intra_c, kt_c, gl_c = xs
        u = uv_c - jnp.einsum('bhck,bhkv->bhcv', w_c, S)
        o = jnp.einsum('bhck,bhkv->bhcv', qd_c, S) + jnp.einsum('bhij,bhjv->bhiv', intra_c, u)
        S = jnp.exp(gl_c)[..., None, None] * S + jnp.einsum('bhck,bhcv->bhkv', kt_c, u)
        return S, o

    xs = tuple(jnp.moveaxis(a, 2, 0) for a in (w_mat, u_v, q_dec, intra, k_tail, g_last))
    s_final, o = lax.scan(step, s0, xs)
    o = jnp.transpose(o, (1, 0, 3, 2, 4)).reshape(B, T, H, v.shape[-1])
    return o, s_final

def bidir_delta(q, k, v, g, beta, s0_f, s0_b):
    o_f, s_f = gated_delta_chunked(q, k, v, g[:, :, 0], beta[:, :, 0], s0_f)
    flip = lambda a: jnp.flip(a, axis=1)
    o_b, s_b = gated_delta_chunked(flip(q), flip(k), flip(v), flip(g[:, :, 1]), flip(beta[:, :, 1]), s0_b)
    return o_f + flip(o_b), s_f, s_b

def window_ctx_attention(q, k, v, k_ctx, v_ctx, sink):
    B, S = q.shape[:2]
    L = k_ctx.shape[1]
    nb = S // ATTN_BLOCK
    qb = q.reshape(B, nb, ATTN_BLOCK, ATTN_KV_HEADS, ATTN_GROUP, HEAD_DIM)

    def band(a):
        ap = jnp.pad(a, ((0, 0), (ATTN_BLOCK, ATTN_BLOCK), (0, 0), (0, 0)))
        ap = ap.reshape(B, nb + 2, ATTN_BLOCK, ATTN_KV_HEADS, HEAD_DIM)
        return jnp.concatenate([ap[:, :-2], ap[:, 1:-1], ap[:, 2:]], axis=2)

    kb, vb = band(k), band(v)
    blk = jnp.arange(nb)[:, None, None]
    qpos = blk * ATTN_BLOCK + jnp.arange(ATTN_BLOCK)[None, :, None]
    kpos = (blk - 1) * ATTN_BLOCK + jnp.arange(3 * ATTN_BLOCK)[None, None, :]
    valid = (jnp.abs(qpos - kpos) <= WINDOW) & (kpos >= 0) & (kpos < S)
    scale = HEAD_DIM ** -0.5
    s_loc = jnp.einsum('bnqgrd,bnkgd->bngrqk', qb, kb) * scale
    s_loc = jnp.where(valid[None, :, None, None], s_loc, NEG_INF)
    s_ctx = jnp.einsum('bnqgrd,bkgd->bngrqk', qb, k_ctx) * scale
    s_sink = jnp.broadcast_to(sink.reshape(ATTN_KV_HEADS, ATTN_GROUP)[None, None, :, :, None, None],
                              s_loc.shape[:-1] + (1,))
    p = jax.nn.softmax(jnp.concatenate([s_loc, s_ctx, s_sink], axis=-1).astype(jnp.float32), axis=-1)
    n_loc = 3 * ATTN_BLOCK
    o = (jnp.einsum('bngrqk,bnkgd->bnqgrd', p[..., :n_loc], vb)
         + jnp.einsum('bngrqk,bkgd->bnqgrd', p[..., n_loc:n_loc + L], v_ctx))
    return o.reshape(B, S, ATTN_WIDTH)

def ctx_self_attention(q, k, v, sink):
    B, L = q.shape[:2]
    qg = q.reshape(B, L, ATTN_KV_HEADS, ATTN_GROUP, HEAD_DIM)
    s = jnp.einsum('bqgrd,bkgd->bgrqk', qg, k) * HEAD_DIM ** -0.5
    s_sink = jnp.broadcast_to(sink.reshape(ATTN_KV_HEADS, ATTN_GROUP)[None, :, :, None, None], s.shape[:-1] + (1,))
    p = jax.nn.softmax(jnp.concatenate([s, s_sink], axis=-1).astype(jnp.float32), axis=-1)
    o = jnp.einsum('bgrqk,bkgd->bqgrd', p[..., :L], v)
    return o.reshape(B, L, ATTN_WIDTH)

def trunk_layer(x, ctx, c, c_ctx, w_ada, b_ada, g_norm1, w_in, q_norm_g, k_norm_g, attn_sink, conv_w,
                a_log, dt_bias, dn_norm_g, w_br_attn, w_br_dn, w_out, g_norm2, w_mlp1, w_mlp2, update_ctx):
    B, S = x.shape[:2]
    L = ctx.shape[1]
    rows = S // GRID_W
    row = jnp.broadcast_to(jnp.arange(rows)[:, None], (rows, GRID_W)).reshape(-1)
    col = jnp.broadcast_to(jnp.arange(GRID_W)[None, :], (rows, GRID_W)).reshape(-1)

    mod = jax.nn.silu(c.astype(jnp.float32)) @ w_ada + b_ada
    mod_c = jax.nn.silu(c_ctx.astype(jnp.float32)) @ w_ada + b_ada
    sh1, sc1, gt1, sh2, sc2, gt2 = [m[:, None] for m in jnp.split(mod, 6, axis=-1)]
    csh1, csc1, cgt1, csh2, csc2, cgt2 = jnp.split(mod_c, 6, axis=-1)

    h = rms_norm_2(x, g_norm1) * (1.0 + sc1) + sh1
    hc = rms_norm_2(ctx, g_norm1) * (1.0 + csc1) + csh1
    aq, ak, av, dq, dk, dv, dz, da, db, ga, gd = split_cols(h @ w_in)
    caq, cak, cav, cdq, cdk, cdv, cdz, cda, cdb, cga, cgd = split_cols(hc @ w_in)

    def heads(a, n_heads):
        return a.reshape(a.shape[0], a.shape[1], n_heads, HEAD_DIM)

    q_a = axial_rope(rms_norm_2(heads(aq, ATTN_Q_HEADS), q_norm_g), row, col)
    k_a = axial_rope(rms_norm_2(heads(ak, ATTN_KV_HEADS), k_norm_g), row, col)
    v_a = heads(av, ATTN_KV_HEADS)
    k_ac = rms_norm_2(heads(cak, ATTN_KV_HEADS), k_norm_g)
    v_ac = heads(cav, ATTN_KV_HEADS)
    y_attn = window_ctx_attention(q_a, k_a, v_a, k_ac, v_ac, attn_sink)

    def dn_inputs(pq, pk, pv, pa, pb):
        qkv = centred_short_conv(jnp.concatenate([pq, pk, pv], axis=-1), conv_w)
        q_d, k_d, v_d = jnp.split(qkv, 3, axis=-1)
        q_d = l2_normalize(heads(q_d, DN_HEADS)) * DN_HEAD_DIM ** -0.5
        k_d = l2_normalize(heads(k_d, DN_HEADS))
        v_d = heads(v_d, DN_HEADS)
        T = pq.shape[1]
        beta = jax.nn.sigmoid(pb.reshape(pb.shape[0], T, N_DIR, DN_HEADS))
        g = -jnp.exp(a_log) * jax.nn.softplus(pa.reshape(pa.shape[0], T, N_DIR, DN_HEADS) + dt_bias)
        return q_d, k_d, v_d, g, beta

    s_zero = jnp.zeros((B, DN_HEADS, DN_HEAD_DIM, DN_HEAD_DIM), jnp.float32)
    o_dc, s_cf, s_cb = bidir_delta(*dn_inputs(cdq, cdk, cdv, cda, cdb), s_zero, s_zero)
    o_dl, _, _ = bidir_delta(*dn_inputs(dq, dk, dv, da, db), s_cf, s_cb)

    def merge(y_a, o_d, z, gate_a, gate_d):
        y_d = (rms_norm_2(o_d, dn_norm_g) * jax.nn.silu(heads(z, DN_HEADS))).reshape(z.shape)
        y = jax.nn.sigmoid(gate_a) * (y_a @ w_br_attn) + jax.nn.sigmoid(gate_d) * (y_d @ w_br_dn)
        return y @ w_out

    def mlp(s, shift, scale_m):
        hm = rms_norm_2(s, g_norm2) * (1.0 + scale_m) + shift
        return jnp.square(jax.nn.relu(hm @ w_mlp1)) @ w_mlp2

    x_new = x.astype(jnp.float32) + gt1 * merge(y_attn, o_dl, dz, ga, gd)
    x_new = x_new + gt2 * mlp(x_new, sh2, sc2)

    if update_ctx:
        q_ac = rms_norm_2(heads(caq, ATTN_Q_HEADS), q_norm_g)
        y_attn_c = ctx_self_attention(q_ac, k_ac, v_ac, attn_sink)
        ctx = ctx.astype(jnp.float32) + cgt1 * merge(y_attn_c, o_dc, cdz, cga, cgd)
        ctx = ctx + cgt2 * mlp(ctx, csh2, csc2)
    return x_new, ctx

def second_inputs(seed: int = 0) -> dict:
    key = jax.random.key(seed)
    ks = jax.random.split(key, 24)
    f32 = jnp.float32
    nrm = lambda k, shape, s: jax.random.normal(k, shape, f32) * s
    dt = jnp.exp(jax.random.uniform(ks[12], (DEPTH_2, N_DIR, DN_HEADS), f32, np.log(1e-3), np.log(1e-1)))
    return {
        "x": nrm(ks[0], (BATCH, SEQ, D_MODEL), 1.0),
        "c": nrm(ks[1], (BATCH, D_MODEL), 1.0),
        "ctx": nrm(ks[2], (BATCH, CTX_LEN, D_MODEL), 1.0),
        "c_ctx": nrm(ks[3], (D_MODEL,), 1.0),
        "w_ada": nrm(ks[4], (DEPTH_2, D_MODEL, 6 * D_MODEL), 0.5 * D_MODEL ** -0.5),
        "b_ada": nrm(ks[5], (DEPTH_2, 6 * D_MODEL), 0.02),
        "g_norm1": 1.0 + nrm(ks[6], (DEPTH_2, D_MODEL), 0.1),
        "w_in": nrm(ks[7], (DEPTH_2, D_MODEL, IN_WIDTH), D_MODEL ** -0.5),
        "q_norm_g": 1.0 + nrm(ks[8], (DEPTH_2, HEAD_DIM), 0.1),
        "k_norm_g": 1.0 + nrm(ks[9], (DEPTH_2, HEAD_DIM), 0.1),
        "attn_sink": nrm(ks[10], (DEPTH_2, ATTN_Q_HEADS), 0.5),
        "conv_w": nrm(ks[11], (DEPTH_2, CONV_W, 3 * DN_WIDTH), CONV_W ** -0.5),
        "a_log": jnp.log(jax.random.uniform(ks[13], (DEPTH_2, N_DIR, DN_HEADS), f32, 1.0, 16.0)),
        "dt_bias": dt + jnp.log(-jnp.expm1(-dt)),
        "dn_norm_g": 1.0 + nrm(ks[14], (DEPTH_2, DN_HEAD_DIM), 0.1),
        "w_br_attn": nrm(ks[15], (DEPTH_2, ATTN_WIDTH, D_MODEL), ATTN_WIDTH ** -0.5),
        "w_br_dn": nrm(ks[16], (DEPTH_2, DN_WIDTH, D_MODEL), DN_WIDTH ** -0.5),
        "w_out": nrm(ks[17], (DEPTH_2, D_MODEL, D_MODEL), D_MODEL ** -0.5),
        "g_norm2": 1.0 + nrm(ks[18], (DEPTH_2, D_MODEL), 0.1),
        "w_mlp1": nrm(ks[19], (DEPTH_2, D_MODEL, D_FF_2), D_MODEL ** -0.5),
        "w_mlp2": nrm(ks[20], (DEPTH_2, D_FF_2, D_MODEL), D_FF_2 ** -0.5),
    }

def second_block(x, c, ctx, c_ctx, w_ada, b_ada, g_norm1, w_in, q_norm_g, k_norm_g, attn_sink, conv_w,
              a_log, dt_bias, dn_norm_g, w_br_attn, w_br_dn, w_out, g_norm2, w_mlp1, w_mlp2):
    out_dtype = x.dtype
    for layer in range(DEPTH_2):
        x, ctx = trunk_layer(x, ctx, c, c_ctx, w_ada[layer], b_ada[layer], g_norm1[layer], w_in[layer],
                             q_norm_g[layer], k_norm_g[layer], attn_sink[layer], conv_w[layer],
                             a_log[layer], dt_bias[layer], dn_norm_g[layer], w_br_attn[layer],
                             w_br_dn[layer], w_out[layer], g_norm2[layer], w_mlp1[layer], w_mlp2[layer],
                             update_ctx=layer < DEPTH_2 - 1)
    return x.astype(out_dtype)


def setup_inputs(seed=0):
    out = dict(first_inputs(seed))
    for name, value in second_inputs(seed + 1).items():
        if name != "x":
            out[name + "_2"] = value
    return out


def reference(
    x, c, ada_w, ada_b, norm_gain, ffn_w_gate, ffn_w_up, ffn_w_down, sb_w_in, sb_w_out,
    moba_w_in, moba_qk_gain, moba_w_out, swa_w_in, swa_qk_gain, swa_sinks, swa_w_out, c_2,
    ctx_2, c_ctx_2, w_ada_2, b_ada_2, g_norm1_2, w_in_2, q_norm_g_2, k_norm_g_2, attn_sink_2,
    conv_w_2, a_log_2, dt_bias_2, dn_norm_g_2, w_br_attn_2, w_br_dn_2, w_out_2, g_norm2_2,
    w_mlp1_2, w_mlp2_2,
):
    x = first_block(
        x, c, ada_w, ada_b, norm_gain, ffn_w_gate, ffn_w_up, ffn_w_down, sb_w_in, sb_w_out,
        moba_w_in, moba_qk_gain, moba_w_out, swa_w_in, swa_qk_gain, swa_sinks, swa_w_out,
    )
    return second_block(
        x, c_2, ctx_2, c_ctx_2, w_ada_2, b_ada_2, g_norm1_2, w_in_2, q_norm_g_2, k_norm_g_2,
        attn_sink_2, conv_w_2, a_log_2, dt_bias_2, dn_norm_g_2, w_br_attn_2, w_br_dn_2, w_out_2,
        g_norm2_2, w_mlp1_2, w_mlp2_2,
    )


_drawn_inputs = setup_inputs


def setup_inputs(seed=0):
    import zlib

    import numpy as np

    out = dict(_drawn_inputs(seed))
    spreads = {}
    factors = {'norm_gain': 3.934,
     'moba_qk_gain': 8.0,
     'swa_qk_gain': 8.0,
     'swa_sinks': 200.0,
     'ctx_2': 4.637,
     'g_norm1_2': 3.457,
     'q_norm_g_2': 8.0,
     'k_norm_g_2': 8.0,
     'attn_sink_2': 8.0,
     'dn_norm_g_2': 5.991,
     'g_norm2_2': 8.0}
    for name, (base, spread) in spreads.items():
        noise = np.random.default_rng([zlib.crc32(name.encode()), seed]).standard_normal(out[name].shape)
        drawn = base * np.exp(spread * noise) if base else spread * noise
        out[name] = __import__('jax').numpy.asarray(drawn.astype(out[name].dtype))
    for name, factor in factors.items():
        out[name] = (out[name] * factor).astype(out[name].dtype)
    return out
```

```python
from contextlib import ExitStack

import numpy as np

import concourse.bass as bass
from concourse import mybir

F32 = mybir.dt.float32
F32R = mybir.dt.float32r
BF16 = mybir.dt.bfloat16
ACT = mybir.ActivationFunctionType
ALU = mybir.AluOpType
AX = mybir.AxisListType

P = 128
D = 1024
SEQ = 256
NT = SEQ // P
KT = D // P
HD = 64
DEPTH = 4
FF = 2816
FFT = FF // P
EPS = 1e-6
UNIT_K = 4
RING = 4
GROUP = 4
NEG = -1e30
KINDS = ["sb", "moba", "swa", "sb"]
CONSTS = ["ident", "ones", "tri", "m_sb", "m_prev", "m_causal"]
NCOL = 104
LAT = DEPTH
LAT_QH = 8
DNH = 8
CH = 64
LEVELS = 6
AQ, AK, AV = 0, 512, 640
DQ, DK, DV, DZ = 768, 1280, 1792, 2304
DAB = 2816
GA = 2848
FF2 = 4096
CONSTS_2 = ["tri_f", "tri_b", "later_f", "later_b", "half"]
MASKS_2 = 2 * LEVELS + 5


class Walk:

    def __init__(self):
        self.s = 0
        self.u = 0
        self.pn = 0
        self.f = 0
        self.a = 0
        self.sums = 0
        self.m = 0
        self.rms = 0
        self.norms = 0
        self.normed = {}
        self.group = 0
        self.sb = 0
        self.sm = 0
        self.kt = 0
        self.swa = 0
        self.slot_done = [0] * RING
        self.free_act = 0
        self.free_dve = 0
        self.panel_free = []

    def end_mixer(self, kind):
        self.group += 4
        self.sb += 4 * (kind == "sb")
        self.sm += 4 * (kind != "sb")
        self.kt += 4 * (kind != "swa")
        self.swa += kind == "swa"

    def next_load(self, loads, kind):
        while True:
            load = loads[self.s]
            slot = self.s % RING
            self.s += 1
            self.slot_done[slot] += 16 * (len(load[1]) if load[0] == "unit" else 1)
            if load[0] == kind:
                return slot, self.slot_done[slot], load

    def panel(self, engine):
        pn = self.pn
        self.pn += 1
        if engine == "act":
            self.free_act += 1
            self.panel_free.append(("act", self.free_act))
        else:
            self.free_dve += 1
            self.panel_free.append(("dve", self.free_dve))
        return pn


def build(nc, w, out):
    with ExitStack() as ctx:
        top = [-(-nc.sbuf_base // 64) * 64]

        def at(name, cols, dtype=F32, offset=None, parts=P):
            if offset is None:
                offset = top[0]
                top[0] += -(-cols * (2 if dtype == BF16 else 4) // 64) * 64
            return nc.alloc_sbuf_tensor_at(name, [parts, cols], dtype, offset=offset), offset

        def tile(name, cols, dtype=F32, offset=None, parts=P):
            return at(name, cols, dtype, offset, parts)[0][:, :]

        def sem(name):
            return ctx.enter_context(nc.semaphore(name))

        raw = tile("raw", RING * 2048).rearrange("p (s n) -> p s n", s=RING)
        w_hi = tile("w_hi", 2 * 2048, F32R).rearrange("p (s k n) -> p s k n", s=2, k=UNIT_K)
        w_lo = tile("w_lo", 2 * 2048, F32R).rearrange("p (s k n) -> p s k n", s=2, k=UNIT_K)
        x_res = tile("x_res", NT * D).rearrange("p (t d) -> p t d", t=NT)
        h_hi = tile("h_hi", KT * SEQ, F32R).rearrange("p (k n) -> p k n", k=KT)
        h_lo = tile("h_lo", KT * SEQ, F32R).rearrange("p (k n) -> p k n", k=KT)
        act_hi_t, act_hi_off = at("act_hi", FFT * SEQ, F32R)
        act_hi = act_hi_t[:, :].rearrange("p (k n) -> p k n", k=FFT)
        act_lo_t, act_lo_off = at("act_lo", FFT * SEQ, F32R)
        act_lo = act_lo_t[:, :].rearrange("p (k n) -> p k n", k=FFT)
        gates = tile("gates", 2 * D).rearrange("p (g n) -> p g n", g=2)
        full = tile("full", 2 * 512).rearrange("p (b n) -> p b n", b=2)
        consts = tile("consts", len(CONSTS) * P).rearrange("p (c n) -> p c n", n=P)
        ident, ones, tri = consts[:, 0], consts[:, 1], consts[:, 2]
        ident_b = tile("ident_b", P, BF16)
        masks_b = tile("masks_b", 3 * P, BF16).rearrange("p (c n) -> p c n", n=P)
        m_sb, m_causal, m_window = masks_b[:, 0], masks_b[:, 2], masks_b[:, 1:3]
        cols_in = tile("cols_in", P, parts=NCOL)
        cols = tile("cols", NCOL)
        c_col = tile("c_col", 24)
        mod = tile("mod", 2 * 48).rearrange("p (l n) -> p l n", l=2)
        gsc = tile("gsc", 2 * 24).rearrange("p (l n) -> p l n", l=2)
        ssq = tile("ssq", 4).rearrange("p (t n) -> p t n", t=2)
        ssum = tile("ssum", 2)
        rms_v = tile("rms_v", 32)
        rms_y = tile("rms_y", 32)
        rms_t = tile("rms_t", 32)
        n_max = tile("n_max", 8)
        p_sum = tile("p_sum", 8)
        p_inv = tile("p_inv", 8)
        sink_e = tile("sink_e", 8)
        rope_cs = tile("rope_cs", 2 * NT * HD).rearrange("p (a t d) -> p a t d", a=2, t=NT)
        rope_g = tile("rope_g", 2 * HD).rearrange("p (q d) -> p q d", q=2)
        rope_t_t, rope_t_off = at("rope_t", 2 * NT * 2 * HD)
        rope_t = rope_t_t[:, :].rearrange("p (a t q d) -> p a t q d", a=2, t=NT, q=2)
        sinks = tile("sinks", 16)
        ss16 = tile("ss16", 16)
        att_t, acc_off = at("att", 6 * D)
        z_sb = tile("z_sb", 3 * 512, offset=acc_off).rearrange("p (b n) -> p b n", b=3)
        e_sb = tile("e_sb", 3 * 512, offset=acc_off + 6144).rearrange("p (b n) -> p b n", b=3)
        aT = tile("aT", 3 * 512, offset=acc_off + 2 * 6144).rearrange("p (b n) -> p b n", b=3)
        qT = tile("qT", 512, offset=acc_off + 3 * 6144).rearrange("p (a n) -> p a n", a=2)
        kT = tile("kT", 512, offset=acc_off + 3 * 6144 + 2048).rearrange("p (a n) -> p a n", a=2)
        qk_t, qk_off = at("qk_st", 2 * NT * 512)
        qk_st = qk_t[:, :].rearrange("p (b t n) -> p b t n", b=2, t=NT)
        n_st = tile("n_st", NT * D, offset=qk_off).rearrange("p (t d) -> p t d", t=NT)
        silu_st = tile("silu_st", NT * 256, offset=qk_off).rearrange("p (t n) -> p t n", t=NT)
        act_st = tile("act_st", NT * 256, offset=qk_off + 2048).rearrange("p (t n) -> p t n", t=NT)
        v_st = tile("v_st", 2 * NT * 512, offset=act_lo_off + 8 * 1024).rearrange("p (b t n) -> p b t n", b=2, t=NT)
        rope_st = tile("rope_st", NT * 512, offset=act_hi_off + 8 * 1024).rearrange("p (t n) -> p t n", t=NT)
        KB = 1024
        acc_t, d_off = at("acc", 2 * 2 * D)
        acc = acc_t[:, :].rearrange("p (b n) -> p b n", b=2)
        acc_c = tile("acc_c", 2 * D, offset=acc_off)
        s_off = d_off + 2 * D * 4
        consts_2 = tile("consts_2", len(CONSTS_2) * P, offset=s_off).rearrange("p (c n) -> p c n", n=P)
        tri_dir, later_dir, half = consts_2[:, 0:2], consts_2[:, 2:4], consts_2[:, 4].rearrange("p (h n) -> p h n", h=2)
        masks_2 = tile("masks_2", MASKS_2 * P, BF16, offset=s_off + len(CONSTS_2) * P * 4).rearrange("p (c n) -> p c n", n=P)
        level_mask = masks_2[:, 0:2 * LEVELS].rearrange("p (d l) n -> p d l n", d=2)
        m_strict, m_incl, m_from = masks_2[:, 2 * LEVELS:2 * LEVELS + 2], masks_2[:, 2 * LEVELS + 2:2 * LEVELS + 4], masks_2[:, 2 * LEVELS + 4]
        dn_rows = tile("dn_rows", 2 * 2 * DNH + HD)
        alog_row, dtb_row, dng_row = dn_rows[:, 0:16], dn_rows[:, 16:32], dn_rows[:, 32:96]
        dab = tile("dab", 4 * 32).rearrange("p (s n) -> p s n", s=4)
        gate_z = tile("gate_z", 4 * 32).rearrange("p (s n) -> p s n", s=4)
        gate_s = tile("gate_s", 4 * 32).rearrange("p (s n) -> p s n", s=4)
        g_all = tile("g_all", 64).rearrange("p (s n) -> p s n", s=4)
        lnb_all = tile("lnb_all", 64).rearrange("p (s n) -> p s n", s=4)
        beta = tile("beta", 64).rearrange("p (s d h) -> p s d h", s=4, d=2)
        neg_G = tile("neg_G", 64).rearrange("p (d s h) -> p d s h", d=2, s=4)
        e_G = tile("e_G", 64).rearrange("p (d s h) -> p d s h", d=2, s=4)
        e_tail = tile("e_tail", 64).rearrange("p (d s h) -> p d s h", d=2, s=4)
        beG = tile("beG", 64).rearrange("p (d s h) -> p d s h", d=2, s=4)
        e_last = tile("e_last", 64).rearrange("p (c h) -> p c h", h=DNH)
        assert top[0] <= nc.sbuf_usable_end, top[0]

        def token_tile(name, cols, offset):
            return tile(name, NT * cols, offset=offset).rearrange("p (t n) -> p t n", t=NT)

        AH, AL, AB, AC = act_hi_off, act_lo_off, acc_off, qk_off
        ctx_raw = token_tile("ctx_raw", D, AL + 8 * KB)
        mask_st = tile("mask_st", MASKS_2 * P, offset=AH + 8 * KB).rearrange("p (c n) -> p c n", n=P)
        dk_x, dv_x, dq_x = (token_tile(n, 512, AH + (8 + 4 * i) * KB) for i, n in enumerate(("dk_x", "dv_x", "dq_x")))
        dk_c, dv_c, dz = (token_tile(n, 512, AL + (8 + 4 * i) * KB) for i, n in enumerate(("dk_c", "dv_c", "dz")))
        aq = token_tile("aq", 512, AB)
        lrope_st = token_tile("lrope_st", 512, AB + 4 * KB)
        lrot = token_tile("lrot", 512, AB + 8 * KB)
        kva_x, kva_c = token_tile("kva_x", 256, AB + 12 * KB), token_tile("kva_c", 256, AB + 14 * KB)
        kdup = tile("kdup", 4 * 256, offset=AB + 16 * KB).rearrange("p (t n) -> p t n", t=4)
        lkT = tile("lkT", 2 * 512, offset=AB + 20 * KB).rearrange("p (g n) -> p g n", g=2)
        lqT = tile("lqT", 4 * SEQ, offset=AB + 8 * KB).rearrange("p (a n) -> p a n", a=4)
        laT = tile("laT", 4 * 512, offset=AB).rearrange("p (b n) -> p b n", b=4)
        p_sb = tile("p_sb", 4 * 512, offset=AC).rearrange("p (b n) -> p b n", b=4)
        conv_rows = tile("conv_rows", 3 * 1536, offset=AB).rearrange("p (w n) -> p w n", w=3)
        prev, nxt = token_tile("prev", 512, AC), token_tile("nxt", 512, AC + 4 * KB)
        sq_t = token_tile("sq_t", 512, AC)
        kT_c = tile("kT_c", 4 * SEQ, offset=AH + 4 * KB).rearrange("p (a n) -> p a n", a=4)
        kT_x = tile("kT_x", 4 * SEQ, offset=AL + 4 * KB).rearrange("p (a n) -> p a n", a=4)
        qT_x = tile("qT_x", 4 * SEQ, offset=d_off).rearrange("p (a n) -> p a n", a=4)
        o_dn = token_tile("o_dn", 512, d_off + 4 * KB)
        LT, X, XT, Y = (tile(n, 1024, offset=AB + 4 * KB * i).rearrange("p (r n) -> p r n", r=2) for i, n in enumerate(("LT", "X", "XT", "Y")))
        wT = tile("wT", 1024, offset=AB + 16 * KB).rearrange("p (r n) -> p r n", r=2)
        u_st = tile("u_st", 1024, offset=AB + 20 * KB).rearrange("p (s n) -> p s n", s=2)
        bek, bv = tile("bek", 512, offset=AC), tile("bv", 512, offset=AC + 2 * KB)
        k_tail = tile("k_tail", 1024, offset=AC + 4 * KB).rearrange("p (d n) -> p d n", d=2)
        q_dec = tile("q_dec", 512, offset=AH + 20 * KB)
        state = tile("state", 512, offset=AL + 20 * KB)
        state_t = tile("state_t", 512, offset=rope_t_off)
        intraT = tile("intraT", 2048, offset=AL + 8 * KB).rearrange("p (d r n) -> p d r n", d=2, r=2)
        q_decT = tile("q_decT", 1024, offset=AH + 4 * KB).rearrange("p (r n) -> p r n", r=2)
        sig = tile("sig", 2 * NT * D, offset=AB).rearrange("p (b t n) -> p b t n", b=2, t=NT)
        relu_st, hid_st = token_tile("relu_st", 512, AC), token_tile("hid_st", 512, AC + 4 * KB)

        G = [ctx.enter_context(nc.psum_tensor(f"G{i}", [P, 512], F32))[:, :] for i in range(4)]
        A = [ctx.enter_context(nc.psum_tensor(f"A{i}", [P, 512], F32))[:, :] for i in range(4)]

        landed = [sem(f"landed{i}") for i in range(RING)]
        raw_free = sem("raw_free")
        hi_ready = sem("hi_ready")
        lo_ready = sem("lo_ready")
        gemm_done = sem("gemm_done")
        free_act = sem("free_act")
        free_dve = sem("free_dve")
        const_in = sem("const_in")
        rope_in = sem("rope_in")
        x_in = sem("x_in")
        gain_in = sem("gain_in")
        rope_ready = sem("rope_ready")
        pool_step = sem("pool_step")
        sq_ready = sem("sq_ready")
        xn_ready = sem("xn_ready")
        rot_ready = sem("rot_ready")
        qk_ready = sem("qk_ready")
        max_ready = sem("max_ready")
        p_ready = sem("p_ready")
        pn_ready = sem("pn_ready")
        pT_done = sem("pT_done")
        sink_ready = sem("sink_ready")
        se_ready = sem("se_ready")
        cast_ready = sem("cast_ready")
        cols_T = sem("cols_T")
        cols_ready = sem("cols_ready")
        c_ready = sem("c_ready")
        acc_zero = sem("acc_zero")
        bias_in = [sem(f"bias_in{i}") for i in range(2)]
        acc_done = sem("acc_done")
        sums_done = sem("sums_done")
        mod_out = sem("mod_out")
        gsc_ready = sem("gsc_ready")
        ss_ready = sem("ss_ready")
        v_ready = sem("v_ready")
        y_ready = sem("y_ready")
        n_ready = sem("n_ready")
        norm_T = sem("norm_T")
        split_full = sem("split_full")
        split_hi = sem("split_hi")
        split_lo = sem("split_lo")
        x_ready = sem("x_ready")
        y_gated = sem("y_gated")
        kvT_done = sem("kvT_done")
        kvT_ready = sem("kvT_ready")
        s_done = sem("s_done")
        qkT_done = sem("qkT_done")
        qT_ready = sem("qT_ready")
        kT_ready = sem("kT_ready")
        z_done = sem("z_done")
        z_copied = sem("z_copied")
        nabs_ready = sem("nabs_ready")
        exp_ready = sem("exp_ready")
        ln_ready = sem("ln_ready")
        sp_ready = sem("sp_ready")
        r_done = sem("r_done")
        d_ready = sem("d_ready")
        aT_ready = sem("aT_ready")
        av_done = sem("av_done")
        silu_ready = sem("silu_ready")
        act_ready = sem("act_ready")
        actT_done = sem("actT_done")
        dve_step = sem("dve_step")
        out_done = sem("out_done")
        accc_zero = sem("accc_zero")
        biasc_in = sem("biasc_in")
        accc_done = sem("accc_done")
        ctx_in = sem("ctx_in")
        lat_in = sem("lat_in")
        masks_in = sem("masks_in")
        masks_ready = sem("masks_ready")
        rope2_ready = sem("rope2_ready")
        ltT_done = sem("ltT_done")
        kq_act = sem("kq_act")
        kq_dve = sem("kq_dve")
        ws_done = sem("ws_done")
        wmax_ready = sem("wmax_ready")
        wp_ready = sem("wp_ready")
        wse_ready = sem("wse_ready")
        wn_ready = sem("wn_ready")
        wpT_done = sem("wpT_done")
        waT_act = sem("waT_act")
        waT_dve = sem("waT_dve")
        woT_done = sem("woT_done")
        cw_in = sem("cw_in")
        shift_in = sem("shift_in")
        conv_ready = sem("conv_ready")
        cs_ready = sem("cs_ready")
        l2_ready = sem("l2_ready")
        gz_ready = sem("gz_ready")
        ge_ready = sem("ge_ready")
        gl_ready = sem("gl_ready")
        ea_ready = sem("ea_ready")
        gates_ready = sem("gates_ready")
        beta_ready = sem("beta_ready")
        gsum_done = sem("gsum_done")
        eg_ready = sem("eg_ready")
        beg_ready = sem("beg_ready")
        dT_done = sem("dT_done")
        dT_act = sem("dT_act")
        dT_dve = sem("dT_dve")
        e_done = sem("e_done")
        kk_done = sem("kk_done")
        E_ready = sem("E_ready")
        LT_ready = sem("LT_ready")
        y_done = sem("y_done")
        X_ready = sem("X_ready")
        Y_ready = sem("Y_ready")
        xy_done = sem("xy_done")
        prep_ready = sem("prep_ready")
        wT_done = sem("wT_done")
        uv_done = sem("uv_done")
        wT_ready = sem("wT_ready")
        uv_ready = sem("uv_ready")
        in_done = sem("in_done")
        ie_ready = sem("ie_ready")
        intra_ready = sem("intra_ready")
        qdT_done = sem("qdT_done")
        qdT_ready = sem("qdT_ready")
        state_zero = sem("state_zero")
        wS_done = sem("wS_done")
        u_ready = sem("u_ready")
        su_done = sem("su_done")
        S_ready = sem("S_ready")
        o_done = sem("o_done")
        oacc_ready = sem("oacc_ready")
        yd_ready = sem("yd_ready")
        ydT_done = sem("ydT_done")
        yy_ready = sem("yy_ready")
        yT_done = sem("yT_done")
        relu_ready = sem("relu_ready")
        hid_ready = sem("hid_ready")
        hidT_done = sem("hidT_done")

        ADA_U = 3 * KT
        SB_SLOTS = {2: [("T", 0)], 3: [("S", 0)], 4: [("C", 0)], 5: [("T", 1)], 6: [("V", 0), ("S", 1)], 7: [("C", 1)],
                    8: [("V", 1), ("T", 2)], 9: [("S", 2)], 10: [("C", 2)], 11: [("V", 2)], 12: [("T", 3), ("S", 3)],
                    13: [("C", 3), ("V", 3)]}
        MOBA_SLOTS = {2: [("N", 0)], 4: [("T", 0), ("N", 1)], 5: [("S", 0)], 6: [("C", 0)], 7: [("V", 0), ("T", 1)],
                      8: [("S", 1), ("N", 2)], 9: [("C", 1)], 10: [("V", 1), ("N", 3), ("T", 2)], 11: [("S", 2)],
                      12: [("C", 2), ("T", 3)], 13: [("V", 2), ("S", 3), ("C", 3), ("V", 3)]}
        SWA_SLOTS = {2: [("N", "kv")], 3: [("T", "kv")], 4: [("N", 0)],
                     5: [(x, g) for g in range(2) for x in "TSCV"],
                     6: [("N", 2)] + [(x, 2) for x in "TSCV"], 7: [(x, 3) for x in "TSCV"]}
        SLOTS = {"sb": SB_SLOTS, "moba": MOBA_SLOTS, "swa": SWA_SLOTS}

        def qkv_panels(kind):
            if kind == "swa":
                return [("kv", 0, [(0, D, 256)])] + [("q", b, [(0, 512 * b, 512)]) for b in range(2)]
            qk = [("qk", g, [(0, 256 * g, 256), (256, D + 256 * g, 256)]) for g in range(4)]
            v = [("v", b, [(0, 2 * D + 512 * b, 512)]) for b in range(2)]
            if kind == "sb":
                return [qk[0], qk[1], v[0], qk[2], v[1], qk[3]]
            return [qk[0], qk[1], v[0], qk[2], qk[3], v[1]]

        def width(panel):
            return sum(n for _, _, n in panel[2])

        def staged(kind, g):
            return (g // 2, 256 * (g % 2)) if kind == "swa" else (g % 2, 0)

        def normed(kind, g):
            if g == "kv":
                return qk_st[:, 1, :, 0:P], 2, slice(1, 2)
            return qk_st[:, staged(kind, g)[0]], 8, slice(0, 1) if kind == "swa" else slice(0, 2)

        def by_table(x, tables):
            return x.rearrange("p (q h d) -> p q h d", q=tables.stop - tables.start, d=HD)

        def for_heads(table, heads):
            p, q, d = table.shape
            return table.rearrange("p q (o d) -> p q o d", o=1).broadcast_to([p, q, heads, d])

        def swap_halves(x):
            n = x.shape[-1] // 2
            return x[..., n:2 * n], x[..., 0:n]

        def rope_layers(kind):
            return 1 if kind == "moba" else 2

        def mixer(l):
            kind = KINDS[l]
            j = l // 3
            w_in = {"sb": "sb_w_in", "moba": "moba_w_in", "swa": "swa_w_in"}[kind]
            w_out = {"sb": "sb_w_out", "moba": "moba_w_out", "swa": "swa_w_out"}[kind]
            return kind, w[w_in][j], w[w_out][j]

        LAT_PANELS = [("kv", AK, 256, True), ("dk", DK, 512, True), ("dv", DV, 512, True), ("dab", DAB, 32, True),
                      ("q", AQ, 512, False), ("dq", DQ, 512, False), ("dz", DZ, 512, False)]
        LAT_STEPS = {1: ["kx"], 2: ["kc"], 5: ["q"]}
        LAT_F = DEPTH * (2 * (KT // 2) + 4 + FF // 256) + KT
        CONV = [(dk_c, 1), (dv_c, 2), (dk_x, 1), (dv_x, 2), (dq_x, 0)]

        def lat_heads(what):
            return {"kx": (kva_x[:, :, 0:P], 2), "kc": (kva_c[:, :, 0:P], 2), "q": (aq, 8)}[what]

        def over_heads(row, n):
            return row.rearrange("p (o d) -> p o d", o=1).broadcast_to([P, n, row.shape[-1]])

        def over_elems(cols, d=HD):
            return cols.rearrange("p (h o) -> p h o", o=1).broadcast_to([cols.shape[0], cols.shape[1], d])

        def heads(x, d=HD):
            return x.rearrange("p (h d) -> p h d", d=d)

        def halves32(x):
            return x.rearrange("p (b d) -> p b d", d=32)

        def hcol(h):
            return (h % 2) * 256 + (h // 2) * HD

        def delta_tile(rd, d):
            t = rd % 2 if d == 0 else 1 - rd % 2
            return t, 2 * (rd // 2) + t

        def rows(ap):
            return ap.rearrange("(k p) n -> p k n", p=P)

        ADA_MIX = [{}, {}, {}, {}]
        ADA_UP = [{}, {}, {}, {}]
        ADA_DOWN = [{}, {}, {}, {}]
        for i in range(2 * KT):
            ADA_MIX[0].setdefault(max(0, i - 2), []).append((0, KT + i))
        for l in (1, 2):
            for i in range(KT):
                ADA_MIX[l].setdefault(i + (l == 1), []).append((l + 1, i))
        for l in range(DEPTH):
            first = KT if l in (1, 2) else 0
            for i in range(first, ADA_U):
                p = max(0, i - first - 2)
                if p < FF // 256:
                    ADA_UP[l].setdefault(p, []).append((l + 1, i))
                else:
                    ADA_DOWN[l].setdefault(p - FF // 256, []).append((l + 1, i))
        SUMS = {(l, pos): piece for l in range(DEPTH) for pos, piece in
                (((("up", 2), "c0"), (("up", 9), "r1"), (("up", 10), "c1")) if l in (1, 2) else
                 ((("up", 9), "c0"), (("down", 7), "r1"), (("down", 9), "c1")))}

        def mods(l, piece):
            return 7 * l + {"c0": 1, "r1": 3, "c1": 4, "c2": 5, "r2": 7}[piece]

        def mod_cols(l, piece):
            return {"c0": slice(0, 16), "c1": slice(16, 24), "c2": slice(24, 32)}[piece]

        units, loads, small = [], [], {}

        def add(m, pieces, kts):
            units.append(("unit", [(c0, mm, c1, n) for c0, mm, c1, n in pieces], list(kts), sum(p[3] for p in pieces)))

        mixer_units = []
        for l in range(DEPTH):
            kind, w_in, w_out = mixer(l)
            for what, g, pieces in qkv_panels(kind):
                for h in range(2):
                    add(w_in, [(c0, w_in, c1, n) for c0, c1, n in pieces], range(4 * h, 4 * h + 4))
            for h in range(2):
                for n in range(2):
                    add(w_out, [(0, w_out, 512 * n, 512)], range(4 * h, 4 * h + 4))
            wg, wu, wd = w["ffn_w_gate"][l], w["ffn_w_up"][l], w["ffn_w_down"][l]
            for p in range(FF // 256):
                for h in range(2):
                    add(wg, [(0, wg, 256 * p, 256), (256, wu, 256 * p, 256)], range(4 * h, 4 * h + 4))
            for n in range(2):
                for h in range(6):
                    add(wd, [(0, wd, 512 * n, 512)], range(4 * h, min(4 * h + 4, FFT)))
        u_lat = len(units)
        w_in2 = w["w_in_2"][0]
        for c, n in [(c, n) for _, c, n, _ in LAT_PANELS] + [(GA + 512 * n, 512) for n in range(4)]:
            for h in range(2):
                add(w_in2, [(0, w_in2, c, n)], range(4 * h, 4 * h + 4))
        for m in (w["w_br_attn_2"][0], w["w_br_dn_2"][0]):
            for n in range(2):
                add(m, [(0, m, 512 * n, 512)], range(4))
        for h in range(2):
            for n in range(2):
                add(None, [(0, w["w_out_2"][0], 512 * n, 512)], range(4 * h, 4 * h + 4))
        for part in range(2):
            for p in range(4):
                for h in range(2):
                    add(None, [(0, w["w_mlp1_2"][0], 2048 * part + 512 * p, 512)], range(4 * h, 4 * h + 4))
            for n in range(2):
                for h in range(4):
                    add(None, [(0, w["w_mlp2_2"][0], 512 * n, 512)], range(16 * part + 4 * h, 16 * part + 4 * h + 4))
        def more_units(n, n_mix):
            return 0 if n == 0 else 2 if n == n_mix - 1 else 1

        for n in range(KT):
            if n == 3:
                small[len(loads)] = [("x",)]
            loads.append(("ada", 0, n))
        ahead = iter(units)
        loads += [next(ahead), next(ahead)]
        for l in range(DEPTH):
            small.setdefault(len(loads), []).append(("mixer", l))
            n_mix = 2 * len(qkv_panels(KINDS[l])) + 4
            for n in range(n_mix):
                loads += [next(ahead) for _ in range(more_units(n, n_mix))]
                loads += [("ada", *a) for a in ADA_MIX[l].get(n, [])]
            for p in range(FF // 256):
                loads += [next(ahead) for _ in range(2 if p else 1)]
                loads += [("ada", *a) for a in ADA_UP[l].get(p, [])]
            for j in range(12):
                loads += [next(ahead) for _ in range(1 if j else 2)]
                loads += [("ada", *a) for a in ADA_DOWN[l].get(j, [])]
        small.setdefault(len(loads) + 1, []).append(("lat",))
        n_conv = len(loads) - 2 + 2 * len(LAT_PANELS) + 4
        small.setdefault(n_conv, []).append(("conv",))
        loads += list(ahead)

        SUM_BANKS = {(l, piece): banks for l in range(DEPTH + 1) for piece, banks in
                     (("c0", [A[2]]), ("r1", [A[2], A[3]]), ("c1", [A[2]]), ("c2", [A[2]]), ("r2", [A[3], A[1]]))}
        SUM_BANKS[0, "r1"], SUM_BANKS[0, "c1"] = [A[1], A[2]], [A[0]]

        block = ctx.enter_context(nc.Block())

        @block.sync
        def _(sp):

            def transfers(what):
                if what[0] == "x":
                    sp.dma_start(x_res, w["x"][0].rearrange("(t p) d -> p t d", p=P)).then_inc(x_in, 16)
                elif what[0] == "mixer":
                    l = what[1]
                    kind = KINDS[l]
                    if kind != "sb":
                        if l > 1:
                            sp.wait_ge(x_ready, 4 * l - 2)
                        g_in = w[f"{kind}_qk_gain"]
                        sp.dma_start(rope_g, g_in[l // 3].rearrange("(o q) d -> o q d", o=1).broadcast_to([P, 2, HD])).then_inc(gain_in, 16)
                    if kind == "swa":
                        sp.dma_start(sinks, w["swa_sinks"][l // 3:l // 3 + 1, :].broadcast_to([P, 16])).then_inc(gain_in, 16)
                elif what[0] == "lat":
                    sp.wait_ge(x_ready, 16)
                    sp.dma_start(ctx_raw, w["ctx_2"][0].rearrange("(t p) d -> p t d", p=P)).then_inc(ctx_in, 16)
                    sp.dma_start(mask_st, w["masks_2"].rearrange("c p n -> p c n")).then_inc(masks_in, 16)
                    sp.dma_start(rope_cs, w["rope_2"].rearrange("a (t p) d -> p a t d", p=P)).then_inc(lat_in, 16)
                    sp.dma_start(rope_g[:, 0], w["q_norm_g_2"].broadcast_to([P, HD])).then_inc(lat_in, 16)
                    sp.dma_start(rope_g[:, 1], w["k_norm_g_2"].broadcast_to([P, HD])).then_inc(lat_in, 16)
                    sp.dma_start(sinks[:, 0:LAT_QH], w["attn_sink_2"].broadcast_to([P, LAT_QH])).then_inc(lat_in, 16)
                    sp.dma_start(alog_row, w["a_log_2"].rearrange("o a b -> o (a b)").broadcast_to([P, 16])).then_inc(lat_in, 16)
                    sp.dma_start(dtb_row, w["dt_bias_2"].rearrange("o a b -> o (a b)").broadcast_to([P, 16])).then_inc(lat_in, 16)
                    sp.dma_start(dng_row, w["dn_norm_g_2"].broadcast_to([P, HD])).then_inc(lat_in, 16)
                    sp.wait_ge(sums_done, mods(LAT, "r2"))
                    sp.dma_start(consts_2, w["consts_2"].rearrange("c p n -> p c n")).then_inc(lat_in, 16)
                elif what[0] == "conv":
                    sp.wait_ge(split_lo, LAT_F + 2)
                    sp.dma_start(conv_rows, w["conv_w_2"].broadcast_to([P, 3, 1536])).then_inc(cw_in, 16)
                    for a, (x, _) in enumerate(CONV):
                        if a:
                            sp.wait_ge(conv_ready, a)
                        sp.dma_start(prev[1:P], x[0:P - 1]).then_inc(shift_in, 16)
                        sp.dma_start(prev[0:1, 1], x[P - 1:P, 0]).then_inc(shift_in, 16)
                        sp.dma_start(prev[0:1, 0], w["zeros"]).then_inc(shift_in, 16)
                        sp.dma_start(nxt[0:P - 1], x[1:P]).then_inc(shift_in, 16)
                        sp.dma_start(nxt[P - 1:P, 0], x[0:1, 1]).then_inc(shift_in, 16)
                        sp.dma_start(nxt[P - 1:P, 1], w["zeros"]).then_inc(shift_in, 16)

            sp.dma_start(cols_in, w["cols"]).then_inc(const_in, 16)
            sp.dma_start(consts, w["consts"].rearrange("c p n -> p c n")).then_inc(const_in, 16)
            sp.dma_start(rope_cs, w["rope"].rearrange("a (t p) d -> p a t d", p=P)).then_inc(rope_in, 16)
            for s, load in enumerate(loads):
                for what in small.get(s, []):
                    transfers(what)
                slot = s % RING
                if s >= RING:
                    sp.wait_ge(raw_free, s - RING + 1)
                if load[0] == "unit":
                    _, pieces, kts, _ = load
                    dst = raw[:, slot].rearrange("p (k n) -> p k n", k=UNIT_K)
                    for c0, m, c1, n in pieces:
                        sp.dma_start(dst[:, 0:len(kts), c0:c0 + n], rows(m)[:, kts[0]:kts[0] + len(kts), c1:c1 + n]).then_inc(landed[slot], 16)
                else:
                    _, l, n = load
                    sp.dma_start(raw[:, slot], (w["ada_w"][l] if l < LAT else w["w_ada_2"][0]).rearrange("(k p) (c n) -> p c k n", p=P, c=3)[:, n // KT, n % KT])\
                        .then_inc(landed[slot], 16)
            sp.wait_ge(x_ready, 4 * DEPTH + 6)
            sp.dma_start(out.rearrange("b (t p) d -> p (b t) d", p=P), x_res).then_inc(out_done, 16)
            sp.wait_ge(out_done, 16)

        @block.gpsimd
        def _(pool):
            chain = [0]

            def link(ins):
                chain[0] += 1
                ins.then_inc(pool_step, 1)
                pool.wait_ge(pool_step, chain[0])

            def tables(kind):
                pool.wait_ge(rope_in, 16)
                pool.wait_ge(gain_in, 16 if kind == "moba" else 48)
                q_gain = rope_g[:, 0]
                link(nc.gpsimd.tensor_scalar(q_gain, q_gain, HD ** -0.5, None, ALU.mult))
                for t in range(NT):
                    def both(x):
                        n = x.shape[-1]
                        return x.rearrange("p (o d) -> p o d", o=1).broadcast_to([P, 2, n])
                    nc.gpsimd.tensor_tensor(rope_t[:, 0, t], both(rope_cs[:, 0, t]), rope_g, ALU.mult)
                    for a, b in ((0, 32), (32, 0)):
                        ins = nc.gpsimd.tensor_tensor(rope_t[:, 1, t, :, a:a + 32], both(rope_cs[:, 1, t, a:a + 32]), rope_g[:, :, b:b + 32], ALU.mult)
                link(ins)
                pool.sem_inc(rope_ready, 1)

            def rotate(kind, g):
                k.norms += 1
                x, heads, tabs = normed(kind, g)
                pool.wait_ge(xn_ready, k.norms)
                for t in range(NT):
                    src, dst = by_table(x[:, t], tabs), by_table(e_sb[:, t, 0:heads * HD], tabs)
                    for a, b in ((0, 32), (32, 0)):
                        ins = nc.gpsimd.tensor_tensor(dst[:, :, :, a:a + 32], src[:, :, :, b:b + 32],
                                                      for_heads(rope_t[:, 1, t, tabs, a:a + 32], heads // (tabs.stop - tabs.start)), ALU.mult)
                ins.then_inc(rot_ready, 1)

            k = Walk()

            def start_sums(b):
                if b >= 2:
                    l, j = (b - 2) // 3, (b - 2) % 3
                    pool.wait_ge(sums_done, mods(l, ("c0", "c1", "r2")[j]))
                l, j = b // 3, b % 3
                nc.gpsimd.memset(acc[:, b % 2], 0.0).then_inc(acc_zero, 1)
                pool.wait_ge(acc_zero, b + 1)
                bias = w["ada_b"][l:l + 1] if l < LAT else w["b_ada_2"]
                nc.gpsimd.dma_start(acc[0:1, b % 2], bias[:, 2 * D * j:2 * D * j + 2 * D]).then_inc(bias_in[b % 2], 16)

            blocks = iter(range(3 * (DEPTH + 1)))
            for _ in range(3):
                start_sums(next(blocks))
            f = 0
            for l in range(DEPTH):
                kind, _, _ = mixer(l)
                if kind != "sb":
                    tables(kind)
                    for n in sorted(SLOTS[kind]):
                        for step, g in SLOTS[kind][n]:
                            if step == "N":
                                rotate(kind, g)
                f += KT // 2 + 4
                if l == DEPTH - 1:
                    pool.wait_ge(split_lo, f)
                    nc.gpsimd.memset(acc_c, 0.0).then_inc(accc_zero, 1)
                    pool.wait_ge(accc_zero, 1)
                    nc.gpsimd.dma_start(acc_c[0:1, :], w["b_ada_2"][:, 0:2 * D]).then_inc(biasc_in, 16)
                for _ in range(5 if l == 0 else 3):
                    b = next(blocks, None)
                    if b is not None:
                        start_sums(b)
                f += KT // 2 + FF // 256

            pool.wait_ge(masks_in, 16)
            pool.wait_ge(sums_done, mods(LAT, "r2"))
            nc.gpsimd.tensor_copy(masks_2, mask_st).then_inc(masks_ready, 1)
            pool.wait_ge(lat_in, 128)
            q_gain = rope_g[:, 0]
            link(nc.gpsimd.tensor_scalar(q_gain, q_gain, HD ** -0.5, None, ALU.mult))
            for t in range(NT):
                nc.gpsimd.tensor_tensor(rope_t[:, 0, t], over_heads(rope_cs[:, 0, t], 2), rope_g, ALU.mult)
                for q in range(2):
                    dst, sin, gain = halves32(rope_t[:, 1, t, q]), halves32(rope_cs[:, 1, t]), halves32(rope_g[:, q])
                    for a, b in ((0, 16), (16, 0)):
                        ins = nc.gpsimd.tensor_tensor(dst[:, :, a:a + 16], sin[:, :, a:a + 16], gain[:, :, b:b + 16], ALU.mult)
            link(ins)
            pool.sem_inc(rope2_ready, 1)
            for what in ("kx", "kc", "q"):
                k.norms += 1
                if what == "kc":
                    continue
                x, nh = lat_heads(what)
                pool.wait_ge(xn_ready, k.norms)
                for t in range(NT):
                    for blk in range(2):
                        o = 32 * blk
                        table = rope_t[:, 1, t, 0 if what == "q" else 1]
                        for a, b in ((0, 16), (16, 0)):
                            ins = nc.gpsimd.tensor_tensor(heads(lrot[:, t, 0:nh * HD])[:, :, o + a:o + a + 16], heads(x[:, t])[:, :, o + b:o + b + 16],
                                                          over_heads(table[:, o + a:o + a + 16], nh), ALU.mult)
                ins.then_inc(rot_ready, 1)
            nc.gpsimd.memset(state, 0.0).then_inc(state_zero, 1)
            pool.wait_ge(beg_ready, 1)
            pool.wait_ge(l2_ready, 3)
            pool.wait_ge(cs_ready, 5)
            for rd in range(4):
                lat = rd >= 2
                for d in range(2):
                    bd = 2 * rd + d
                    t, st = delta_tile(rd, d)
                    kk, vv = (dk_x, dv_x) if lat else (dk_c, dv_c)
                    if bd:
                        pool.wait_ge(uv_done, 2 * bd)
                    if rd:
                        pool.wait_ge(su_done, 2 * rd)
                    nc.gpsimd.tensor_tensor(heads(bek), heads(kk[:, t]), over_elems(beG[:, d, st]), ALU.mult)
                    nc.gpsimd.tensor_tensor(heads(bv), heads(vv[:, t]), over_elems(beta[:, st, d]), ALU.mult)
                    ins = nc.gpsimd.tensor_tensor(heads(k_tail[:, d]), heads(kk[:, t]), over_elems(e_tail[:, d, st]), ALU.mult)
                    if lat:
                        if bd > 4:
                            pool.wait_ge(qdT_done, 2 * (bd - 4))
                        ins = nc.gpsimd.tensor_tensor(heads(q_dec), heads(dq_x[:, t]), over_elems(e_G[:, d, st]), ALU.mult)
                    ins.then_inc(prep_ready, 1)

        @block.scalar
        def _(act):
            k = Walk()

            def convert():
                if k.u == len(units):
                    return
                slot, count, (_, _, kts, n) = k.next_load(loads, "unit")
                u = k.u
                k.u += 1
                act.wait_ge(landed[slot], count)
                if u >= 2:
                    act.wait_ge(gemm_done, u - 1)
                nc.scalar.copy(w_hi[:, u % 2, 0:len(kts), 0:n], raw[:, slot].rearrange("p (k n) -> p k n", k=UNIT_K)[:, 0:len(kts), 0:n])\
                    .then_inc(hi_ready, 1)

            def modulation(l, piece):
                for i in range(1 if piece[0] == "c" else 2):
                    k.sums += 1
                    act.wait_ge(sums_done, k.sums)
                    bank = SUM_BANKS[l, piece][i]
                    if piece[0] == "r":
                        dst = gates[:, int(piece[1]) - 1, 512 * i:512 * i + 512]
                        nc.scalar.copy(dst, bank).then_inc(mod_out, 1)
                    else:
                        dst = mod[:, l % 2, mod_cols(l, piece)]
                        n = dst.shape[-1]
                        if l == LAT and piece == "c0":
                            nc.scalar.copy(mod[:, l % 2, 32:48], bank[:, 16:32])
                        nc.scalar.copy(dst, bank[:, 0:n]).then_inc(mod_out, 1)

            def split(dst_hi, emit_full):
                f = k.f
                k.f += 1
                if f >= 2:
                    act.wait_ge(split_lo, f - 1)
                emit_full(full[:, f % 2]).then_inc(split_full, 1)
                act.wait_ge(split_full, f + 1)
                nc.scalar.copy(dst_hi, full[:, f % 2].rearrange("p (a n) -> p a n", n=SEQ)).then_inc(split_hi, 1)

            def rsqrt(n):
                k.rms += 1
                act.wait_ge(v_ready, k.rms)
                nc.scalar.activation(rms_y[:, 0:n], rms_v[:, 0:n], ACT.Ln).then_inc(exp_ready, 1)
                n_exp[0] += 1
                act.wait_ge(exp_ready, n_exp[0])
                nc.scalar.activation(rms_y[:, 0:n], rms_y[:, 0:n], ACT.Exp, scale=-0.5).then_inc(y_ready, 1)

            def squares(half, x=x_res):
                sl = slice(512 * half, 512 * half + 512)
                for t in range(NT):
                    ins = nc.scalar.activation(n_st[:, t, sl], x[:, t, sl], ACT.Square, accum_out=ssq[:, t, half:half + 1])
                ins.then_inc(ss_ready, 1)

            def norm(l, which, gain, dst=h_hi, sums=None):
                m = k.m
                k.m += 1
                rsqrt(NT)
                for piece in sums or []:
                    modulation(l, piece)
                act.wait_ge(gsc_ready, m + 1)
                for q in range(KT // 2):
                    act.wait_ge(norm_T, 4 * m + q + 1)

                    def emit(dst):
                        for i in range(2):
                            c = 2 * q + i
                            ins = nc.scalar.activation(dst[:, i * SEQ:(i + 1) * SEQ], A[q][:, i * SEQ:(i + 1) * SEQ], ACT.Identity,
                                                       scale=gsc[:, l % 2, gain + c:gain + c + 1],
                                                       bias=mod[:, l % 2, which + c:which + c + 1])
                        return ins
                    split(dst[:, 2 * q:2 * q + 2], emit)

            n_exp = [0]

            def evac_panel(u_end, what, g):
                act.wait_ge(gemm_done, u_end)
                pn = k.panel("act")
                if what == "q" and g == 1:
                    act.wait_ge(kvT_done, k.swa + 1)
                for t in range(NT):
                    bank = G[2 * (pn % 2) + t]
                    if what == "kv":
                        nc.scalar.copy(qk_st[:, 1, t, 0:P], bank[:, 0:P])
                        ins = nc.scalar.copy(v_st[:, 0, t, 0:P], bank[:, P:2 * P])
                    else:
                        ins = nc.scalar.copy((v_st if what == "v" else qk_st)[:, g % 2, t], bank)
                ins.then_inc(free_act, 1)

            def step_softmax(step, g, kind):
                if step == "N":
                    act.wait_ge(free_act, k.free_act)
                    if k.norms:
                        act.wait_ge(qk_ready, k.norms)
                    k.norms += 1
                    x, heads, _ = normed(kind, g)
                    nc.scalar.activation(e_sb[:, 0:NT, 0:heads * HD], x, ACT.Square).then_inc(sq_ready, 1)
                    rsqrt(NT * heads)
                    return
                if g == "kv":
                    return
                n = k.group + g
                if step == "T":
                    act.wait_ge(qkT_done, 2 * n + (2 if kind == "swa" else 1))
                    nc.scalar.copy(qT, A[0].rearrange("p (a n) -> p a n", a=2)).then_inc(qT_ready, 1)
                elif step == "S":
                    act.wait_ge(max_ready, k.sm + g + 1)
                    for b in (2, 0, 1):
                        for h in ((0, 2, 1, 3), (0, 2), (1, 3))[(2, 0, 1).index(b)]:
                            par, i = h % 2, h // 2
                            c = (0 if b == 2 else 4) + 2 * par + i
                            if b == 2:
                                src = A[2 + par][:, i * P:i * P + P]
                                dst = z_sb[:, 2, par * SEQ + i * P:par * SEQ + i * P + P]
                            else:
                                src, dst = A[par][:, i * SEQ:i * SEQ + SEQ], z_sb[:, par, i * SEQ:i * SEQ + SEQ]
                            ins = nc.scalar.activation(dst, src, ACT.Exp, bias=n_max[:, c:c + 1], accum_out=p_sum[:, c:c + 1])
                        ins.then_inc(p_ready, 1)
                    if kind == "swa":
                        act.wait_ge(sink_ready, 4 * k.swa + g + 1)
                        nc.scalar.activation(sink_e, sink_e, ACT.Exp).then_inc(se_ready, 1)
                elif step == "C":
                    for o, b in enumerate((2, 0, 1)):
                        act.wait_ge(pT_done, 3 * (k.sm + g) + o + 1)
                        nc.scalar.copy(aT[:, b], A[b]).then_inc(aT_ready, 1)
                elif step == "V":
                    act.wait_ge(av_done, n + 1)
                    split(act_hi[:, 2 * g:2 * g + 2], lambda dst: nc.scalar.copy(dst, A[3]))

            def step_sb(step, g):
                n = k.group + g
                ns = k.sb + g
                if step == "T":
                    act.wait_ge(qkT_done, 2 * n + 1)
                    nc.scalar.activation(qT, A[0].rearrange("p (a n) -> p a n", a=2), ACT.Copy, scale=HD ** -0.5).then_inc(qT_ready, 1)
                elif step == "S":
                    for b in (2, 0, 1):
                        o = (2, 0, 1).index(b)
                        act.wait_ge(z_done, 3 * ns + o + 1)
                        if b == 2:
                            nc.scalar.copy(z_sb[:, 2, 0:SEQ], A[2][:, 0:SEQ])
                            nc.scalar.copy(z_sb[:, 2, SEQ:2 * SEQ], A[3][:, 0:SEQ]).then_inc(z_copied, 1)
                        else:
                            nc.scalar.copy(z_sb[:, b], A[b]).then_inc(z_copied, 1)
                    for b in (2, 0, 1):
                        o = (2, 0, 1).index(b)
                        act.wait_ge(nabs_ready, 3 * ns + o + 1)
                        nc.scalar.activation(e_sb[:, b], e_sb[:, b], ACT.Exp).then_inc(exp_ready, 1)
                        n_exp[0] += 1
                        act.wait_ge(exp_ready, n_exp[0])
                        nc.scalar.activation(e_sb[:, b], e_sb[:, b], ACT.Ln, bias=1.0).then_inc(ln_ready, 1)
                elif step == "C":
                    for b in (2, 0, 1):
                        o = (2, 0, 1).index(b)
                        act.wait_ge(d_ready, 3 * ns + o + 1)
                        nc.scalar.activation(aT[:, b], aT[:, b], ACT.Exp).then_inc(aT_ready, 1)
                elif step == "V":
                    act.wait_ge(av_done, n + 1)
                    split(act_hi[:, 2 * g:2 * g + 2], lambda dst: nc.scalar.copy(dst, A[3]))

            act.wait_ge(cols_T, 1)
            nc.scalar.copy(cols, A[0][:, 0:NCOL]).then_inc(cols_ready, 1)
            act.wait_ge(cols_ready, 1)
            nc.scalar.activation(c_col, cols[:, 64:88], ACT.Silu).then_inc(c_ready, 1)
            convert()
            convert()
            modulation(0, "c0")
            nc.scalar.preload_act_table_set("natural_log_exp_and_others")
            act.wait_ge(x_in, 16)
            squares(0)
            for l in range(DEPTH):
                kind, _, _ = mixer(l)
                if l:
                    act.wait_ge(x_ready, 4 * l)
                squares(1)
                norm(l, 0, 0, sums=["c2", "r2"] if l else None)
                panels = qkv_panels(kind)
                u0 = k.u - 2
                nq = 2 * len(panels)
                for n in range(nq + 4):
                    if n % 2 == 0 and 0 < n <= nq:
                        what, g, _ = panels[n // 2 - 1]
                        evac_panel(u0 + n, what, g)
                    if n:
                        convert()
                    if n == nq + 3:
                        act.wait_ge(x_ready, 4 * l + 1)
                        squares(0)
                        convert()
                    for step, g in SLOTS[kind].get(n, []):
                        (step_sb(step, g) if kind == "sb" else step_softmax(step, g, kind))
                    if l == 0 and n == nq + 1:
                        modulation(0, "r1")
                        modulation(0, "c1")
                k.panel("dve")
                k.panel("dve")
                k.end_mixer(kind)
                act.wait_ge(x_ready, 4 * l + 2)
                squares(1)
                norm(l, 16, 8, sums=None if l else ["c2", "r2"])
                nc.scalar.preload_act_table(ACT.Silu)
                uf = k.u - 2

                def silu(p):
                    act.wait_ge(gemm_done, uf + 2 * p + 2)
                    pn = k.panel("dve")
                    if p >= 1:
                        act.wait_ge(act_ready, (FF // 256) * l + p)
                    for t in range(NT):
                        ins = nc.scalar.activation(silu_st[:, t], G[2 * (pn % 2) + t][:, 0:256], ACT.Silu)
                    ins.then_inc(silu_ready, 1)

                def split_act(p):
                    act.wait_ge(actT_done, (FF // 256) * l + p + 1)
                    split(act_hi[:, 2 * p:2 * p + 2], lambda dst: nc.scalar.copy(dst, A[p % 2]))

                for p in range(FF // 256):
                    convert()
                    if p >= 1:
                        silu(p - 1)
                        convert()
                        split_act(p - 1)
                    if (l, ("up", p - 1)) in SUMS:
                        modulation(l + 1, SUMS[l, ("up", p - 1)])
                for j in range(12):
                    convert()
                    if j == 0:
                        silu(FF // 256 - 1)
                        nc.scalar.preload_act_table_set("natural_log_exp_and_others")
                        convert()
                        split_act(FF // 256 - 1)
                        if (l, ("up", FF // 256 - 1)) in SUMS:
                            modulation(l + 1, SUMS[l, ("up", FF // 256 - 1)])
                    if (l, ("down", j - 1)) in SUMS:
                        modulation(l + 1, SUMS[l, ("down", j - 1)])
                    if j == 9:
                        act.wait_ge(x_ready, 4 * l + 3)
                        squares(0)
                k.panel("dve")
                k.panel("dve")

            act.wait_ge(x_ready, 4 * LAT)
            squares(1)
            norm(LAT, 0, 0, sums=["c2", "r2"])
            act.wait_ge(ctx_in, 16)
            squares(0, ctx_raw)
            squares(1, ctx_raw)
            norm(LAT, 32, 16, act_hi)
            u0 = k.u - 2

            def square(x, n, dst):
                k.norms += 1
                nc.scalar.activation(dst, x, ACT.Square).then_inc(sq_ready, 1)
                rsqrt(n)

            dsts = {"kv": (kva_x, kva_c), "dk": (dk_x, dk_c), "dv": (dv_x, dv_c), "dab": (dab[:, 2:4], dab[:, 0:2]),
                    "q": (aq,), "dq": (dq_x,), "dz": (dz,)}
            for pi, (what, _, n, _) in enumerate(LAT_PANELS):
                convert()
                convert()
                act.wait_ge(gemm_done, u0 + 2 * pi + 2)
                if what == "dk":
                    act.wait_ge(masks_ready, 1)
                for dst in dsts[what]:
                    pn = k.panel("act")
                    for t in range(NT):
                        ins = nc.scalar.copy(dst[:, t], G[2 * (pn % 2) + t][:, 0:n])
                    ins.then_inc(free_act, 1)
                for step in LAT_STEPS.get(pi, []):
                    act.wait_ge(free_act, k.free_act)
                    act.wait_ge(qk_ready, k.norms)
                    x, nh = lat_heads(step)
                    square(x, NT * nh, lrot[:, :, 0:nh * HD])
            act.wait_ge(ltT_done, 1)
            nc.scalar.copy(lkT[:, 0], A[0]).then_inc(kq_act, 1)
            act.wait_ge(ltT_done, 3)
            nc.scalar.copy(lqT[:, 0:2].rearrange("p a n -> p (a n)"), A[2]).then_inc(kq_act, 1)
            for s in range(4):
                act.wait_ge(wmax_ready, s + 1)
                for b in range(4):
                    ins = nc.scalar.activation(p_sb[:, b], A[b], ACT.Exp, bias=n_max[:, b:b + 1], accum_out=p_sum[:, b:b + 1])
                ins.then_inc(wp_ready, 1)
                nc.scalar.activation(sink_e[:, 0:4], sink_e[:, 0:4], ACT.Exp).then_inc(wse_ready, 1)
                for b in (0, 2):
                    act.wait_ge(wpT_done, 4 * s + b + 1)
                    nc.scalar.copy(laT[:, b], A[b]).then_inc(waT_act, 1)
                if s % 2:
                    act.wait_ge(woT_done, s + 1)

                    def emit(dst):
                        for i in range(2):
                            ins = nc.scalar.copy(dst[:, i * SEQ:i * SEQ + SEQ], G[s - 1 + i][:, 0:SEQ])
                        return ins
                    split(act_hi[:, s - 1:s + 1], emit)
            nc.scalar.preload_act_table(ACT.Silu)
            nc.scalar.activation(dz, dz, ACT.Silu).then_inc(cs_ready, 1)
            for a, (x, _) in enumerate(CONV):
                act.wait_ge(conv_ready, a + 1)
                nc.scalar.activation(x, x, ACT.Silu).then_inc(cs_ready, 1)
            nc.scalar.preload_act_table_set("natural_log_exp_and_others")
            for a, x in ((0, dk_c), (2, dk_x), (4, dq_x)):
                act.wait_ge(cs_ready, a + 2)
                if a:
                    act.wait_ge(l2_ready, a // 2)
                square(x, 16, sq_t)
            act.wait_ge(gz_ready, 1)
            nc.scalar.activation(gate_s, gate_s, ACT.Exp).then_inc(ge_ready, 1)
            act.wait_ge(ge_ready, 1)
            nc.scalar.activation(gate_s, gate_s, ACT.Ln, bias=1.0).then_inc(gl_ready, 1)
            nc.scalar.activation(alog_row, alog_row, ACT.Exp).then_inc(ea_ready, 1)
            act.wait_ge(gates_ready, 1)
            nc.scalar.activation(beta, lnb_all.rearrange("p s (d h) -> p s d h", d=2), ACT.Exp).then_inc(beta_ready, 1)
            act.wait_ge(gsum_done, 1)
            nc.scalar.activation(neg_G.rearrange("p d s h -> p (d s h)"), A[0][:, 0:64], ACT.Copy, scale=-1.0)
            nc.scalar.activation(e_G.rearrange("p d s h -> p (d s h)"), A[0][:, 0:64], ACT.Exp)
            nc.scalar.activation(e_tail.rearrange("p d s h -> p (d s h)"), A[0][:, 64:128], ACT.Exp)
            nc.scalar.activation(e_last.rearrange("p c h -> p (c h)"), A[1][:, 0:64], ACT.Exp).then_inc(eg_ready, 1)
            for i, dst in enumerate((kT_c, kT_x, qT_x)):
                act.wait_ge(dT_done, 2 * i + 1)
                nc.scalar.copy(dst[:, 0:2].rearrange("p a n -> p (a n)"), (A[2], G[0], G[2])[i]).then_inc(dT_act, 1)
            act.wait_ge(eg_ready, 1)
            for rd in range(4):
                lat = rd >= 2
                for d in range(2):
                    bd = 2 * rd + d
                    t, st = delta_tile(rd, d)
                    for r in range(2):
                        act.wait_ge(e_done, 2 * bd + r + 1)
                        for i in range(4):
                            h = 2 * i + r
                            ins = nc.scalar.activation(LT[:, r, i * P:i * P + P], A[r][:, i * P:i * P + P], ACT.Exp, bias=neg_G[:, d, st, h:h + 1])
                        ins.then_inc(E_ready, 1)
                    for r in range(2):
                        act.wait_ge(uv_done, 2 * bd + r + 1)
                        for c in range(2):
                            step = c if d == 0 else 1 - c
                            ins = nc.scalar.copy(u_st[CH * c:CH * c + CH, step, 256 * r:256 * r + 256], A[r][CH * c:CH * c + CH, 0:256])
                        ins.then_inc(uv_ready, 1)
                    if lat:
                        for r in range(2):
                            act.wait_ge(in_done, 2 * (bd - 4) + r + 1)
                            for i in range(4):
                                h = 2 * i + r
                                ins = nc.scalar.activation(intraT[:, d, r, i * P:i * P + P], G[r][:, i * P:i * P + P], ACT.Exp, bias=neg_G[:, d, st, h:h + 1])
                            ins.then_inc(ie_ready, 1)
                        for r in range(2):
                            act.wait_ge(qdT_done, 2 * (bd - 4) + r + 1)
                            nc.scalar.copy(q_decT[CH * d:CH * d + CH, r], A[r][CH * d:CH * d + CH, :]).then_inc(qdT_ready, 1)
                act.wait_ge(wT_done, 2 * rd + 2)
                for r in range(2):
                    ins = nc.scalar.copy(wT[:, r], G[2 + r])
                ins.then_inc(wT_ready, 1)
            act.wait_ge(oacc_ready, 2)
            square(o_dn, 16, sq_t)
            for q in range(2):
                act.wait_ge(ydT_done, q + 1)
                split(act_hi[:, 4 + 2 * q:6 + 2 * q], lambda dst: nc.scalar.copy(dst, A[q]))
            nc.scalar.preload_act_table(ACT.Sigmoid)
            um = k.u - 2
            for n in range(4):
                convert()
                convert()
                act.wait_ge(gemm_done, um + 2 * n + 2)
                pn = k.panel("act")
                for t in range(NT):
                    ins = nc.scalar.activation(sig[:, n // 2, t, 512 * (n % 2):512 * (n % 2) + 512], G[2 * (pn % 2) + t], ACT.Sigmoid)
                ins.then_inc(free_act, 1)
            for n in range(4):
                convert()
                k.panel("dve")
            for q in range(4):
                act.wait_ge(yT_done, q + 1)
                split(h_hi[:, 2 * q:2 * q + 2], lambda dst: nc.scalar.copy(dst, A[q]))
            nc.scalar.preload_act_table_set("natural_log_exp_and_others")
            convert()
            convert()
            convert()
            act.wait_ge(x_ready, 4 * LAT + 1)
            squares(0)
            convert()
            k.panel("dve")
            k.panel("dve")
            act.wait_ge(x_ready, 4 * LAT + 2)
            squares(1)
            norm(LAT, 16, 8)
            um = k.u - 2

            def relu(p, u_end):
                act.wait_ge(gemm_done, u_end)
                pn = k.panel("dve")
                if p >= 1:
                    act.wait_ge(hid_ready, p)
                if p == 4:
                    act.wait_ge(x_ready, 4 * LAT + 4)
                for t in range(NT):
                    ins = nc.scalar.activation(relu_st[:, t], G[2 * (pn % 2) + t], ACT.Relu)
                ins.then_inc(relu_ready, 1)

            def split_hidden(p):
                for q in range(2):
                    act.wait_ge(hidT_done, 2 * p + q + 1)
                    kt = 4 * (p % 4) + 2 * q
                    split(act_hi[:, kt:kt + 2], lambda dst: nc.scalar.copy(dst, A[2 * (p % 2) + q]))

            for part in range(2):
                for p in range(4):
                    hp = 4 * part + p
                    if p >= 1:
                        relu(hp - 1, um + 16 * part + 2 * p)
                    convert()
                    if p >= 1:
                        split_hidden(hp - 1)
                    convert()
                for j in range(8):
                    if j == 0:
                        relu(4 * part + 3, um + 16 * part + 8)
                    convert()
                    if j == 0:
                        split_hidden(4 * part + 3)
                k.panel("dve")
                k.panel("dve")

        @block.vector
        def _(dve):
            k = Walk()
            chain = [0]

            def link(ins):
                chain[0] += 1
                ins.then_inc(dve_step, 1)
                dve.wait_ge(dve_step, chain[0])

            def convert():
                if k.u == len(units):
                    return
                slot, _, (_, _, kts, n) = k.next_load(loads, "unit")
                u = k.u
                k.u += 1
                dve.wait_ge(hi_ready, u + 1)
                if u >= 2:
                    dve.wait_ge(gemm_done, u - 1)
                nc.vector.tensor_tensor(w_lo[:, u % 2, 0:len(kts), 0:n], raw[:, slot].rearrange("p (k n) -> p k n", k=UNIT_K)[:, 0:len(kts), 0:n],
                                        w_hi[:, u % 2, 0:len(kts), 0:n].bitcast(F32), ALU.subtract).then_inc(lo_ready, 1)
                dve.wait_ge(lo_ready, u + 1)
                dve.sem_inc(raw_free, 1)

            def modulation_units():
                while k.s < len(loads) and loads[k.s][0] == "ada":
                    slot, count, (_, l, n) = k.next_load(loads, "ada")
                    b = 3 * l + n // KT
                    dve.wait_ge(landed[slot], count)
                    if n % KT == 0:
                        dve.wait_ge(bias_in[b % 2], 16 * (b // 2 + 1))
                    else:
                        dve.wait_ge(acc_done, k.a)
                    c = (KT if l == LAT else 0) + n % KT
                    nc.vector.scalar_tensor_tensor(out=acc[:, b % 2], in0=raw[:, slot], scalar=c_col[:, c:c + 1], in1=acc[:, b % 2],
                                                   op0=ALU.mult, op1=ALU.add).then_inc(acc_done, 1)
                    k.a += 1
                    if l == LAT and n < KT:
                        if n == 0:
                            dve.wait_ge(biasc_in, 16)
                        else:
                            dve.wait_ge(accc_done, n)
                        nc.vector.scalar_tensor_tensor(out=acc_c, in0=raw[:, slot], scalar=c_col[:, 2 * KT + n:2 * KT + n + 1], in1=acc_c,
                                                       op0=ALU.mult, op1=ALU.add).then_inc(accc_done, 1)
                        dve.wait_ge(accc_done, n + 1)
                    dve.wait_ge(acc_done, k.a)
                    dve.sem_inc(raw_free, 1)

            def split(dst_lo, dst_hi):
                f = k.f
                k.f += 1
                dve.wait_ge(split_hi, f + 1)
                nc.vector.tensor_tensor(dst_lo, full[:, f % 2].rearrange("p (a n) -> p a n", n=SEQ), dst_hi.bitcast(F32),
                                        ALU.subtract).then_inc(split_lo, 1)

            def rsqrt(ss, n, width, eps=EPS):
                k.rms += 1
                v, y, t = rms_v[:, 0:n], rms_y[:, 0:n], rms_t[:, 0:n]
                nc.vector.tensor_scalar(v, ss, 1.0 / width, eps, ALU.mult, ALU.add).then_inc(v_ready, 1)
                dve.wait_ge(y_ready, k.rms)
                link(nc.vector.tensor_tensor(t, y, y, ALU.mult))
                link(nc.vector.tensor_tensor(t, t, v, ALU.mult))
                link(nc.vector.tensor_scalar(t, t, -0.5, 1.5, ALU.mult, ALU.add))
                link(nc.vector.tensor_tensor(y, y, t, ALU.mult))

            def gains(l, which, scale, col):
                return nc.vector.scalar_tensor_tensor(out=gsc[:, l % 2, which:which + 8], in0=mod[:, l % 2, scale:scale + 8], scalar=1.0,
                                                      in1=cols[:, col:col + 8], op0=ALU.add, op1=ALU.mult)

            def norm(x=x_res, lo=h_lo, hi=h_hi, late=lambda: None, between=lambda: None):
                m = k.m
                k.m += 1
                dve.wait_ge(ss_ready, 2 * m + 2)
                link(nc.vector.tensor_tensor(ssum, ssq[:, :, 0], ssq[:, :, 1], ALU.add))
                rsqrt(ssum, NT, D)
                for t in range(NT):
                    nc.vector.tensor_scalar(n_st[:, t], x[:, t], rms_y[:, t:t + 1], None, ALU.mult).then_inc(n_ready, 1)
                late()
                between()
                for q in range(KT // 2):
                    split(lo[:, 2 * q:2 * q + 2], hi[:, 2 * q:2 * q + 2])

            def residual(u_end, n, gate, l):
                dve.wait_ge(gemm_done, u_end)
                dve.wait_ge(mod_out, mods(l, ("r1", "r2")[gate]))
                pn = k.panel("dve")
                sl = slice(512 * n, 512 * n + 512)
                for t in range(NT):
                    ins = nc.vector.tensor_tensor(n_st[:, t, sl], G[2 * (pn % 2) + t], gates[:, gate, sl], ALU.mult)
                ins.then_inc(free_dve, 1)
                dve.wait_ge(free_dve, k.free_dve)
                for t in range(NT):
                    ins = nc.vector.tensor_tensor(x_res[:, t, sl], x_res[:, t, sl], n_st[:, t, sl], ALU.add)
                ins.then_inc(x_ready, 1)

            def step_sb(step, g):
                n = k.group + g
                ns = k.sb + g
                if step == "T":
                    dve.wait_ge(qkT_done, 2 * n + 2)
                    nc.vector.tensor_copy(kT, A[1].rearrange("p (a n) -> p a n", a=2)).then_inc(kT_ready, 1)
                elif step == "S":
                    for o, b in enumerate((2, 0, 1)):
                        dve.wait_ge(z_copied, 3 * ns + o + 1)
                        nc.vector.scalar_tensor_tensor(out=e_sb[:, b], in0=z_sb[:, b], scalar=-1.0, in1=z_sb[:, b],
                                                       op0=ALU.mult, op1=ALU.min).then_inc(nabs_ready, 1)
                    for o, b in enumerate((2, 0, 1)):
                        dve.wait_ge(ln_ready, 3 * ns + o + 1)
                        nc.vector.scalar_tensor_tensor(out=e_sb[:, b], in0=z_sb[:, b], scalar=0.0, in1=e_sb[:, b],
                                                       op0=ALU.max, op1=ALU.add).then_inc(sp_ready, 1)
                elif step == "C":
                    for o, b in enumerate((2, 0, 1)):
                        dve.wait_ge(r_done, 3 * ns + o + 1)
                        nc.vector.tensor_tensor(aT[:, b], z_sb[:, b], A[b], ALU.subtract).then_inc(d_ready, 1)
                elif step == "V":
                    split(act_lo[:, 2 * g:2 * g + 2], act_hi[:, 2 * g:2 * g + 2])

            def step_softmax(step, g, kind):
                n = k.group + g if g != "kv" else 0
                if step == "N":
                    k.norms += 1
                    x, heads, tables = normed(kind, g)
                    per_table = heads // (tables.stop - tables.start)
                    dve.wait_ge(sq_ready, k.norms)
                    link(nc.vector.tensor_reduce(ss16[:, 0:NT * heads].rearrange("p (t h) -> p t h", t=NT),
                                                 e_sb[:, 0:NT, 0:heads * HD].rearrange("p t (h d) -> p t h d", d=HD), AX.X, ALU.add))
                    rsqrt(ss16[:, 0:NT * heads], NT * heads, HD)
                    for t in range(NT):
                        xt = x[:, t].rearrange("p (h d) -> p h d", d=HD)
                        r = rms_y[:, t * heads:(t + 1) * heads].rearrange("p (h o) -> p h o", o=1).broadcast_to([P, heads, HD])
                        ins = nc.vector.tensor_tensor(xt, xt, r, ALU.mult)
                    ins.then_inc(xn_ready, 1)
                    dve.wait_ge(xn_ready, k.norms)
                    dve.wait_ge(rope_ready, rope_layers(kind))
                    for t in range(NT):
                        ins = nc.vector.tensor_tensor(by_table(rope_st[:, t, 0:heads * HD], tables), by_table(x[:, t], tables),
                                                      for_heads(rope_t[:, 0, t, tables], per_table), ALU.mult)
                    link(ins)
                    dve.wait_ge(rot_ready, k.norms)
                    for t in range(NT):
                        c, r = rope_st[:, t, 0:heads * HD], e_sb[:, t, 0:heads * HD]
                        if g == "kv":
                            dst = qk_st[:, 1, t, 256:512].rearrange("p (h o d) -> p h o d", h=2, o=2)
                            c, r = (for_heads(y.rearrange("p (h d) -> p h d", d=HD), 2) for y in (c, r))
                        else:
                            dst = x[:, t]
                        ins = nc.vector.tensor_tensor(dst, c, r, ALU.add)
                    ins.then_inc(qk_ready, 1)
                elif step == "T":
                    if g == "kv":
                        dve.wait_ge(kvT_done, k.swa + 1)
                        nc.vector.tensor_copy(kT, A[1].rearrange("p (a n) -> p a n", a=2)).then_inc(kvT_ready, 1)
                    elif kind == "moba":
                        dve.wait_ge(qkT_done, 2 * n + 2)
                        nc.vector.tensor_copy(kT, A[1].rearrange("p (a n) -> p a n", a=2)).then_inc(kT_ready, 1)
                elif step == "S":
                    for t in range(NT):
                        dve.wait_ge(s_done, 2 * (k.sm + g) + t + 1)
                        for par in range(2):
                            nk = P * (t + 1)
                            ins = nc.vector.tensor_reduce(n_max[:, 4 * t + 2 * par:4 * t + 2 * par + 2],
                                                          A[2 - 2 * t + par][:, 0:2 * nk].rearrange("p (i n) -> p i n", i=2),
                                                          AX.X, ALU.max, negate=True)
                    if kind == "swa":
                        link(ins)
                        by_head = sinks[:, 4 * g:4 * g + 4].rearrange("p (i r) -> p r i", i=2)
                        for t in range(NT):
                            m = n_max[:, 4 * t:4 * t + 4].rearrange("p (r i) -> p r i", r=2)
                            ins = nc.vector.scalar_tensor_tensor(out=m, in0=by_head, scalar=-1.0, in1=m, op0=ALU.mult, op1=ALU.min)
                        link(ins)
                        for t in range(NT):
                            m = n_max[:, 4 * t:4 * t + 4].rearrange("p (r i) -> p r i", r=2)
                            ins = nc.vector.tensor_tensor(sink_e[:, 4 * t:4 * t + 4].rearrange("p (r i) -> p r i", r=2), by_head, m, ALU.add)
                        ins.then_inc(sink_ready, 1)
                        dve.wait_ge(sink_ready, 4 * k.swa + g + 1)
                        dve.sem_inc(max_ready, 1)
                    else:
                        ins.then_inc(max_ready, 1)
                elif step == "C":
                    dve.wait_ge(p_ready, 3 * (k.sm + g) + 3)
                    if kind == "swa":
                        dve.wait_ge(se_ready, 4 * k.swa + g + 1)
                        link(nc.vector.tensor_tensor(p_inv, p_sum, sink_e, ALU.add))
                        link(nc.vector.reciprocal(p_inv, p_inv))
                    else:
                        link(nc.vector.reciprocal(p_inv, p_sum))
                    for b in (2, 0, 1):
                        if b == 2:
                            p, r = z_sb[:, 2].rearrange("p (c n) -> p c n", c=4), p_inv[:, 0:4]
                        else:
                            p, r = z_sb[:, b].rearrange("p (c n) -> p c n", c=2), p_inv[:, 4 + 2 * b:6 + 2 * b]
                        nc.vector.tensor_tensor(p, p, over_elems(r, p.shape[-1]), ALU.mult).then_inc(pn_ready, 1)
                elif step == "V":
                    split(act_lo[:, 2 * g:2 * g + 2], act_hi[:, 2 * g:2 * g + 2])

            dve.wait_ge(const_in, 32)
            nc.vector.tensor_copy(ident_b, ident).then_inc(cast_ready, 1)
            nc.vector.tensor_copy(masks_b, consts[:, 3:6]).then_inc(cast_ready, 1)
            dve.wait_ge(c_ready, 1)
            modulation_units()
            convert()
            for l in range(DEPTH):
                kind, _, _ = mixer(l)
                c_gain = 16 * l

                def gains1():
                    dve.wait_ge(mod_out, mods(l, "c0"))
                    gains(l, 0, 8, c_gain).then_inc(gsc_ready, 1)

                def gains2():
                    dve.wait_ge(mod_out, mods(l, "c2"))
                    gains(l, 8, 24, c_gain + 8).then_inc(gsc_ready, 1)

                norm(late=gains1, between=convert)
                panels = qkv_panels(kind)
                u0 = k.u - 2
                nq = 2 * len(panels)
                for n in range(nq + 4):
                    if n % 2 == 0 and 0 < n <= nq:
                        k.panel("act")
                    if n:
                        convert()
                    if n == nq + 3:
                        residual(u0 + nq + 3, 0, 0, l)
                        residual(u0 + nq + 4, 1, 0, l)
                    else:
                        modulation_units()
                    for step, g in SLOTS[kind].get(n, []):
                        (step_sb(step, g) if kind == "sb" else step_softmax(step, g, kind))
                k.end_mixer(kind)
                norm(late=gains2, between=convert)

                def act_mul(p):
                    dve.wait_ge(silu_ready, (FF // 256) * l + p + 1)
                    pn = k.panel("dve")
                    if p >= 1:
                        dve.wait_ge(actT_done, (FF // 256) * l + p)
                    for t in range(NT):
                        ins = nc.vector.tensor_tensor(act_st[:, t], G[2 * (pn % 2) + t][:, 256:512], silu_st[:, t], ALU.mult)
                    ins.then_inc(act_ready, 1)
                    dve.wait_ge(act_ready, (FF // 256) * l + p + 1)
                    dve.sem_inc(free_dve, 1)

                for p in range(FF // 256):
                    convert()
                    if p >= 1:
                        act_mul(p - 1)
                        convert()
                        split(act_lo[:, 2 * p - 2:2 * p], act_hi[:, 2 * p - 2:2 * p])
                    modulation_units()
                p = FF // 256
                ud = k.u - 1
                for j in range(12):
                    if j < 11:
                        convert()
                        if j == 0:
                            act_mul(p - 1)
                            convert()
                            split(act_lo[:, 2 * p - 2:2 * p], act_hi[:, 2 * p - 2:2 * p])
                        modulation_units()
                    else:
                        residual(ud + 12, 1, 1, l)
                    if j == 7:
                        residual(ud + 6, 0, 1, l)

            def gains_lat():
                dve.wait_ge(mod_out, mods(LAT, "c0"))
                gains(LAT, 16, 40, 88)
                gains(LAT, 0, 8, 88).then_inc(gsc_ready, 1)

            def gains_ctx():
                dve.sem_inc(gsc_ready, 1)

            norm(late=gains_lat, between=convert)
            norm(ctx_raw, act_lo, act_hi, late=gains_ctx)
            u0 = k.u - 2
            for pi, (what, _, n, both) in enumerate(LAT_PANELS):
                convert()
                convert()
                for _ in range(2 if both else 1):
                    k.panel("act")
                for step in LAT_STEPS.get(pi, []):
                    k.norms += 1
                    x, nh = lat_heads(step)
                    dve.wait_ge(sq_ready, k.norms)
                    link(nc.vector.tensor_reduce(ss16[:, 0:NT * nh].rearrange("p (t h) -> p t h", t=NT),
                                                 lrot[:, :, 0:nh * HD].rearrange("p t (h d) -> p t h d", d=HD), AX.X, ALU.add))
                    rsqrt(ss16[:, 0:NT * nh], NT * nh, HD)
                    for t in range(NT):
                        ins = nc.vector.tensor_tensor(heads(x[:, t]), heads(x[:, t]), over_elems(rms_y[:, t * nh:(t + 1) * nh]), ALU.mult)
                    ins.then_inc(xn_ready, 1)
                    dve.wait_ge(xn_ready, k.norms)
                    dve.wait_ge(rope2_ready, 1)

                    def twice(y):
                        return y.rearrange("p (h o d) -> p h o d", h=2, o=1).broadcast_to([P, 2, 2, HD])

                    def kdst(t):
                        return kdup[:, t].rearrange("p (h o d) -> p h o d", h=2, o=2)
                    if step == "kc":
                        gain = rope_g[:, 1].rearrange("p (a b d) -> p a b d", a=1, b=1).broadcast_to([P, 2, 2, HD])
                        for t in range(NT):
                            ins = nc.vector.tensor_tensor(kdst(2 + t), twice(x[:, t]), gain, ALU.mult)
                    else:
                        q = 0 if step == "q" else 1
                        for t in range(NT):
                            ins = nc.vector.tensor_tensor(heads(lrope_st[:, t, 0:nh * HD]), heads(x[:, t]), over_heads(rope_t[:, 0, t, q], nh), ALU.mult)
                        link(ins)
                        dve.wait_ge(rot_ready, k.norms - (1 if step == "q" else 0))
                        for t in range(NT):
                            c, r = lrope_st[:, t, 0:nh * HD], lrot[:, t, 0:nh * HD]
                            if step == "q":
                                ins = nc.vector.tensor_tensor(x[:, t], c, r, ALU.add)
                            else:
                                ins = nc.vector.tensor_tensor(kdst(t), twice(c), twice(r), ALU.add)
                    ins.then_inc(qk_ready, 1)
            dve.wait_ge(ltT_done, 2)
            nc.vector.tensor_copy(lkT[:, 1], A[1]).then_inc(kq_dve, 1)
            dve.wait_ge(ltT_done, 4)
            nc.vector.tensor_copy(lqT[:, 2:4].rearrange("p a n -> p (a n)"), A[3]).then_inc(kq_dve, 1)
            for s in range(4):
                for b in range(4):
                    dve.wait_ge(ws_done, 4 * s + b + 1)
                    ins = nc.vector.tensor_reduce(n_max[:, b:b + 1], A[b], AX.X, ALU.max, negate=True)
                link(ins)
                sink = sinks[:, 2 * s:2 * s + 2].rearrange("p (o r) -> p o r", o=1).broadcast_to([P, 2, 2])
                mx = n_max[:, 0:4].rearrange("p (t r) -> p t r", t=2)
                link(nc.vector.scalar_tensor_tensor(out=mx, in0=sink, scalar=-1.0, in1=mx, op0=ALU.mult, op1=ALU.min))
                nc.vector.tensor_tensor(sink_e[:, 0:4].rearrange("p (t r) -> p t r", t=2), sink, mx, ALU.add).then_inc(wmax_ready, 1)
                dve.wait_ge(wp_ready, s + 1)
                dve.wait_ge(wse_ready, s + 1)
                link(nc.vector.tensor_tensor(p_inv[:, 0:4], p_sum[:, 0:4], sink_e[:, 0:4], ALU.add))
                link(nc.vector.reciprocal(p_inv[:, 0:4], p_inv[:, 0:4]))
                for b in range(4):
                    ins = nc.vector.tensor_scalar(p_sb[:, b], p_sb[:, b], p_inv[:, b:b + 1], None, ALU.mult)
                ins.then_inc(wn_ready, 1)
                for b in (1, 3):
                    dve.wait_ge(wpT_done, 4 * s + b + 1)
                    nc.vector.tensor_copy(laT[:, b], A[b]).then_inc(waT_dve, 1)
                if s % 2:
                    split(act_lo[:, s - 1:s + 1], act_hi[:, s - 1:s + 1])
            dve.wait_ge(cw_in, 16)
            for a, (x, wi) in enumerate(CONV):
                dve.wait_ge(shift_in, 96 * (a + 1))
                for y, tap in ((prev, 0), (x, 1), (nxt, 2)):
                    row = conv_rows[:, tap, 512 * wi:512 * wi + 512]
                    ins = nc.vector.tensor_tensor(y, y, over_heads(row, NT), ALU.mult)
                link(ins)
                link(nc.vector.tensor_tensor(x, x, prev, ALU.add))
                nc.vector.tensor_tensor(x, x, nxt, ALU.add).then_inc(conv_ready, 1)
            for a, x in enumerate((dk_c, dk_x, dq_x)):
                k.norms += 1
                dve.wait_ge(sq_ready, k.norms)
                link(nc.vector.tensor_reduce(ss16.rearrange("p (t h) -> p t h", t=NT), sq_t.rearrange("p t (h d) -> p t h d", d=HD), AX.X, ALU.add))
                rsqrt(ss16, 16, 1.0 / HD if a == 2 else 1.0, HD * EPS if a == 2 else EPS)
                for t in range(NT):
                    ins = nc.vector.tensor_tensor(heads(x[:, t]), heads(x[:, t]), over_elems(rms_y[:, 8 * t:8 * t + 8]), ALU.mult)
                ins.then_inc(l2_ready, 1)
            dve.wait_ge(free_act, k.free_act)
            dve.wait_ge(lat_in, 128)
            dtb = dtb_row.rearrange("p (o n) -> p o n", o=1).broadcast_to([P, 4, 16])
            nc.vector.tensor_tensor(gate_z[:, :, 0:16], dab[:, :, 0:16], dtb, ALU.add)
            link(nc.vector.tensor_scalar(gate_z[:, :, 16:32], dab[:, :, 16:32], -1.0, None, ALU.mult))
            nc.vector.scalar_tensor_tensor(out=gate_s, in0=gate_z, scalar=-1.0, in1=gate_z, op0=ALU.mult, op1=ALU.min).then_inc(gz_ready, 1)
            dve.wait_ge(gl_ready, 1)
            dve.wait_ge(ea_ready, 1)
            link(nc.vector.scalar_tensor_tensor(out=gate_s, in0=gate_z, scalar=0.0, in1=gate_s, op0=ALU.max, op1=ALU.add))
            ea = alog_row.rearrange("p (o n) -> p o n", o=1).broadcast_to([P, 4, 16])
            nc.vector.scalar_tensor_tensor(out=g_all, in0=gate_s[:, :, 0:16], scalar=-1.0, in1=ea, op0=ALU.mult, op1=ALU.mult)
            nc.vector.tensor_scalar(lnb_all, gate_s[:, :, 16:32], -1.0, None, ALU.mult).then_inc(gates_ready, 1)
            dve.wait_ge(eg_ready, 1)
            dve.wait_ge(beta_ready, 1)
            for d in range(2):
                ins = nc.vector.tensor_tensor(beG[:, d], beta[:, :, d], e_G[:, d], ALU.mult)
            ins.then_inc(beg_ready, 1)
            for i, dst in enumerate((kT_c, kT_x, qT_x)):
                dve.wait_ge(dT_done, 2 * i + 2)
                nc.vector.tensor_copy(dst[:, 2:4].rearrange("p a n -> p (a n)"), (A[3], G[1], G[3])[i]).then_inc(dT_dve, 1)

            def four(m):
                return m.rearrange("p (o n) -> p o n", o=1).broadcast_to([P, 4, P])

            def by4(x):
                return x.rearrange("p (i n) -> p i n", i=4)

            for rd in range(4):
                lat = rd >= 2
                for d in range(2):
                    bd = 2 * rd + d
                    for r in range(2):
                        dve.wait_ge(E_ready, 2 * bd + r + 1)
                        dve.wait_ge(kk_done, 2 * bd + r + 1)
                        nc.vector.tensor_tensor(LT[:, r], LT[:, r], A[2 + r], ALU.mult).then_inc(LT_ready, 1)
                        dve.wait_ge(LT_ready, 2 * bd + r + 1)
                        link(nc.vector.tensor_tensor(by4(XT[:, r]), by4(LT[:, r]), four(level_mask[:, 1 - d, 0]), ALU.mult))
                        nc.vector.tensor_tensor(by4(XT[:, r]), four(ident), by4(XT[:, r]), ALU.subtract)
                    for lev in range(LEVELS):
                        for r in range(2):
                            dve.wait_ge(y_done, 2 * (LEVELS * bd + lev) + r + 1)
                            ins = nc.vector.tensor_tensor(by4(Y[:, r]), by4(A[r]), four(level_mask[:, d, lev]), ALU.mult)
                            if lev:
                                ins.then_inc(Y_ready, 1)
                            else:
                                link(ins)
                                nc.vector.tensor_tensor(by4(X[:, r]), four(ident), by4(Y[:, r]), ALU.subtract).then_inc(X_ready, 1)
                        for r in range(2):
                            if lev:
                                dve.wait_ge(xy_done, 2 * ((LEVELS - 1) * bd + lev - 1) + r + 1)
                                if lev < LEVELS - 1:
                                    nc.vector.tensor_tensor(X[:, r], X[:, r], A[2 + r], ALU.subtract)
                                nc.vector.tensor_tensor(XT[:, r], XT[:, r], G[r], ALU.subtract).then_inc(X_ready, 1)
                    if lat:
                        for r in range(2):
                            dve.wait_ge(ie_ready, 2 * (bd - 4) + r + 1)
                            nc.vector.tensor_tensor(intraT[:, d, r], intraT[:, d, r], A[2 + r], ALU.mult).then_inc(intra_ready, 1)
                for step in range(2):
                    c = 2 * rd + step
                    if c:
                        dve.wait_ge(S_ready, c)
                    else:
                        dve.wait_ge(state_zero, 1)
                    if c < 7:
                        for r in range(2):
                            decay = over_elems(e_last[:, c].rearrange("p (i r) -> p r i", r=2)[:, r])
                            ins = nc.vector.tensor_tensor(heads(state_t[:, 256 * r:256 * r + 256]), heads(state[:, 256 * r:256 * r + 256]), decay, ALU.mult)
                    dve.wait_ge(wS_done, c + 1)
                    dve.wait_ge(uv_ready, 4 * rd + 4)
                    nc.vector.tensor_tensor(u_st[:, step], u_st[:, step], A[0], ALU.subtract).then_inc(u_ready, 1)
                    if c < 7:
                        dve.wait_ge(u_ready, c + 1)
                        dve.wait_ge(su_done, c + 1)
                        nc.vector.tensor_tensor(state, state_t, A[3], ALU.add).then_inc(S_ready, 1)
                if lat:
                    dve.wait_ge(o_done, rd - 1)
                    for d in range(2):
                        t, _ = delta_tile(rd, d)
                        if rd == 2:
                            link(nc.vector.tensor_copy(o_dn[:, t], A[1 + d]))
                        else:
                            link(nc.vector.tensor_tensor(o_dn[:, t], o_dn[:, t], A[1 + d], ALU.add))
                        ins = nc.vector.tensor_tensor(o_dn[:, t], o_dn[:, t], G[d], ALU.add)
                    ins.then_inc(oacc_ready, 1)
            k.norms += 1
            dve.wait_ge(sq_ready, k.norms)
            link(nc.vector.tensor_reduce(ss16.rearrange("p (t h) -> p t h", t=NT), sq_t.rearrange("p t (h d) -> p t h d", d=HD), AX.X, ALU.add))
            rsqrt(ss16, 16, HD)
            for t in range(NT):
                ins = nc.vector.tensor_tensor(heads(o_dn[:, t]), heads(o_dn[:, t]), over_elems(rms_y[:, 8 * t:8 * t + 8]), ALU.mult)
            link(ins)
            for t in range(NT):
                ins = nc.vector.tensor_tensor(heads(o_dn[:, t]), heads(o_dn[:, t]), over_heads(dng_row, DNH), ALU.mult)
            link(ins)
            for t in range(NT):
                gate = dz[:, t].rearrange("p (i r d) -> p r i d", r=2, d=HD)
                ins = nc.vector.tensor_tensor(gate, gate, o_dn[:, t].rearrange("p (r i d) -> p r i d", r=2, d=HD), ALU.mult)
            ins.then_inc(yd_ready, 1)
            for q in range(2):
                split(act_lo[:, 4 + 2 * q:6 + 2 * q], act_hi[:, 4 + 2 * q:6 + 2 * q])
            um = k.u - 2
            for n in range(4):
                convert()
                convert()
                k.panel("act")
            for n in range(4):
                convert()
                dve.wait_ge(gemm_done, um + 9 + n)
                pn = k.panel("dve")
                sl = slice(512 * (n % 2), 512 * (n % 2) + 512)
                dve.wait_ge(free_act, k.free_act)
                for t in range(NT):
                    ins = nc.vector.tensor_tensor(sig[:, n // 2, t, sl], sig[:, n // 2, t, sl], G[2 * (pn % 2) + t], ALU.mult)
                ins.then_inc(free_dve, 1)
                if n >= 2:
                    dve.wait_ge(free_dve, k.free_dve)
                    nc.vector.tensor_tensor(n_st[:, :, sl], sig[:, 0, :, sl], sig[:, 1, :, sl], ALU.add).then_inc(yy_ready, 1)
            for q in range(4):
                split(h_lo[:, 2 * q:2 * q + 2], h_hi[:, 2 * q:2 * q + 2])
            convert()
            convert()
            residual(um + 15, 0, 0, LAT)
            convert()
            residual(um + 16, 1, 0, LAT)

            def gains_lat2():
                dve.wait_ge(mod_out, mods(LAT, "c2"))
                gains(LAT, 8, 24, 96).then_inc(gsc_ready, 1)

            norm(late=gains_lat2, between=convert)
            um = k.u - 2

            def hidden(p):
                dve.wait_ge(relu_ready, p + 1)
                pn = k.panel("dve")
                if p >= 1:
                    dve.wait_ge(hidT_done, 2 * p)
                for t in range(NT):
                    ins = nc.vector.tensor_tensor(hid_st[:, t], G[2 * (pn % 2) + t], relu_st[:, t], ALU.mult)
                ins.then_inc(hid_ready, 1)
                dve.wait_ge(hid_ready, p + 1)
                dve.sem_inc(free_dve, 1)

            def split_hidden(p):
                for q in range(2):
                    kt = 4 * (p % 4) + 2 * q
                    split(act_lo[:, kt:kt + 2], act_hi[:, kt:kt + 2])

            for part in range(2):
                for p in range(4):
                    hp = 4 * part + p
                    if p >= 1:
                        hidden(hp - 1)
                    convert()
                    if p >= 1:
                        split_hidden(hp - 1)
                    convert()
                for j in range(8):
                    if j == 0:
                        hidden(4 * part + 3)
                    convert()
                    if j == 0:
                        split_hidden(4 * part + 3)
                    if j == 5:
                        residual(um + 16 * part + 12, 0, 1, LAT)
                residual(um + 16 * part + 16, 1, 1, LAT)

        @block.tensor
        def _(pe):
            k = Walk()

            def wait_panel_free(pn):
                if pn >= 2:
                    who, count = k.panel_free[pn - 2]
                    pe.wait_ge(free_act if who == "act" else free_dve, count)

            def unit(x_hi, x_lo, kts, banks, first, last, n=512, done=gemm_done):
                u = k.u
                k.u += 1
                pe.wait_ge(hi_ready, u + 1)
                pe.wait_ge(lo_ready, u + 1)
                for t in range(NT):
                    ts = slice(t * P, t * P + P)
                    for i, kt in enumerate(kts):
                        st = first and i == 0
                        en = last and i == len(kts) - 1
                        nc.tensor.matmul(banks[t][:, 0:n], x_hi[:, kt, ts], w_hi[:, u % 2, i, 0:n], start=st, stop=False)
                        nc.tensor.matmul(banks[t][:, 0:n], x_hi[:, kt, ts], w_lo[:, u % 2, i, 0:n], start=False, stop=False)
                        ins = nc.tensor.matmul(banks[t][:, 0:n], x_lo[:, kt, ts], w_hi[:, u % 2, i, 0:n], start=False, stop=en)
                if done is not None:
                    ins.then_inc(done, 1)

            def norm_transposes():
                m = k.m
                k.m += 1
                for t in range(NT):
                    pe.wait_ge(n_ready, 2 * m + t + 1)
                if k.sums:
                    pe.wait_ge(mod_out, k.sums)
                if k.f:
                    pe.wait_ge(split_full, k.f)
                for q in range(KT // 2):
                    for i in range(2):
                        for t in range(NT):
                            ins = nc.tensor.transpose(A[q][:, i * SEQ + t * P:i * SEQ + t * P + P],
                                                      n_st[:, t, (2 * q + i) * P:(2 * q + i + 1) * P], ident)
                    ins.then_inc(norm_T, 1)
                k.f += KT // 2

            def modulation(l, piece):
                j = int(piece[1])
                pe.wait_ge(acc_done, ADA_U * l + KT * (j + 1))
                if k.sums:
                    pe.wait_ge(mod_out, k.sums)
                if k.f:
                    pe.wait_ge(split_full, k.f)
                else:
                    pe.wait_ge(cols_ready, 1)
                src, banks = acc[:, (3 * l + j) % 2], SUM_BANKS[l, piece]
                if piece[0] == "r":
                    for i in range(2):
                        o = (0, D)[j - 1] + 512 * i
                        nc.tensor.matmul(banks[i], ones, src[:, o:o + 512], start=True, stop=True).then_inc(sums_done, 1)
                        k.sums += 1
                    return
                blocks = [(c, src, c) for c in range(2 * KT)] if j == 0 else [(c, src, c + (KT if j == 1 else 0)) for c in range(KT)]
                if l == LAT and j == 0:
                    pe.wait_ge(accc_done, KT)
                    blocks += [(2 * KT + c, acc_c, c) for c in range(2 * KT)]
                for dst, x, c in blocks:
                    ins = nc.tensor.matmul(banks[0][:, dst:dst + 1], x[:, c * P:c * P + P], ones[:, 0:1], start=True, stop=True)
                ins.then_inc(sums_done, 1)
                k.sums += 1

            def step_sb(step, g, evac):
                n = k.group + g
                ns = k.sb + g
                if step == "T":
                    pe.wait_ge(free_act, evac)
                    if ns:
                        pe.wait_ge(d_ready, 3 * ns)
                    for what in range(2):
                        for a in range(2):
                            for t in range(NT):
                                ins = nc.tensor.transpose(A[what][:, a * SEQ + t * P:a * SEQ + t * P + P],
                                                          qk_st[:, g % 2, t, 256 * what + a * P:256 * what + a * P + P], ident)
                        ins.then_inc(qkT_done, 1)
                elif step == "S":
                    pe.wait_ge(qT_ready, n + 1)
                    pe.wait_ge(kT_ready, k.kt + g + 1)
                    pe.wait_ge(cast_ready, 2)
                    if k.f:
                        pe.wait_ge(split_full, k.f)
                    for h in range(GROUP):
                        r = slice(HD * (h % 2), HD * (h % 2) + HD)
                        o = A[2 + h % 2][:, h // 2 * P:h // 2 * P + P]
                        nc.tensor.matmul(o, kT[r, h // 2, P:2 * P], qT[r, h // 2, P:2 * P], start=True, stop=False)
                        ins = nc.tensor.matmul(o, ident_b, m_sb, start=False, stop=True)
                    ins.then_inc(z_done, 1)
                    for h in range(GROUP):
                        r = slice(HD * (h % 2), HD * (h % 2) + HD)
                        o = A[h % 2][:, (h // 2) * SEQ:(h // 2) * SEQ + SEQ]
                        nc.tensor.matmul(o, kT[r, h // 2, 0:P], qT[r, h // 2, :], start=True, stop=False)
                        ins = nc.tensor.matmul(o[:, 0:P], ident_b, m_sb, start=False, stop=True)
                        if h >= 2:
                            ins.then_inc(z_done, 1)
                elif step == "C":
                    pe.wait_ge(sp_ready, 3 * ns + 1)
                    nc.tensor.matmul(A[2], tri, e_sb[:, 2], start=True, stop=True).then_inc(r_done, 1)
                    for b in range(2):
                        pe.wait_ge(sp_ready, 3 * ns + 2 + b)
                        nc.tensor.matmul(A[b], tri, e_sb[:, b], start=True, stop=False)
                        nc.tensor.matmul(A[b].rearrange("p (h n) -> p h n", h=2)[:, :, P:SEQ], ones,
                                         e_sb[:, 2, 256 * b:256 * b + 256].rearrange("p (h n) -> p h n", h=2),
                                         start=False, stop=True).then_inc(r_done, 1)
                elif step == "V":
                    weighted_values(n, g, evac, "sb")

            def weighted_values(n, g, evac, kind):
                pe.wait_ge(aT_ready, 3 * n + 3)
                pe.wait_ge(free_act, evac)
                v = v_st[:, 0 if kind == "swa" else g // 2]
                for i in range(2):
                    for par in range(2):
                        c = HD * (g // 2) if kind == "swa" else 256 * (g % 2) + HD * (2 * i + par)
                        o = A[3][HD * par:HD * par + HD, SEQ * i:SEQ * i + SEQ]
                        nc.tensor.matmul(o, v[:, 0, c:c + HD], aT[:, par, i * SEQ:i * SEQ + SEQ], start=True, stop=False)
                        ins = nc.tensor.matmul(o[:, P:SEQ], v[:, 1, c:c + HD], aT[:, 2, SEQ * par + P * i:SEQ * par + P * i + P], start=False, stop=True)
                ins.then_inc(av_done, 1)
                k.f += 1

            def step_softmax(step, g, kind, evac):
                if step == "N":
                    k.norms += 1
                    k.normed[g] = k.norms
                    return
                if g == "kv":
                    pe.wait_ge(qk_ready, k.normed["kv"])
                    for a in range(2):
                        for t in range(NT):
                            ins = nc.tensor.transpose(A[1][:, a * SEQ + t * P:a * SEQ + t * P + P],
                                                      qk_st[:, 1, t, 256 + a * P:256 + a * P + P], ident)
                    ins.then_inc(kvT_done, 1)
                    return
                n = k.group + g
                if step == "T":
                    if n:
                        pe.wait_ge(aT_ready, 3 * n)
                    pe.wait_ge(qk_ready, k.normed[2 * (g // 2) if kind == "swa" else g])
                    b, c = staged(kind, g)
                    for what in range(1 if kind == "swa" else 2):
                        for a in range(2):
                            for t in range(NT):
                                ins = nc.tensor.transpose(A[what][:, a * SEQ + t * P:a * SEQ + t * P + P],
                                                          qk_st[:, b, t, c + 256 * what + a * P:c + 256 * what + a * P + P], ident)
                        ins.then_inc(qkT_done, 2 if kind == "swa" else 1)
                elif step == "S":
                    pe.wait_ge(qT_ready, n + 1)
                    if kind == "swa":
                        pe.wait_ge(kvT_ready, k.swa + 1)
                    else:
                        pe.wait_ge(kT_ready, k.kt + g + 1)
                    if k.f:
                        pe.wait_ge(split_full, k.f)
                    for t in range(NT):
                        nk = P * (t + 1)
                        for h in range(GROUP):
                            r = slice(HD * (h % 2), HD * (h % 2) + HD)
                            o = A[2 - 2 * t + h % 2][:, h // 2 * nk:(h // 2 + 1) * nk]
                            nc.tensor.matmul(o, qT[r, h // 2, t * P:t * P + P], kT[r, g // 2 if kind == "swa" else h // 2, 0:nk],
                                             start=True, stop=False)
                            if t and kind == "swa":
                                ins = nc.tensor.matmul(o, ident_b, m_window.rearrange("p c n -> p (c n)"), start=False, stop=True)
                            else:
                                ins = nc.tensor.matmul(o[:, t * P:t * P + P], ident_b, m_causal, start=False, stop=True)
                        ins.then_inc(s_done, 1)
                elif step == "C":
                    pe.wait_ge(pn_ready, 3 * (k.sm + g) + 3)
                    for h in range(GROUP):
                        par, i = h % 2, h // 2
                        ins = nc.tensor.transpose(A[2][:, SEQ * par + P * i:SEQ * par + P * i + P], z_sb[:, par, SEQ * i + P:SEQ * i + SEQ], ident)
                    ins.then_inc(pT_done, 1)
                    for par in range(2):
                        for i in range(2):
                            nc.tensor.transpose(A[par][:, SEQ * i:SEQ * i + P], z_sb[:, 2, SEQ * par + P * i:SEQ * par + P * i + P], ident)
                            ins = nc.tensor.transpose(A[par][:, SEQ * i + P:SEQ * i + SEQ], z_sb[:, par, SEQ * i:SEQ * i + P], ident)
                        ins.then_inc(pT_done, 1)
                elif step == "V":
                    weighted_values(n, g, evac, kind)

            def attend(kind, step, g, evac):
                if kind == "sb":
                    step_sb(step, g, evac["v", g // 2] if step == "V" else evac["qk", g])
                else:
                    step_softmax(step, g, kind, evac["kv", 0] if kind == "swa" else evac.get(("v", (0 if g == "kv" else g // 2))))

            pe.wait_ge(const_in, 32)
            nc.tensor.transpose(A[0][:, 0:NCOL], cols_in, ident[0:NCOL, 0:NCOL]).then_inc(cols_T, 1)
            modulation(0, "c0")
            for l in range(DEPTH):
                kind, _, _ = mixer(l)
                norm_transposes()
                f_h = k.f
                panels = qkv_panels(kind)
                evac = {}
                pns = []
                f_o = {}
                for n in range(2 * len(panels)):
                    pi, h = n // 2, n % 2
                    what, g, _ = panels[pi]
                    if h == 0:
                        pns.append(k.panel("act"))
                        evac[what, g] = k.free_act
                        wait_panel_free(pns[-1])
                    pe.wait_ge(split_lo, f_h - 2 + 2 * h)
                    unit(h_hi, h_lo, range(4 * h, 4 * h + 4), G[2 * (pns[-1] % 2):2 * (pns[-1] % 2) + 2], h == 0, h == 1,
                         width(panels[pi]))
                    for step, g in SLOTS[kind].get(n, []):
                        attend(kind, step, g, evac)
                        if step == "V":
                            f_o[g] = k.f
                po = [k.panel("dve"), k.panel("dve")]
                n = 2 * len(panels)
                for h in range(2):
                    pe.wait_ge(split_lo, f_o[2 * h + 1])
                    for j in range(2):
                        if h == 0:
                            wait_panel_free(po[j])
                        unit(act_hi, act_lo, range(4 * h, 4 * h + 4), G[2 * (po[j] % 2):2 * (po[j] % 2) + 2], h == 0, h == 1)
                        for step, g in SLOTS[kind].get(n, []):
                            attend(kind, step, g, evac)
                            if step == "V":
                                f_o[g] = k.f
                        if l == 0 and n == 2 * len(panels) + 1:
                            modulation(0, "r1")
                            modulation(0, "c1")
                        n += 1
                k.end_mixer(kind)
                if l == 0:
                    modulation(0, "c2")
                    modulation(0, "r2")
                norm_transposes()
                f_h = k.f

                def act_transposes(p):
                    pe.wait_ge(act_ready, (FF // 256) * l + p + 1)
                    pe.wait_ge(split_full, k.f - 1)
                    for a in range(2):
                        for t in range(NT):
                            ins = nc.tensor.transpose(A[p % 2][:, a * SEQ + t * P:a * SEQ + t * P + P], act_st[:, t, a * P:a * P + P], ident)
                    ins.then_inc(actT_done, 1)
                    k.f += 1

                for p in range(FF // 256):
                    pn = k.panel("dve")
                    wait_panel_free(pn)
                    for h in range(2):
                        pe.wait_ge(split_lo, f_h - 2 + 2 * h)
                        unit(h_hi, h_lo, range(4 * h, 4 * h + 4), G[2 * (pn % 2):2 * (pn % 2) + 2], h == 0, h == 1)
                        if h == 0 and p >= 1:
                            act_transposes(p - 1)
                    if (l, ("up", p)) in SUMS and p < FF // 256 - 1:
                        modulation(l + 1, SUMS[l, ("up", p)])
                f_a = k.f + 1
                for j in range(2):
                    pn = k.panel("dve")
                    wait_panel_free(pn)
                    for h in range(6):
                        kts = range(4 * h, min(4 * h + 4, FFT))
                        pe.wait_ge(split_lo, f_a - FF // 256 + (kts[-1] // 2 + 1))
                        unit(act_hi, act_lo, kts, G[2 * (pn % 2):2 * (pn % 2) + 2], h == 0, h == 5)
                        if j == 0 and h == 0:
                            act_transposes(FF // 256 - 1)
                            if (l, ("up", FF // 256 - 1)) in SUMS:
                                modulation(l + 1, SUMS[l, ("up", FF // 256 - 1)])
                        if (l, ("down", 6 * j + h)) in SUMS:
                            modulation(l + 1, SUMS[l, ("down", 6 * j + h)])
                modulation(l + 1, "c2")
                modulation(l + 1, "r2")

            norm_transposes()
            norm_transposes()
            f_h = k.f
            for pi, (what, _, n, both) in enumerate(LAT_PANELS):
                banks = []
                for _ in range(2 if both else 1):
                    pn = k.panel("act")
                    wait_panel_free(pn)
                    banks.append(G[2 * (pn % 2):2 * (pn % 2) + 2])
                for h in range(2):
                    pe.wait_ge(split_lo, f_h - 2 + 2 * h if both else f_h)
                    kts = range(4 * h, 4 * h + 4)
                    unit(h_hi, h_lo, kts, banks[0], h == 0, h == 1, n, None if both else gemm_done)
                    if both:
                        k.u -= 1
                        unit(act_hi, act_lo, kts, banks[1], h == 0, h == 1, n)
                for step in LAT_STEPS.get(pi, []):
                    k.norms += 1
            pe.wait_ge(split_full, k.f)
            pe.wait_ge(qk_ready, k.norms)
            for g in range(2):
                for t in range(4):
                    ins = nc.tensor.transpose(A[g][:, t * P:t * P + P], kdup[:, t, g * P:g * P + P], ident)
                ins.then_inc(ltT_done, 1)
            for b in range(2):
                for i in range(2):
                    for t in range(NT):
                        ins = nc.tensor.transpose(A[2 + b][:, i * SEQ + t * P:i * SEQ + t * P + P], aq[:, t, (2 * b + i) * P:(2 * b + i + 1) * P], ident)
                ins.then_inc(ltT_done, 1)
            pe.wait_ge(kq_act, 2)
            pe.wait_ge(kq_dve, 2)
            pe.wait_ge(masks_ready, 1)
            for s in range(4):
                for t in range(NT):
                    for r in range(2):
                        hr = slice(HD * r, HD * r + HD)
                        b = 2 * t + r
                        nc.tensor.matmul(A[b], lqT[hr, s, t * P:t * P + P], lkT[hr, s // 2], start=True, stop=False)
                        nc.tensor.matmul(A[b][:, (1 - t) * P:(2 - t) * P], ident_b, m_from if t else m_causal, start=False, stop=True).then_inc(ws_done, 1)
                pe.wait_ge(wn_ready, s + 1)
                for kt in range(4):
                    for b in range(4):
                        ins = nc.tensor.transpose(A[kt][:, b * P:b * P + P], p_sb[:, b, kt * P:kt * P + P], ident)
                    ins.then_inc(wpT_done, 1)
                pe.wait_ge(waT_act, 2 * s + 2)
                pe.wait_ge(waT_dve, 2 * s + 2)
                pe.wait_ge(free_act, k.free_act)
                for r in range(2):
                    for kt in range(4):
                        v = (kva_x, kva_c)[kt // 2][:, kt % 2, P + HD * (s // 2):P + HD * (s // 2) + HD]
                        p = laT[:, kt].rearrange("p (t r n) -> p r t n", t=NT, r=2)[:, r]
                        ins = nc.tensor.matmul(G[s][HD * r:HD * r + HD, 0:SEQ].rearrange("p (t n) -> p t n", t=NT), v, p,
                                               start=kt == 0, stop=kt == 3)
                ins.then_inc(woT_done, 1)
            k.f += 2
            pe.wait_ge(gates_ready, 1)
            pe.wait_ge(lat_in, 128)
            for d in range(2):
                for i, m_ in enumerate((tri_dir, later_dir)):
                    nc.tensor.matmul(A[0][:, 64 * i + 32 * d:64 * i + 32 * d + 32].rearrange("p (s h) -> p s h", s=4), m_[:, d], g_all[:, :, 8 * d:8 * d + 8],
                                     start=True, stop=True)
                for rd in range(4):
                    for step in range(2):
                        c = 2 * rd + step
                        _, st = delta_tile(rd, d)
                        ins = nc.tensor.matmul(A[1][CH * d:CH * d + CH, 8 * c:8 * c + 8], half[:, step if d == 0 else 1 - step], g_all[:, st, 8 * d:8 * d + 8],
                                               start=True, stop=True)
            ins.then_inc(gsum_done, 1)
            pe.wait_ge(split_full, k.f)
            for i, x in enumerate((dk_c, dk_x, dq_x)):
                pe.wait_ge(l2_ready, i + 1)
                for b in range(2):
                    for a in range(2):
                        for t in range(NT):
                            ins = nc.tensor.transpose((A[2:4], G[0:2], G[2:4])[i][b][:, a * SEQ + t * P:a * SEQ + t * P + P],
                                                      x[:, t, (2 * b + a) * P:(2 * b + a + 1) * P], ident)
                    ins.then_inc(dT_done, 1)
            pe.wait_ge(dT_act, 3)
            pe.wait_ge(dT_dve, 3)
            pe.wait_ge(eg_ready, 1)

            def decay(bank, d, st, r, mask, with_beta):
                for i in range(4):
                    h = 8 * d + 2 * i + r
                    o = bank[:, i * P:i * P + P]
                    nc.tensor.matmul(o, g_all[:, st, h:h + 1].broadcast_to([P, P]), tri_dir[:, d], start=True, stop=False)
                    if with_beta:
                        nc.tensor.matmul(o, lnb_all[:, st, h:h + 1].broadcast_to([P, P]), ident, start=False, stop=False)
                    ins = nc.tensor.matmul(o, ident_b, mask[:, d], start=False, stop=True)
                return ins

            def dots(bank, kT_s, other, t, r):
                for i in range(4):
                    hr = slice(HD * r, HD * r + HD)
                    ins = nc.tensor.matmul(bank[:, i * P:i * P + P], kT_s[hr, i, t * P:t * P + P], other[hr, i, t * P:t * P + P], start=True, stop=True)
                return ins

            def four(bank, lhsT, rhs):
                for i in range(4):
                    sl = slice(i * P, i * P + P)
                    ins = nc.tensor.matmul(bank[:, sl], lhsT[:, sl], rhs[:, sl], start=True, stop=True)
                return ins

            for rd in range(4):
                lat = rd >= 2
                kT_s = kT_x if lat else kT_c
                for d in range(2):
                    bd = 2 * rd + d
                    t, st = delta_tile(rd, d)
                    if bd:
                        pe.wait_ge(uv_ready, 2 * bd)
                    if bd > 4:
                        pe.wait_ge(qdT_ready, 2 * (bd - 4))
                        pe.wait_ge(intra_ready, 2 * (bd - 4))
                    if rd and d == 0:
                        pe.wait_ge(S_ready, 2 * rd)
                        if rd == 3:
                            pe.wait_ge(oacc_ready, 1)
                    for r in range(2):
                        decay(A[r], d, st, r, m_strict, True).then_inc(e_done, 1)
                        dots(A[2 + r], kT_s, kT_s, t, r).then_inc(kk_done, 1)
                    for lev in range(LEVELS):
                        for r in range(2):
                            if lev == 0:
                                pe.wait_ge(LT_ready, 2 * bd + r + 1)
                                for i in range(4):
                                    ins = nc.tensor.transpose(A[r][:, i * P:i * P + P], LT[:, r, i * P:i * P + P], ident)
                                ins.then_inc(y_done, 1)
                            else:
                                pe.wait_ge(X_ready, 2 * (LEVELS * bd + lev - 1) + r + 1)
                                four(A[r], LT[:, r], X[:, r]).then_inc(y_done, 1)
                        if lev:
                            for r in range(2):
                                pe.wait_ge(Y_ready, 2 * ((LEVELS - 1) * bd + lev - 1) + r + 1)
                                if lev < LEVELS - 1:
                                    four(A[2 + r], XT[:, r], Y[:, r])
                                four(G[r], Y[:, r], XT[:, r]).then_inc(xy_done, 1)
                    pe.wait_ge(prep_ready, bd + 1)
                    if rd and d == 0:
                        pe.wait_ge(wT_ready, rd)
                    for r in range(2):
                        pe.wait_ge(X_ready, 2 * (LEVELS * bd + LEVELS - 1) + r + 1)
                        for i in range(4):
                            h = 2 * i + r
                            ins = nc.tensor.matmul(G[2 + r][CH * d:CH * d + CH, i * P:i * P + P], bek[:, HD * h:HD * h + HD], XT[:, r, i * P:i * P + P],
                                                   start=True, stop=True)
                    ins.then_inc(wT_done, 1)
                    for r in range(2):
                        for i in range(4):
                            h = 2 * i + r
                            ins = nc.tensor.matmul(A[r][:, i * HD:i * HD + HD], XT[:, r, i * P:i * P + P], bv[:, HD * h:HD * h + HD], start=True, stop=True)
                        ins.then_inc(uv_done, 1)
                    if lat:
                        for r in range(2):
                            decay(G[r], d, st, r, m_incl, False)
                            dots(A[2 + r], kT_s, qT_x, t, r).then_inc(in_done, 1)
                        for r in range(2):
                            pe.wait_ge(uv_ready, 2 * bd + r + 1)
                            for i in range(4):
                                h = 2 * i + r
                                ins = nc.tensor.matmul(A[r][CH * d:CH * d + CH, i * P:i * P + P], q_dec[:, HD * h:HD * h + HD], ident,
                                                       start=True, stop=True)
                            ins.then_inc(qdT_done, 1)
                pe.wait_ge(wT_ready, rd + 1)
                pe.wait_ge(uv_ready, 4 * rd + 4)
                if lat:
                    pe.wait_ge(qdT_ready, 4 * (rd - 2) + 4)
                    pe.wait_ge(intra_ready, 4 * (rd - 2) + 4)
                for step in range(2):
                    c = 2 * rd + step
                    if c:
                        pe.wait_ge(S_ready, c)
                    else:
                        pe.wait_ge(state_zero, 1)
                    for d in range(2):
                        ch = step if d == 0 else 1 - step
                        cs, ds = slice(CH * ch, CH * ch + CH), slice(CH * d, CH * d + CH)
                        for h in range(DNH):
                            hs = slice(hcol(h), hcol(h) + HD)
                            i, r = h // 2, h % 2
                            ins = nc.tensor.matmul(A[0][cs, hs], wT[ds, r, i * P + CH * ch:i * P + CH * ch + CH], state[ds, hs], start=True, stop=True)
                    ins.then_inc(wS_done, 1)
                    if lat:
                        for d in range(2):
                            ch = step if d == 0 else 1 - step
                            cs, ds = slice(CH * ch, CH * ch + CH), slice(CH * d, CH * d + CH)
                            for h in range(DNH):
                                hs = slice(hcol(h), hcol(h) + HD)
                                i, r = h // 2, h % 2
                                nc.tensor.matmul(A[1 + d][cs, hs], q_decT[ds, r, i * P + CH * ch:i * P + CH * ch + CH], state[ds, hs], start=True, stop=True)
                    pe.wait_ge(u_ready, c + 1)
                    for d in range(2):
                        ch = step if d == 0 else 1 - step
                        cs, ds = slice(CH * ch, CH * ch + CH), slice(CH * d, CH * d + CH)
                        if c < 7:
                            for h in range(DNH):
                                hs = slice(hcol(h), hcol(h) + HD)
                                ins = nc.tensor.matmul(A[3][ds, hs], k_tail[cs, d, HD * h:HD * h + HD], u_st[cs, step, hs], start=True, stop=True)
                    if c < 7:
                        ins.then_inc(su_done, 1)
                    if lat:
                        for d in range(2):
                            ch = step if d == 0 else 1 - step
                            cs = slice(CH * ch, CH * ch + CH)
                            for h in range(DNH):
                                hs = slice(hcol(h), hcol(h) + HD)
                                i, r = h // 2, h % 2
                                ins = nc.tensor.matmul(G[d][cs, hs], intraT[cs, d, r, i * P + CH * ch:i * P + CH * ch + CH], u_st[cs, step, hs],
                                                       start=True, stop=True)
                        if step:
                            ins.then_inc(o_done, 1)
            pe.wait_ge(yd_ready, 1)
            for q in range(2):
                for a in range(2):
                    for t in range(NT):
                        ins = nc.tensor.transpose(A[q][:, a * SEQ + t * P:a * SEQ + t * P + P], dz[:, t, (2 * q + a) * P:(2 * q + a + 1) * P], ident)
                ins.then_inc(ydT_done, 1)
            k.f += 2
            f_y = k.f
            for n in range(4):
                pn = k.panel("act")
                wait_panel_free(pn)
                for h in range(2):
                    unit(h_hi, h_lo, range(4 * h, 4 * h + 4), G[2 * (pn % 2):2 * (pn % 2) + 2], h == 0, h == 1)
            pe.wait_ge(split_lo, f_y)
            for n in range(4):
                pn = k.panel("dve")
                wait_panel_free(pn)
                unit(act_hi[:, 4 * (n // 2):], act_lo[:, 4 * (n // 2):], range(4), G[2 * (pn % 2):2 * (pn % 2) + 2], True, True)
            pe.wait_ge(split_full, f_y)
            for q in range(4):
                pe.wait_ge(yy_ready, q // 2 + 1)
                for i in range(2):
                    for t in range(NT):
                        ins = nc.tensor.transpose(A[q][:, i * SEQ + t * P:i * SEQ + t * P + P], n_st[:, t, (2 * q + i) * P:(2 * q + i + 1) * P], ident)
                ins.then_inc(yT_done, 1)
            k.f += 4
            po = [k.panel("dve"), k.panel("dve")]
            for h in range(2):
                pe.wait_ge(split_lo, k.f - 2 + 2 * h)
                for j in range(2):
                    if h == 0:
                        wait_panel_free(po[j])
                    unit(h_hi, h_lo, range(4 * h, 4 * h + 4), G[2 * (po[j] % 2):2 * (po[j] % 2) + 2], h == 0, h == 1)
            norm_transposes()
            f_h = k.f

            def hidden_transposes(p):
                pe.wait_ge(hid_ready, p + 1)
                pe.wait_ge(split_full, k.f - 2)
                for q in range(2):
                    for a in range(2):
                        for t in range(NT):
                            ins = nc.tensor.transpose(A[2 * (p % 2) + q][:, a * SEQ + t * P:a * SEQ + t * P + P],
                                                      hid_st[:, t, (2 * q + a) * P:(2 * q + a + 1) * P], ident)
                    ins.then_inc(hidT_done, 1)
                k.f += 2

            for part in range(2):
                for p in range(4):
                    pn = k.panel("dve")
                    wait_panel_free(pn)
                    for h in range(2):
                        pe.wait_ge(split_lo, f_h - 2 + 2 * h)
                        unit(h_hi, h_lo, range(4 * h, 4 * h + 4), G[2 * (pn % 2):2 * (pn % 2) + 2], h == 0, h == 1)
                        if h == 0 and p >= 1:
                            hidden_transposes(4 * part + p - 1)
                f_a = k.f + 2
                for j in range(2):
                    pn = k.panel("dve")
                    wait_panel_free(pn)
                    for h in range(4):
                        pe.wait_ge(split_lo, f_a - 8 + 2 * (h + 1))
                        unit(act_hi, act_lo, range(4 * h, 4 * h + 4), G[2 * (pn % 2):2 * (pn % 2) + 2], h == 0, h == 3)
                        if j == 0 and h == 0:
                            hidden_transposes(4 * part + 3)


def kernel(**inputs):
    import concourse.bacc as _bacc
    from concourse.bass_utils import run_bass_kernel_spmd as _run

    nc = _bacc.Bacc("TRN2", target_bir_lowering=False, num_devices=1)
    arrays = {n: np.ascontiguousarray(v) for n, v in inputs.items()}
    cols = np.concatenate([arrays.pop(n).reshape(-1, P) for n in
                           ("norm_gain", "c", "c_2", "c_ctx_2", "g_norm1_2", "g_norm2_2")])
    arrays["cols"] = cols
    i = np.arange(P)
    eye = np.eye(P, dtype=np.float32)
    one = np.ones((P, P), np.float32)
    tri = (i[:, None] >= i[None, :]).astype(np.float32)
    m_sb = np.where(i[:, None] < i[None, :], 0.0, NEG).astype(np.float32)
    m_causal = np.where(i[None, :] <= i[:, None], 0.0, NEG).astype(np.float32)
    m_prev = np.where(i[None, :] > i[:, None], 0.0, NEG).astype(np.float32)
    arrays["consts"] = np.stack([eye, one, tri, m_sb, m_prev, m_causal])
    freq = (np.float32(1.0) / np.float32(10000.0) ** (np.arange(0, HD, 2, dtype=np.float32) / np.float32(HD))).astype(np.float32)
    ang = np.arange(SEQ, dtype=np.float32)[:, None] * freq[None, :]
    cos, sin = np.cos(ang), np.sin(ang)
    arrays["rope"] = np.stack([np.concatenate([cos, cos], 1), np.concatenate([-sin, sin], 1)]).astype(np.float32)
    freq = (np.float32(10000.0) ** (-np.arange(16, dtype=np.float32) / np.float32(16))).astype(np.float32)
    pos = np.arange(SEQ)
    ang = [(pos // 64).astype(np.float32)[:, None] * freq[None, :], (pos % 64).astype(np.float32)[:, None] * freq[None, :]]
    arrays["rope_2"] = np.stack([np.concatenate([f(a) for a in ang for f in (np.cos, np.cos)], 1),
                                 np.concatenate([f(a) for a in ang for f in (lambda x: -np.sin(x), np.sin)], 1)]).astype(np.float32)
    a, b = i[:, None], i[None, :]
    same = a // CH == b // CH
    half = np.concatenate([np.repeat(i[:, None] // CH == h, CH, 1) for h in range(2)], 1)
    arrays["consts_2"] = np.stack([same & (a <= b), same & (a >= b), same & (a > b), same & (a < b), half]).astype(np.float32)
    lower = [(a // (2 * s) == b // (2 * s)) & (a // s % 2 == 1) & (b // s % 2 == 0) for s in (1, 2, 4, 8, 16, 32)]
    allow = lambda m: np.where(m, 0.0, NEG)
    arrays["masks_2"] = np.stack(lower + [m.T for m in lower] + [allow(same & (a < b)), allow(same & (a > b)), allow(same & (a <= b)),
                                                                 allow(same & (a >= b)), allow(b >= a)]).astype(np.float32)
    arrays["zeros"] = np.zeros((1, 512), np.float32)
    keep = ["x", "cols", "consts", "rope", "ada_w", "ada_b", "ffn_w_gate", "ffn_w_up", "ffn_w_down", "sb_w_in", "sb_w_out",
            "moba_w_in", "moba_w_out", "moba_qk_gain", "swa_w_in", "swa_w_out", "swa_qk_gain", "swa_sinks",
            "ctx_2", "w_ada_2", "b_ada_2", "w_in_2", "q_norm_g_2", "k_norm_g_2", "attn_sink_2", "conv_w_2", "a_log_2", "dt_bias_2",
            "dn_norm_g_2", "w_br_attn_2", "w_br_dn_2", "w_out_2", "w_mlp1_2", "w_mlp2_2", "rope_2", "consts_2", "masks_2", "zeros"]
    arrays = {n: arrays[n] for n in keep}
    w = {n: nc.dram_tensor(f"in_{n}", a.shape, mybir.dt.from_np(a.dtype), kind="ExternalInput").ap() for n, a in arrays.items()}
    out = nc.dram_tensor("out_x", (1, SEQ, D), F32, kind="ExternalOutput").ap()
    build(nc, w, out)
    r = _run(nc, [{f"in_{n}": a for n, a in arrays.items()}], core_ids=[0])
    return r.results[0]["out_x"]
```

```python
from contextlib import ExitStack

import numpy as np

import concourse.bass as bass
from concourse import mybir

F32 = mybir.dt.float32
F32R = mybir.dt.float32r
BF16 = mybir.dt.bfloat16
ACT = mybir.ActivationFunctionType
ALU = mybir.AluOpType
AX = mybir.AxisListType

P = 128
D = 1024
SEQ = 256
NT = SEQ // P
KT = D // P
HD = 64
DEPTH = 4
FF = 2816
FFT = FF // P
EPS = 1e-6
UNIT_K = 4
RING = 4
GROUP = 4
NEG = -1e30
KINDS = ["sb", "moba", "swa", "sb"]
CONSTS = ["ident", "ones", "tri", "m_sb", "m_prev", "m_causal"]
NCOL = 104
LAT = DEPTH
LAT_QH = 8
DNH = 8
CH = 64
LEVELS = 6
AQ, AK, AV = 0, 512, 640
DQ, DK, DV, DZ = 768, 1280, 1792, 2304
DAB = 2816
GA = 2848
FF2 = 4096
CONSTS_2 = ["tri_f", "tri_b", "later_f", "later_b", "half"]
MASKS_2 = 2 * LEVELS + 5


class Walk:

    def __init__(self):
        self.s = 0
        self.u = 0
        self.pn = 0
        self.f = 0
        self.a = 0
        self.sums = 0
        self.m = 0
        self.rms = 0
        self.norms = 0
        self.normed = {}
        self.group = 0
        self.sb = 0
        self.sm = 0
        self.kt = 0
        self.swa = 0
        self.slot_done = [0] * RING
        self.free_act = 0
        self.free_dve = 0
        self.panel_free = []

    def end_mixer(self, kind):
        self.group += 4
        self.sb += 4 * (kind == "sb")
        self.sm += 4 * (kind != "sb")
        self.kt += 4 * (kind != "swa")
        self.swa += kind == "swa"

    def next_load(self, loads, kind):
        while True:
            load = loads[self.s]
            slot = self.s % RING
            self.s += 1
            self.slot_done[slot] += 16 * (len(load[1]) if load[0] == "unit" else 1)
            if load[0] == kind:
                return slot, self.slot_done[slot], load

    def panel(self, engine):
        pn = self.pn
        self.pn += 1
        if engine == "act":
            self.free_act += 1
            self.panel_free.append(("act", self.free_act))
        else:
            self.free_dve += 1
            self.panel_free.append(("dve", self.free_dve))
        return pn


def build(nc, w, out):
    with ExitStack() as ctx:
        top = [-(-nc.sbuf_base // 64) * 64]

        def at(name, cols, dtype=F32, offset=None, parts=P):
            if offset is None:
                offset = top[0]
                top[0] += -(-cols * (2 if dtype == BF16 else 4) // 64) * 64
            return nc.alloc_sbuf_tensor_at(name, [parts, cols], dtype, offset=offset), offset

        def tile(name, cols, dtype=F32, offset=None, parts=P):
            return at(name, cols, dtype, offset, parts)[0][:, :]

        def sem(name):
            return ctx.enter_context(nc.semaphore(name))

        raw_t, raw_off = at("raw", RING * 2048)
        raw = raw_t[:, :].rearrange("p (s n) -> p s n", s=RING)
        w_hi = tile("w_hi", 2 * 2048, F32R).rearrange("p (s k n) -> p s k n", s=2, k=UNIT_K)
        w_lo = tile("w_lo", 2 * 2048, F32R).rearrange("p (s k n) -> p s k n", s=2, k=UNIT_K)
        x_res = tile("x_res", NT * D).rearrange("p (t d) -> p t d", t=NT)
        h_hi_t, h_off = at("h_hi", KT * SEQ, F32R)
        h_hi = h_hi_t[:, :].rearrange("p (k n) -> p k n", k=KT)
        h_lo = tile("h_lo", KT * SEQ, F32R).rearrange("p (k n) -> p k n", k=KT)
        act_hi_t, act_hi_off = at("act_hi", FFT * SEQ, F32R)
        act_hi = act_hi_t[:, :].rearrange("p (k n) -> p k n", k=FFT)
        act_lo_t, act_lo_off = at("act_lo", FFT * SEQ, F32R)
        act_lo = act_lo_t[:, :].rearrange("p (k n) -> p k n", k=FFT)
        gates = tile("gates", 2 * D).rearrange("p (g n) -> p g n", g=2)
        full = tile("full", 2 * 512).rearrange("p (b n) -> p b n", b=2)
        consts = tile("consts", len(CONSTS) * P).rearrange("p (c n) -> p c n", n=P)
        ident, ones, tri = consts[:, 0], consts[:, 1], consts[:, 2]
        ident_b = tile("ident_b", P, BF16)
        masks_b = tile("masks_b", 3 * P, BF16).rearrange("p (c n) -> p c n", n=P)
        m_sb, m_causal, m_window = masks_b[:, 0], masks_b[:, 2], masks_b[:, 1:3]
        cols_in = tile("cols_in", P, parts=NCOL)
        cols_in2 = tile("cols_in2", P, parts=36)
        cols = tile("cols", NCOL + 36)
        c_col = tile("c_col", 24)
        mod = tile("mod", 2 * 48).rearrange("p (l n) -> p l n", l=2)
        gsc = tile("gsc", 2 * 24).rearrange("p (l n) -> p l n", l=2)
        ssq = tile("ssq", 4).rearrange("p (t n) -> p t n", t=2)
        ssum = tile("ssum", 2)
        rms_v = tile("rms_v", 48)
        rms_y = tile("rms_y", 48)
        rms_t = tile("rms_t", 48)
        n_max = tile("n_max", 8)
        p_sum = tile("p_sum", 8)
        p_inv = tile("p_inv", 8)
        sink_e = tile("sink_e", 8)
        rope_cs = tile("rope_cs", 2 * NT * HD).rearrange("p (a t d) -> p a t d", a=2, t=NT)
        rope_g = tile("rope_g", 2 * HD).rearrange("p (q d) -> p q d", q=2)
        rope_t_t, rope_t_off = at("rope_t", 2 * NT * 2 * HD)
        rope_t = rope_t_t[:, :].rearrange("p (a t q d) -> p a t q d", a=2, t=NT, q=2)
        sinks = tile("sinks", 16)
        ss16 = tile("ss16", 48)
        att_t, acc_off = at("att", 6 * D)
        z_sb = tile("z_sb", 3 * 512, offset=acc_off).rearrange("p (b n) -> p b n", b=3)
        e_sb = tile("e_sb", 3 * 512, offset=acc_off + 6144).rearrange("p (b n) -> p b n", b=3)
        aT = tile("aT", 3 * 512, offset=acc_off + 2 * 6144).rearrange("p (b n) -> p b n", b=3)
        qT = tile("qT", 512, offset=acc_off + 3 * 6144).rearrange("p (a n) -> p a n", a=2)
        kT = tile("kT", 512, offset=acc_off + 3 * 6144 + 2048).rearrange("p (a n) -> p a n", a=2)
        qk_t, qk_off = at("qk_st", 2 * NT * 512)
        qk_st = qk_t[:, :].rearrange("p (b t n) -> p b t n", b=2, t=NT)
        n_st = tile("n_st", NT * D, offset=qk_off).rearrange("p (t d) -> p t d", t=NT)
        silu_st = tile("silu_st", NT * 256, offset=qk_off).rearrange("p (t n) -> p t n", t=NT)
        act_st = tile("act_st", NT * 256, offset=qk_off + 2048).rearrange("p (t n) -> p t n", t=NT)
        v_st = tile("v_st", 2 * NT * 512, offset=act_lo_off + 8 * 1024).rearrange("p (b t n) -> p b t n", b=2, t=NT)
        rope_st = tile("rope_st", NT * 512, offset=act_hi_off + 8 * 1024).rearrange("p (t n) -> p t n", t=NT)
        KB = 1024
        acc_t, d_off = at("acc", 2 * 2 * D)
        acc = acc_t[:, :].rearrange("p (b n) -> p b n", b=2)
        acc_c = tile("acc_c", 2 * D, offset=acc_off)
        s_off = d_off + 2 * D * 4
        consts_2 = tile("consts_2", len(CONSTS_2) * P, offset=s_off).rearrange("p (c n) -> p c n", n=P)
        tri_dir, later_dir, half = consts_2[:, 0:2], consts_2[:, 2:4], consts_2[:, 4].rearrange("p (h n) -> p h n", h=2)
        masks_2 = tile("masks_2", MASKS_2 * P, BF16, offset=s_off + len(CONSTS_2) * P * 4).rearrange("p (c n) -> p c n", n=P)
        level_mask = masks_2[:, 0:2 * LEVELS].rearrange("p (d l) n -> p d l n", d=2)
        m_strict, m_incl, m_from = masks_2[:, 2 * LEVELS:2 * LEVELS + 2], masks_2[:, 2 * LEVELS + 2:2 * LEVELS + 4], masks_2[:, 2 * LEVELS + 4]
        dn_rows = tile("dn_rows", 2 * 2 * DNH + HD)
        alog_row, dtb_row, dng_row = dn_rows[:, 0:16], dn_rows[:, 16:32], dn_rows[:, 32:96]
        dab = tile("dab", 4 * 32).rearrange("p (s n) -> p s n", s=4)
        gate_z = tile("gate_z", 4 * 32).rearrange("p (s n) -> p s n", s=4)
        gate_s = tile("gate_s", 4 * 32).rearrange("p (s n) -> p s n", s=4)
        g_all = tile("g_all", 64).rearrange("p (s n) -> p s n", s=4)
        lnb_all = tile("lnb_all", 64).rearrange("p (s n) -> p s n", s=4)
        beta = tile("beta", 64).rearrange("p (s d h) -> p s d h", s=4, d=2)
        neg_G = tile("neg_G", 64).rearrange("p (d s h) -> p d s h", d=2, s=4)
        e_G = tile("e_G", 64).rearrange("p (d s h) -> p d s h", d=2, s=4)
        e_tail = tile("e_tail", 64).rearrange("p (d s h) -> p d s h", d=2, s=4)
        beG = tile("beG", 64).rearrange("p (d s h) -> p d s h", d=2, s=4)
        lnb_G = tile("lnb_G", 64).rearrange("p (d s h) -> p d s h", d=2, s=4)
        e_last = tile("e_last", 64).rearrange("p (c h) -> p c h", h=DNH)
        assert top[0] <= nc.sbuf_usable_end, top[0]

        def token_tile(name, cols, offset):
            return tile(name, NT * cols, offset=offset).rearrange("p (t n) -> p t n", t=NT)

        AH, AL, AB, AC = act_hi_off, act_lo_off, acc_off, qk_off
        ctx_raw = token_tile("ctx_raw", D, AL + 8 * KB)
        mask_st = tile("mask_st", MASKS_2 * P, offset=AH + 8 * KB).rearrange("p (c n) -> p c n", n=P)
        dk_x, dv_x, dq_x = (token_tile(n, 512, AH + (8 + 4 * i) * KB) for i, n in enumerate(("dk_x", "dv_x", "dq_x")))
        dk_c, dv_c, dz = (token_tile(n, 512, AL + (8 + 4 * i) * KB) for i, n in enumerate(("dk_c", "dv_c", "dz")))
        aq = token_tile("aq", 512, AB)
        lrope_st = token_tile("lrope_st", 512, AB + 4 * KB)
        lrot = token_tile("lrot", 512, AB + 8 * KB)
        kva_x, kva_c = token_tile("kva_x", 256, AB + 12 * KB), token_tile("kva_c", 256, AB + 14 * KB)
        kdup = tile("kdup", 4 * 256, offset=AB + 16 * KB).rearrange("p (t n) -> p t n", t=4)
        lkT = tile("lkT", 2 * 512, offset=AB + 20 * KB).rearrange("p (g n) -> p g n", g=2)
        lqT = tile("lqT", 4 * SEQ, offset=AB + 8 * KB).rearrange("p (a n) -> p a n", a=4)
        laT = tile("laT", 4 * 512, offset=AB).rearrange("p (b n) -> p b n", b=4)
        p_sb = tile("p_sb", 4 * 512, offset=AC).rearrange("p (b n) -> p b n", b=4)
        conv_t = tile("conv_t", 2 * 4 * SEQ, offset=AC).rearrange("p (b a n) -> p b a n", b=2, a=4)
        sq_t = [token_tile(f"sq_t{i}", 512, AB + (16 + 4 * i) * KB) for i in range(2)]
        kT_c = tile("kT_c", 4 * SEQ, offset=AH + 4 * KB).rearrange("p (a n) -> p a n", a=4)
        kT_x = tile("kT_x", 4 * SEQ, offset=AL + 4 * KB).rearrange("p (a n) -> p a n", a=4)
        qT_x = tile("qT_x", 4 * SEQ, offset=d_off).rearrange("p (a n) -> p a n", a=4)
        o_dn = token_tile("o_dn", 512, d_off + 4 * KB)
        wT = tile("wT", 1024, offset=AC).rearrange("p (r n) -> p r n", r=2)
        u_st = tile("u_st", 1024, offset=AB + 20 * KB).rearrange("p (s n) -> p s n", s=2)
        k_tail = tile("k_tail", 1024, offset=AC + 4 * KB).rearrange("p (d n) -> p d n", d=2)
        state = tile("state", 512, offset=AL)
        state_t = tile("state_t", 512, offset=rope_t_off)
        intraT = tile("intraT", 2048, offset=AL + 8 * KB).rearrange("p (d r n) -> p d r n", d=2, r=2)
        q_decT = tile("q_decT", 1024, offset=AH + 4 * KB).rearrange("p (r n) -> p r n", r=2)
        sig = tile("sig", 2 * NT * D, offset=AB).rearrange("p (b t n) -> p b t n", b=2, t=NT)
        relu_st, hid_st = token_tile("relu_st", 512, AC), token_tile("hid_st", 512, AC + 4 * KB)

        G = [ctx.enter_context(nc.psum_tensor(f"G{i}", [P, 512], F32))[:, :] for i in range(4)]
        A = [ctx.enter_context(nc.psum_tensor(f"A{i}", [P, 512], F32))[:, :] for i in range(4)]

        landed = [sem(f"landed{i}") for i in range(RING)]
        raw_free = sem("raw_free")
        hi_ready = sem("hi_ready")
        lo_ready = sem("lo_ready")
        gemm_done = sem("gemm_done")
        free_act = sem("free_act")
        free_dve = sem("free_dve")
        const_in = sem("const_in")
        rope_in = sem("rope_in")
        x_in = sem("x_in")
        gain_in = sem("gain_in")
        rope_ready = sem("rope_ready")
        pool_step = sem("pool_step")
        sq_ready = sem("sq_ready")
        xn_ready = sem("xn_ready")
        rot_ready = sem("rot_ready")
        qk_ready = sem("qk_ready")
        max_ready = sem("max_ready")
        p_ready = sem("p_ready")
        pn_ready = sem("pn_ready")
        pT_done = sem("pT_done")
        sink_ready = sem("sink_ready")
        se_ready = sem("se_ready")
        cast_ready = sem("cast_ready")
        cols_T = sem("cols_T")
        cols_ready = sem("cols_ready")
        c_ready = sem("c_ready")
        acc_zero = sem("acc_zero")
        bias_in = [sem(f"bias_in{i}") for i in range(2)]
        acc_done = sem("acc_done")
        sums_done = sem("sums_done")
        mod_out = sem("mod_out")
        gsc_ready = sem("gsc_ready")
        ss_ready = sem("ss_ready")
        v_ready = sem("v_ready")
        y_ready = sem("y_ready")
        n_ready = sem("n_ready")
        norm_T = sem("norm_T")
        split_full = sem("split_full")
        split_hi = sem("split_hi")
        split_lo = sem("split_lo")
        x_ready = sem("x_ready")
        y_gated = sem("y_gated")
        kvT_done = sem("kvT_done")
        kvT_ready = sem("kvT_ready")
        s_done = sem("s_done")
        qkT_done = sem("qkT_done")
        qT_ready = sem("qT_ready")
        kT_ready = sem("kT_ready")
        z_done = sem("z_done")
        z_copied = sem("z_copied")
        nabs_ready = sem("nabs_ready")
        exp_ready = sem("exp_ready")
        ln_ready = sem("ln_ready")
        sp_ready = sem("sp_ready")
        r_done = sem("r_done")
        d_ready = sem("d_ready")
        aT_ready = sem("aT_ready")
        av_done = sem("av_done")
        silu_ready = sem("silu_ready")
        act_ready = sem("act_ready")
        actT_done = sem("actT_done")
        dve_step = sem("dve_step")
        out_done = sem("out_done")
        accc_zero = sem("accc_zero")
        biasc_in = sem("biasc_in")
        accc_done = sem("accc_done")
        ctx_in = sem("ctx_in")
        lat_in = sem("lat_in")
        masks_in = sem("masks_in")
        masks_ready = sem("masks_ready")
        rope2_ready = sem("rope2_ready")
        ltT_done = sem("ltT_done")
        kq_act = sem("kq_act")
        kq_dve = sem("kq_dve")
        ws_done = sem("ws_done")
        wmax_ready = sem("wmax_ready")
        wp_ready = sem("wp_ready")
        wse_ready = sem("wse_ready")
        wn_ready = sem("wn_ready")
        wpT_done = sem("wpT_done")
        waT_act = sem("waT_act")
        waT_dve = sem("waT_dve")
        woT_done = sem("woT_done")
        cvT_done = sem("cvT_done")
        cvB_done = sem("cvB_done")
        cb_ready = sem("cb_ready")
        dz_ready = sem("dz_ready")
        l2q_ready = sem("l2q_ready")
        l2s_ready = sem("l2s_ready")
        sig_ready = sem("sig_ready")
        conv_ready = sem("conv_ready")
        cs_ready = sem("cs_ready")
        l2_ready = sem("l2_ready")
        gz_ready = sem("gz_ready")
        ge_ready = sem("ge_ready")
        gl_ready = sem("gl_ready")
        ea_ready = sem("ea_ready")
        gates_ready = sem("gates_ready")
        beta_ready = sem("beta_ready")
        gsum_done = sem("gsum_done")
        eg_ready = sem("eg_ready")
        beg_ready = sem("beg_ready")
        dT_done = sem("dT_done")
        dT_act = sem("dT_act")
        dT_dve = sem("dT_dve")
        e_done = sem("e_done")
        kk_done = sem("kk_done")
        E_ready = sem("E_ready")
        LT_ready = sem("LT_ready")
        y_done = sem("y_done")
        X_ready = sem("X_ready")
        x_done = sem("x_done")
        xT_done = sem("xT_done")
        prep_ready = sem("prep_ready")
        wT_done = sem("wT_done")
        uv_done = sem("uv_done")
        wT_ready = sem("wT_ready")
        uv_ready = sem("uv_ready")
        in_done = sem("in_done")
        id_done = sem("id_done")
        ie_ready = sem("ie_ready")
        intra_ready = sem("intra_ready")
        qdT_done = sem("qdT_done")
        qdT_ready = sem("qdT_ready")
        state_zero = sem("state_zero")
        wS_done = sem("wS_done")
        u_ready = sem("u_ready")
        su_done = sem("su_done")
        S_ready = sem("S_ready")
        o_done = sem("o_done")
        oacc_ready = sem("oacc_ready")
        yd_ready = sem("yd_ready")
        ydT_done = sem("ydT_done")
        yy_ready = sem("yy_ready")
        yT_done = sem("yT_done")
        relu_ready = sem("relu_ready")
        hid_ready = sem("hid_ready")
        hidT_done = sem("hidT_done")

        L_ready = sem("L_ready")
        Z_ready = sem("Z_ready")
        XT_ready = sem("XT_ready")

        ADA_U = 3 * KT
        SB_SLOTS = {2: [("T", 0)], 3: [("S", 0)], 4: [("C", 0)], 5: [("T", 1)], 6: [("V", 0), ("S", 1)], 7: [("C", 1)],
                    8: [("V", 1), ("T", 2)], 9: [("S", 2)], 10: [("C", 2)], 11: [("V", 2)], 12: [("T", 3), ("S", 3)],
                    13: [("C", 3), ("V", 3)]}
        MOBA_SLOTS = {2: [("N", 0)], 4: [("T", 0), ("N", 1)], 5: [("S", 0)], 6: [("C", 0)], 7: [("V", 0), ("T", 1)],
                      8: [("S", 1), ("N", 2)], 9: [("C", 1)], 10: [("V", 1), ("N", 3), ("T", 2)], 11: [("S", 2)],
                      12: [("C", 2), ("T", 3)], 13: [("V", 2), ("S", 3), ("C", 3), ("V", 3)]}
        SWA_SLOTS = {2: [("N", "kv")], 3: [("T", "kv")], 4: [("N", 0)],
                     5: [(x, g) for g in range(2) for x in "TSCV"],
                     6: [("N", 2)] + [(x, 2) for x in "TSCV"], 7: [(x, 3) for x in "TSCV"]}
        SLOTS = {"sb": SB_SLOTS, "moba": MOBA_SLOTS, "swa": SWA_SLOTS}

        def qkv_panels(kind):
            if kind == "swa":
                return [("kv", 0, [(0, D, 256)])] + [("q", b, [(0, 512 * b, 512)]) for b in range(2)]
            qk = [("qk", g, [(0, 256 * g, 256), (256, D + 256 * g, 256)]) for g in range(4)]
            v = [("v", b, [(0, 2 * D + 512 * b, 512)]) for b in range(2)]
            if kind == "sb":
                return [qk[0], qk[1], v[0], qk[2], v[1], qk[3]]
            return [qk[0], qk[1], v[0], qk[2], qk[3], v[1]]

        def width(panel):
            return sum(n for _, _, n in panel[2])

        def staged(kind, g):
            return (g // 2, 256 * (g % 2)) if kind == "swa" else (g % 2, 0)

        def normed(kind, g):
            if g == "kv":
                return qk_st[:, 1, :, 0:P], 2, slice(1, 2)
            return qk_st[:, staged(kind, g)[0]], 8, slice(0, 1) if kind == "swa" else slice(0, 2)

        def by_table(x, tables):
            return x.rearrange("p (q h d) -> p q h d", q=tables.stop - tables.start, d=HD)

        def for_heads(table, heads):
            p, q, d = table.shape
            return table.rearrange("p q (o d) -> p q o d", o=1).broadcast_to([p, q, heads, d])

        def swap_halves(x):
            n = x.shape[-1] // 2
            return x[..., n:2 * n], x[..., 0:n]

        def rope_layers(kind):
            return 1 if kind == "moba" else 2

        def mixer(l):
            kind = KINDS[l]
            j = l // 3
            w_in = {"sb": "sb_w_in", "moba": "moba_w_in", "swa": "swa_w_in"}[kind]
            w_out = {"sb": "sb_w_out", "moba": "moba_w_out", "swa": "swa_w_out"}[kind]
            return kind, w[w_in][j], w[w_out][j]

        LAT_PANELS = [("kv", AK, 256, True), ("q", AQ, 512, False), ("dk", DK, 512, True), ("dv", DV, 512, True), ("dab", DAB, 32, True),
                      ("dq", DQ, 512, False), ("dz", DZ, 512, False)] + [(f"gate{n}", GA + 512 * n, 512, False) for n in range(4)]
        LAT_UNITS = 2 * len(LAT_PANELS)
        LAT_SLOTS = {2: [("N", "kx"), ("N", "kc")], 4: [("N", "q")], 5: [("T", 0), ("S", 0)], 6: [("P", 0)], 7: [("V", 0), ("S", 1)],
                     8: [("P", 1)], 9: [("V", 1), ("S", 2)], 10: [("P", 2)], 11: [("V", 2), ("S", 3)], 12: [("P", 3)], 13: [("V", 3)],
                     14: [("X", 0)], 15: [("Y", 0), ("X", 1)], 16: [("Y", 1), ("X", 2)], 17: [("Y", 2), ("X", 3)],
                     18: [("Y", 3), ("X", 4)], 19: [("Y", 4)], 20: [("L", 0)], 21: [("W", 0)]}
        Y_ATTN = [20, 21, 2, 3]
        LAT_F = DEPTH * (2 * (KT // 2) + 4 + FF // 256) + KT
        CONV = [(dk_c, 1), (dv_c, 2), (dk_x, 1), (dv_x, 2), (dq_x, 0)]

        def lat_heads(what):
            return {"kx": (kva_x[:, :, 0:P], 2), "kc": (kva_c[:, :, 0:P], 2), "q": (aq, 8)}[what]

        def over_heads(row, n):
            return row.rearrange("p (o d) -> p o d", o=1).broadcast_to([row.shape[0], n, row.shape[-1]])

        def over_elems(cols, d=HD):
            return cols.rearrange("p (h o) -> p h o", o=1).broadcast_to([cols.shape[0], cols.shape[1], d])

        def heads(x, d=HD):
            return x.rearrange("p (h d) -> p h d", d=d)

        def halves32(x):
            return x.rearrange("p (b d) -> p b d", d=32)

        def hcol(h):
            return (h % 2) * 256 + (h // 2) * HD

        def solved(rd, lev, c):
            return 4 * (LEVELS * rd + lev) + c + 1

        def joined(rd, lev, c, last=LEVELS):
            return 4 * ((last - 1) * rd + lev - 1) + c + 1

        def delta_tile(rd, d):
            t = rd % 2 if d == 0 else 1 - rd % 2
            return t, 2 * (rd // 2) + t

        def rows(ap):
            return ap.rearrange("(k p) n -> p k n", p=P)

        ADA_MIX = [{}, {}, {}, {}]
        ADA_UP = [{}, {}, {}, {}]
        ADA_DOWN = [{}, {}, {}, {}]
        for i in range(2 * KT):
            ADA_MIX[0].setdefault(max(0, i - 2), []).append((0, KT + i))
        for l in (1, 2):
            for i in range(KT):
                ADA_MIX[l].setdefault(i + (l == 1), []).append((l + 1, i))
        for l in range(DEPTH):
            first = KT if l in (1, 2) else 0
            for i in range(first, ADA_U):
                p = max(0, i - first - 2)
                if p < FF // 256:
                    ADA_UP[l].setdefault(p, []).append((l + 1, i))
                else:
                    ADA_DOWN[l].setdefault(p - FF // 256, []).append((l + 1, i))
        SUMS = {(l, pos): piece for l in range(DEPTH) for pos, piece in
                (((("up", 2), "c0"), (("up", 9), "r1"), (("up", 10), "c1")) if l in (1, 2) else
                 ((("up", 9), "c0"), (("down", 7), "r1"), (("down", 9), "c1")))}

        def mods(l, piece):
            return 7 * l + {"c0": 1, "r1": 3, "c1": 4, "c2": 5, "r2": 7}[piece]

        def mod_cols(l, piece):
            return {"c0": slice(0, 16), "c1": slice(16, 24), "c2": slice(24, 32)}[piece]

        units, loads, small = [], [], {}

        def add(m, pieces, kts):
            units.append(("unit", [(c0, mm, c1, n) for c0, mm, c1, n in pieces], list(kts), sum(p[3] for p in pieces)))

        mixer_units = []
        for l in range(DEPTH):
            kind, w_in, w_out = mixer(l)
            for what, g, pieces in qkv_panels(kind):
                for h in range(2):
                    add(w_in, [(c0, w_in, c1, n) for c0, c1, n in pieces], range(4 * h, 4 * h + 4))
            for h in range(2):
                for n in range(2):
                    add(w_out, [(0, w_out, 512 * n, 512)], range(4 * h, 4 * h + 4))
            wg, wu, wd = w["ffn_w_gate"][l], w["ffn_w_up"][l], w["ffn_w_down"][l]
            for p in range(FF // 256):
                for h in range(2):
                    add(wg, [(0, wg, 256 * p, 256), (256, wu, 256 * p, 256)], range(4 * h, 4 * h + 4))
            for n in range(2):
                for h in range(6):
                    add(wd, [(0, wd, 512 * n, 512)], range(4 * h, min(4 * h + 4, FFT)))
        u_lat = len(units)
        w_in2 = w["w_in_2"][0]
        for _, c, n, _ in LAT_PANELS:
            for h in range(2):
                add(w_in2, [(0, w_in2, c, n)], range(4 * h, 4 * h + 4))
        for m in (w["w_br_attn_2"][0], w["w_br_dn_2"][0]):
            for n in range(2):
                add(m, [(0, m, 512 * n, 512)], range(4))
        for h in range(2):
            for n in range(2):
                add(None, [(0, w["w_out_2"][0], 512 * n, 512)], range(4 * h, 4 * h + 4))
        for part in range(2):
            for p in range(4):
                for h in range(2):
                    add(None, [(0, w["w_mlp1_2"][0], 2048 * part + 512 * p, 512)], range(4 * h, 4 * h + 4))
            for n in range(2):
                for h in range(4):
                    add(None, [(0, w["w_mlp2_2"][0], 512 * n, 512)], range(16 * part + 4 * h, 16 * part + 4 * h + 4))
        def more_units(n, n_mix):
            return 0 if n == 0 else 2 if n == n_mix - 1 else 1

        for n in range(KT):
            if n == 3:
                small[len(loads)] = [("x",)]
            loads.append(("ada", 0, n))
        ahead = iter(units)
        loads += [next(ahead), next(ahead)]
        for l in range(DEPTH):
            small.setdefault(len(loads), []).append(("mixer", l))
            n_mix = 2 * len(qkv_panels(KINDS[l])) + 4
            for n in range(n_mix):
                loads += [next(ahead) for _ in range(more_units(n, n_mix))]
                loads += [("ada", *a) for a in ADA_MIX[l].get(n, [])]
            for p in range(FF // 256):
                loads += [next(ahead) for _ in range(2 if p else 1)]
                loads += [("ada", *a) for a in ADA_UP[l].get(p, [])]
            for j in range(12):
                loads += [next(ahead) for _ in range(1 if j else 2)]
                loads += [("ada", *a) for a in ADA_DOWN[l].get(j, [])]
        small.setdefault(len(loads) + 1, []).append(("lat",))
        loads += list(ahead)

        HELD = len(loads) - len(units) + u_lat + LAT_UNITS + 3
        def chains(name, offset):
            return tile(name, 4 * 512, offset=offset).rearrange("p (c n) -> p c n", c=4)

        def held_slot(i):
            return raw_off + (HELD + i) % RING * 8 * KB

        LT, X = chains("LT", h_off), chains("X", h_off + 8 * KB)
        XT, Z = chains("XT", held_slot(0)), chains("Z", held_slot(1))
        bek, bv, q_dec = (tile(n, 1024, offset=o).rearrange("p (d n) -> p d n", d=2)
                          for n, o in (("bek", held_slot(2)), ("bv", held_slot(2) + 4 * KB), ("q_dec", AB + 16 * KB)))

        SUM_BANKS = {(l, piece): banks for l in range(DEPTH + 1) for piece, banks in
                     (("c0", [A[2]]), ("r1", [A[2], A[3]]), ("c1", [A[2]]), ("c2", [A[2]]), ("r2", [A[3], A[1]]))}
        KQ_BANKS = [(A[2], A[3]), (A[0], A[1]), (A[2], A[3])]
        SUM_BANKS[0, "r1"], SUM_BANKS[0, "c1"] = [A[1], A[2]], [A[0]]

        block = ctx.enter_context(nc.Block())

        @block.sync
        def _(sp):

            def transfers(what):
                if what[0] == "x":
                    sp.dma_start(x_res, w["x"][0].rearrange("(t p) d -> p t d", p=P)).then_inc(x_in, 16)
                elif what[0] == "mixer":
                    l = what[1]
                    kind = KINDS[l]
                    if kind != "sb":
                        if l > 1:
                            sp.wait_ge(x_ready, 4 * l - 2)
                        g_in = w[f"{kind}_qk_gain"]
                        sp.dma_start(rope_g, g_in[l // 3].rearrange("(o q) d -> o q d", o=1).broadcast_to([P, 2, HD])).then_inc(gain_in, 16)
                    if kind == "swa":
                        sp.dma_start(sinks, w["swa_sinks"][l // 3:l // 3 + 1, :].broadcast_to([P, 16])).then_inc(gain_in, 16)
                elif what[0] == "lat":
                    sp.wait_ge(x_ready, 16)
                    sp.dma_start(ctx_raw, w["ctx_2"][0].rearrange("(t p) d -> p t d", p=P)).then_inc(ctx_in, 16)
                    sp.dma_start(mask_st, w["masks_2"].rearrange("c p n -> p c n")).then_inc(masks_in, 16)
                    sp.dma_start(rope_cs, w["rope_2"].rearrange("a (t p) d -> p a t d", p=P)).then_inc(lat_in, 16)
                    sp.dma_start(rope_g[:, 0], w["q_norm_g_2"].broadcast_to([P, HD])).then_inc(lat_in, 16)
                    sp.dma_start(rope_g[:, 1], w["k_norm_g_2"].broadcast_to([P, HD])).then_inc(lat_in, 16)
                    sp.dma_start(sinks[:, 0:LAT_QH], w["attn_sink_2"].broadcast_to([P, LAT_QH])).then_inc(lat_in, 16)
                    sp.dma_start(alog_row, w["a_log_2"].rearrange("o a b -> o (a b)").broadcast_to([P, 16])).then_inc(lat_in, 16)
                    sp.dma_start(dtb_row, w["dt_bias_2"].rearrange("o a b -> o (a b)").broadcast_to([P, 16])).then_inc(lat_in, 16)
                    sp.dma_start(dng_row, w["dn_norm_g_2"].broadcast_to([P, HD])).then_inc(lat_in, 16)
                    sp.wait_ge(sums_done, mods(LAT, "r2"))
                    sp.dma_start(consts_2, w["consts_2"].rearrange("c p n -> p c n")).then_inc(lat_in, 16)
            sp.dma_start(cols_in, w["cols"]).then_inc(const_in, 16)
            sp.dma_start(cols_in2, w["cols_2"]).then_inc(const_in, 16)
            sp.dma_start(consts, w["consts"].rearrange("c p n -> p c n")).then_inc(const_in, 16)
            sp.dma_start(rope_cs, w["rope"].rearrange("a (t p) d -> p a t d", p=P)).then_inc(rope_in, 16)
            for s, load in enumerate(loads):
                for what in small.get(s, []):
                    transfers(what)
                slot = s % RING
                if s == HELD:
                    sp.wait_ge(qdT_done, 4)
                if s >= RING:
                    sp.wait_ge(raw_free, s - RING + 1)
                if load[0] == "unit":
                    _, pieces, kts, _ = load
                    dst = raw[:, slot].rearrange("p (k n) -> p k n", k=UNIT_K)
                    for c0, m, c1, n in pieces:
                        sp.dma_start(dst[:, 0:len(kts), c0:c0 + n], rows(m)[:, kts[0]:kts[0] + len(kts), c1:c1 + n]).then_inc(landed[slot], 16)
                else:
                    _, l, n = load
                    sp.dma_start(raw[:, slot], (w["ada_w"][l] if l < LAT else w["w_ada_2"][0]).rearrange("(k p) (c n) -> p c k n", p=P, c=3)[:, n // KT, n % KT])\
                        .then_inc(landed[slot], 16)
            sp.wait_ge(x_ready, 4 * DEPTH + 6)
            sp.dma_start(out.rearrange("b (t p) d -> p (b t) d", p=P), x_res).then_inc(out_done, 16)
            sp.wait_ge(out_done, 16)

        @block.gpsimd
        def _(pool):
            chain = [0]

            def link(ins):
                chain[0] += 1
                ins.then_inc(pool_step, 1)
                pool.wait_ge(pool_step, chain[0])

            def tables(kind):
                pool.wait_ge(rope_in, 16)
                pool.wait_ge(gain_in, 16 if kind == "moba" else 48)
                q_gain = rope_g[:, 0]
                link(nc.gpsimd.tensor_scalar(q_gain, q_gain, HD ** -0.5, None, ALU.mult))
                for t in range(NT):
                    def both(x):
                        n = x.shape[-1]
                        return x.rearrange("p (o d) -> p o d", o=1).broadcast_to([P, 2, n])
                    nc.gpsimd.tensor_tensor(rope_t[:, 0, t], both(rope_cs[:, 0, t]), rope_g, ALU.mult)
                    for a, b in ((0, 32), (32, 0)):
                        ins = nc.gpsimd.tensor_tensor(rope_t[:, 1, t, :, a:a + 32], both(rope_cs[:, 1, t, a:a + 32]), rope_g[:, :, b:b + 32], ALU.mult)
                link(ins)
                pool.sem_inc(rope_ready, 1)

            def rotate(kind, g):
                k.norms += 1
                x, heads, tabs = normed(kind, g)
                pool.wait_ge(xn_ready, k.norms)
                for t in range(NT):
                    src, dst = by_table(x[:, t], tabs), by_table(e_sb[:, t, 0:heads * HD], tabs)
                    for a, b in ((0, 32), (32, 0)):
                        ins = nc.gpsimd.tensor_tensor(dst[:, :, :, a:a + 32], src[:, :, :, b:b + 32],
                                                      for_heads(rope_t[:, 1, t, tabs, a:a + 32], heads // (tabs.stop - tabs.start)), ALU.mult)
                ins.then_inc(rot_ready, 1)

            k = Walk()

            def start_sums(b):
                if b >= 2:
                    l, j = (b - 2) // 3, (b - 2) % 3
                    pool.wait_ge(sums_done, mods(l, ("c0", "c1", "r2")[j]))
                l, j = b // 3, b % 3
                nc.gpsimd.memset(acc[:, b % 2], 0.0).then_inc(acc_zero, 1)
                pool.wait_ge(acc_zero, b + 1)
                bias = w["ada_b"][l:l + 1] if l < LAT else w["b_ada_2"]
                nc.gpsimd.dma_start(acc[0:1, b % 2], bias[:, 2 * D * j:2 * D * j + 2 * D]).then_inc(bias_in[b % 2], 16)

            blocks = iter(range(3 * (DEPTH + 1)))
            for _ in range(3):
                start_sums(next(blocks))
            f = 0
            for l in range(DEPTH):
                kind, _, _ = mixer(l)
                if kind != "sb":
                    tables(kind)
                    for n in sorted(SLOTS[kind]):
                        for step, g in SLOTS[kind][n]:
                            if step == "N":
                                rotate(kind, g)
                f += KT // 2 + 4
                if l == DEPTH - 1:
                    pool.wait_ge(split_lo, f)
                    nc.gpsimd.memset(acc_c, 0.0).then_inc(accc_zero, 1)
                    pool.wait_ge(accc_zero, 1)
                    nc.gpsimd.dma_start(acc_c[0:1, :], w["b_ada_2"][:, 0:2 * D]).then_inc(biasc_in, 16)
                for _ in range(5 if l == 0 else 3):
                    b = next(blocks, None)
                    if b is not None:
                        start_sums(b)
                f += KT // 2 + FF // 256

            pool.wait_ge(masks_in, 16)
            pool.wait_ge(sums_done, mods(LAT, "r2"))
            nc.gpsimd.tensor_copy(masks_2, mask_st).then_inc(masks_ready, 1)
            pool.wait_ge(lat_in, 128)
            q_gain = rope_g[:, 0]
            link(nc.gpsimd.tensor_scalar(q_gain, q_gain, HD ** -0.5, None, ALU.mult))
            for t in range(NT):
                nc.gpsimd.tensor_tensor(rope_t[:, 0, t], over_heads(rope_cs[:, 0, t], 2), rope_g, ALU.mult)
                for q in range(2):
                    dst, sin, gain = halves32(rope_t[:, 1, t, q]), halves32(rope_cs[:, 1, t]), halves32(rope_g[:, q])
                    for a, b in ((0, 16), (16, 0)):
                        ins = nc.gpsimd.tensor_tensor(dst[:, :, a:a + 16], sin[:, :, a:a + 16], gain[:, :, b:b + 16], ALU.mult)
            link(ins)
            pool.sem_inc(rope2_ready, 1)
            for what in ("kx", "kc", "q"):
                k.norms += 1
                if what == "kc":
                    continue
                x, nh = lat_heads(what)
                pool.wait_ge(xn_ready, k.norms)
                for t in range(NT):
                    for blk in range(2):
                        o = 32 * blk
                        table = rope_t[:, 1, t, 0 if what == "q" else 1]
                        for a, b in ((0, 16), (16, 0)):
                            ins = nc.gpsimd.tensor_tensor(heads(lrot[:, t, 0:nh * HD])[:, :, o + a:o + a + 16], heads(x[:, t])[:, :, o + b:o + b + 16],
                                                          over_heads(table[:, o + a:o + a + 16], nh), ALU.mult)
                ins.then_inc(rot_ready, 1)
            pool.wait_ge(beg_ready, 1)
            pool.wait_ge(l2_ready, 3)
            pool.wait_ge(cb_ready, 5)
            nc.gpsimd.memset(state, 0.0).then_inc(state_zero, 1)
            pool.wait_ge(raw_free, HELD - 1)
            for rd in range(4):
                lat = rd >= 2
                for d in range(2):
                    t, st = delta_tile(rd, d)
                    kk, vv = (dk_x, dv_x) if lat else (dk_c, dv_c)
                    if rd:
                        pool.wait_ge(uv_done, 2 * rd)
                        pool.wait_ge(su_done, 2 * rd)
                    nc.gpsimd.tensor_tensor(heads(bek[:, d]), heads(kk[:, t]), over_elems(beG[:, d, st]), ALU.mult)
                    nc.gpsimd.tensor_tensor(heads(bv[:, d]), heads(vv[:, t]), over_elems(beta[:, st, d]), ALU.mult)
                    ins = nc.gpsimd.tensor_tensor(heads(k_tail[:, d]), heads(kk[:, t]), over_elems(e_tail[:, d, st]), ALU.mult)
                    if lat:
                        if rd == 3:
                            pool.wait_ge(qdT_done, 2)
                        ins = nc.gpsimd.tensor_tensor(heads(q_dec[:, d]), heads(dq_x[:, t]), over_elems(e_G[:, d, st]), ALU.mult)
                    ins.then_inc(prep_ready, 1)

        @block.scalar
        def _(act):
            k = Walk()

            def convert():
                if k.u == len(units):
                    return
                slot, count, (_, _, kts, n) = k.next_load(loads, "unit")
                u = k.u
                k.u += 1
                act.wait_ge(landed[slot], count)
                if u >= 2:
                    act.wait_ge(gemm_done, u - 1)
                nc.scalar.copy(w_hi[:, u % 2, 0:len(kts), 0:n], raw[:, slot].rearrange("p (k n) -> p k n", k=UNIT_K)[:, 0:len(kts), 0:n])\
                    .then_inc(hi_ready, 1)

            def modulation(l, piece):
                for i in range(1 if piece[0] == "c" else 2):
                    k.sums += 1
                    act.wait_ge(sums_done, k.sums)
                    bank = SUM_BANKS[l, piece][i]
                    if piece[0] == "r":
                        dst = gates[:, int(piece[1]) - 1, 512 * i:512 * i + 512]
                        nc.scalar.copy(dst, bank).then_inc(mod_out, 1)
                    else:
                        dst = mod[:, l % 2, mod_cols(l, piece)]
                        n = dst.shape[-1]
                        if l == LAT and piece == "c0":
                            nc.scalar.copy(mod[:, l % 2, 32:48], bank[:, 16:32])
                        nc.scalar.copy(dst, bank[:, 0:n]).then_inc(mod_out, 1)

            def split(dst_hi, emit_full):
                f = k.f
                k.f += 1
                if f >= 2:
                    act.wait_ge(split_lo, f - 1)
                emit_full(full[:, f % 2, 0:SEQ * dst_hi.shape[1]]).then_inc(split_full, 1)
                act.wait_ge(split_full, f + 1)
                nc.scalar.copy(dst_hi, full[:, f % 2, 0:SEQ * dst_hi.shape[1]].rearrange("p (a n) -> p a n", n=SEQ)).then_inc(split_hi, 1)

            def rsqrt(n):
                k.rms += 1
                act.wait_ge(v_ready, k.rms)
                nc.scalar.activation(rms_y[:, 0:n], rms_v[:, 0:n], ACT.Ln).then_inc(exp_ready, 1)
                n_exp[0] += 1
                act.wait_ge(exp_ready, n_exp[0])
                nc.scalar.activation(rms_y[:, 0:n], rms_y[:, 0:n], ACT.Exp, scale=-0.5).then_inc(y_ready, 1)

            def squares(half, x=x_res):
                sl = slice(512 * half, 512 * half + 512)
                for t in range(NT):
                    ins = nc.scalar.activation(n_st[:, t, sl], x[:, t, sl], ACT.Square, accum_out=ssq[:, t, half:half + 1])
                ins.then_inc(ss_ready, 1)

            def norm(l, which, gain, dst=h_hi, sums=None):
                m = k.m
                k.m += 1
                rsqrt(NT)
                for piece in sums or []:
                    modulation(l, piece)
                act.wait_ge(gsc_ready, m + 1)
                for q in range(KT // 2):
                    act.wait_ge(norm_T, 4 * m + q + 1)

                    def emit(dst):
                        for i in range(2):
                            c = 2 * q + i
                            ins = nc.scalar.activation(dst[:, i * SEQ:(i + 1) * SEQ], A[q][:, i * SEQ:(i + 1) * SEQ], ACT.Identity,
                                                       scale=gsc[:, l % 2, gain + c:gain + c + 1],
                                                       bias=mod[:, l % 2, which + c:which + c + 1])
                        return ins
                    split(dst[:, 2 * q:2 * q + 2], emit)

            n_exp = [0]

            def evac_panel(u_end, what, g):
                act.wait_ge(gemm_done, u_end)
                pn = k.panel("act")
                if what == "q" and g == 1:
                    act.wait_ge(kvT_done, k.swa + 1)
                for t in range(NT):
                    bank = G[2 * (pn % 2) + t]
                    if what == "kv":
                        nc.scalar.copy(qk_st[:, 1, t, 0:P], bank[:, 0:P])
                        ins = nc.scalar.copy(v_st[:, 0, t, 0:P], bank[:, P:2 * P])
                    else:
                        ins = nc.scalar.copy((v_st if what == "v" else qk_st)[:, g % 2, t], bank)
                ins.then_inc(free_act, 1)

            def step_softmax(step, g, kind):
                if step == "N":
                    act.wait_ge(free_act, k.free_act)
                    if k.norms:
                        act.wait_ge(qk_ready, k.norms)
                    k.norms += 1
                    x, heads, _ = normed(kind, g)
                    nc.scalar.activation(e_sb[:, 0:NT, 0:heads * HD], x, ACT.Square).then_inc(sq_ready, 1)
                    rsqrt(NT * heads)
                    return
                if g == "kv":
                    return
                n = k.group + g
                if step == "T":
                    act.wait_ge(qkT_done, 2 * n + (2 if kind == "swa" else 1))
                    nc.scalar.copy(qT, A[0].rearrange("p (a n) -> p a n", a=2)).then_inc(qT_ready, 1)
                elif step == "S":
                    act.wait_ge(max_ready, k.sm + g + 1)
                    for b in (2, 0, 1):
                        for h in ((0, 2, 1, 3), (0, 2), (1, 3))[(2, 0, 1).index(b)]:
                            par, i = h % 2, h // 2
                            c = (0 if b == 2 else 4) + 2 * par + i
                            if b == 2:
                                src = A[2 + par][:, i * P:i * P + P]
                                dst = z_sb[:, 2, par * SEQ + i * P:par * SEQ + i * P + P]
                            else:
                                src, dst = A[par][:, i * SEQ:i * SEQ + SEQ], z_sb[:, par, i * SEQ:i * SEQ + SEQ]
                            ins = nc.scalar.activation(dst, src, ACT.Exp, bias=n_max[:, c:c + 1], accum_out=p_sum[:, c:c + 1])
                        ins.then_inc(p_ready, 1)
                    if kind == "swa":
                        act.wait_ge(sink_ready, 4 * k.swa + g + 1)
                        nc.scalar.activation(sink_e, sink_e, ACT.Exp).then_inc(se_ready, 1)
                elif step == "C":
                    for o, b in enumerate((2, 0, 1)):
                        act.wait_ge(pT_done, 3 * (k.sm + g) + o + 1)
                        nc.scalar.copy(aT[:, b], A[b]).then_inc(aT_ready, 1)
                elif step == "V":
                    act.wait_ge(av_done, n + 1)
                    split(act_hi[:, 2 * g:2 * g + 2], lambda dst: nc.scalar.copy(dst, A[3]))

            def step_sb(step, g):
                n = k.group + g
                ns = k.sb + g
                if step == "T":
                    act.wait_ge(qkT_done, 2 * n + 1)
                    nc.scalar.activation(qT, A[0].rearrange("p (a n) -> p a n", a=2), ACT.Copy, scale=HD ** -0.5).then_inc(qT_ready, 1)
                elif step == "S":
                    for b in (2, 0, 1):
                        o = (2, 0, 1).index(b)
                        act.wait_ge(z_done, 3 * ns + o + 1)
                        if b == 2:
                            nc.scalar.copy(z_sb[:, 2, 0:SEQ], A[2][:, 0:SEQ])
                            nc.scalar.copy(z_sb[:, 2, SEQ:2 * SEQ], A[3][:, 0:SEQ]).then_inc(z_copied, 1)
                        else:
                            nc.scalar.copy(z_sb[:, b], A[b]).then_inc(z_copied, 1)
                    for b in (2, 0, 1):
                        o = (2, 0, 1).index(b)
                        act.wait_ge(nabs_ready, 3 * ns + o + 1)
                        nc.scalar.activation(e_sb[:, b], e_sb[:, b], ACT.Exp).then_inc(exp_ready, 1)
                        n_exp[0] += 1
                        act.wait_ge(exp_ready, n_exp[0])
                        nc.scalar.activation(e_sb[:, b], e_sb[:, b], ACT.Ln, bias=1.0).then_inc(ln_ready, 1)
                elif step == "C":
                    for b in (2, 0, 1):
                        o = (2, 0, 1).index(b)
                        act.wait_ge(d_ready, 3 * ns + o + 1)
                        nc.scalar.activation(aT[:, b], aT[:, b], ACT.Exp).then_inc(aT_ready, 1)
                elif step == "V":
                    act.wait_ge(av_done, n + 1)
                    split(act_hi[:, 2 * g:2 * g + 2], lambda dst: nc.scalar.copy(dst, A[3]))

            act.wait_ge(cols_T, 1)
            nc.scalar.copy(cols, A[0][:, 0:NCOL + 36]).then_inc(cols_ready, 1)
            act.wait_ge(cols_ready, 1)
            nc.scalar.activation(c_col, cols[:, 64:88], ACT.Silu).then_inc(c_ready, 1)
            convert()
            convert()
            modulation(0, "c0")
            nc.scalar.preload_act_table_set("natural_log_exp_and_others")
            act.wait_ge(x_in, 16)
            squares(0)
            for l in range(DEPTH):
                kind, _, _ = mixer(l)
                if l:
                    act.wait_ge(x_ready, 4 * l)
                squares(1)
                norm(l, 0, 0, sums=["c2", "r2"] if l else None)
                panels = qkv_panels(kind)
                u0 = k.u - 2
                nq = 2 * len(panels)
                for n in range(nq + 4):
                    if n % 2 == 0 and 0 < n <= nq:
                        what, g, _ = panels[n // 2 - 1]
                        evac_panel(u0 + n, what, g)
                    if n:
                        convert()
                    if n == nq + 3:
                        act.wait_ge(x_ready, 4 * l + 1)
                        squares(0)
                        convert()
                    for step, g in SLOTS[kind].get(n, []):
                        (step_sb(step, g) if kind == "sb" else step_softmax(step, g, kind))
                    if l == 0 and n == nq + 1:
                        modulation(0, "r1")
                        modulation(0, "c1")
                k.panel("dve")
                k.panel("dve")
                k.end_mixer(kind)
                act.wait_ge(x_ready, 4 * l + 2)
                squares(1)
                norm(l, 16, 8, sums=None if l else ["c2", "r2"])
                nc.scalar.preload_act_table(ACT.Silu)
                uf = k.u - 2

                def silu(p):
                    act.wait_ge(gemm_done, uf + 2 * p + 2)
                    pn = k.panel("dve")
                    if p >= 1:
                        act.wait_ge(act_ready, (FF // 256) * l + p)
                    for t in range(NT):
                        ins = nc.scalar.activation(silu_st[:, t], G[2 * (pn % 2) + t][:, 0:256], ACT.Silu)
                    ins.then_inc(silu_ready, 1)

                def split_act(p):
                    act.wait_ge(actT_done, (FF // 256) * l + p + 1)
                    split(act_hi[:, 2 * p:2 * p + 2], lambda dst: nc.scalar.copy(dst, A[p % 2]))

                for p in range(FF // 256):
                    convert()
                    if p >= 1:
                        silu(p - 1)
                        convert()
                        split_act(p - 1)
                    if (l, ("up", p - 1)) in SUMS:
                        modulation(l + 1, SUMS[l, ("up", p - 1)])
                for j in range(12):
                    convert()
                    if j == 0:
                        silu(FF // 256 - 1)
                        nc.scalar.preload_act_table_set("natural_log_exp_and_others")
                        convert()
                        split_act(FF // 256 - 1)
                        if (l, ("up", FF // 256 - 1)) in SUMS:
                            modulation(l + 1, SUMS[l, ("up", FF // 256 - 1)])
                    if (l, ("down", j - 1)) in SUMS:
                        modulation(l + 1, SUMS[l, ("down", j - 1)])
                    if j == 9:
                        act.wait_ge(x_ready, 4 * l + 3)
                        squares(0)
                k.panel("dve")
                k.panel("dve")

            act.wait_ge(x_ready, 4 * LAT)
            squares(1)
            norm(LAT, 0, 0, sums=["c2", "r2"])
            act.wait_ge(ctx_in, 16)
            squares(0, ctx_raw)
            squares(1, ctx_raw)
            norm(LAT, 32, 16, act_hi)
            u0 = k.u - 2

            def square(x, n, dst):
                k.norms += 1
                nc.scalar.activation(dst, x, ACT.Square).then_inc(sq_ready, 1)
                rsqrt(n)

            dsts = {"kv": (kva_x, kva_c), "dk": (dk_x, dk_c), "dv": (dv_x, dv_c), "dab": (dab[:, 2:4], dab[:, 0:2]),
                    "q": (aq,), "dq": (dq_x,), "dz": (dz,)}
            dsts |= {f"gate{n}": (sig[:, n // 2, :, 512 * (n % 2):512 * (n % 2) + 512],) for n in range(4)}

            def lat_evac(pi):
                what, _, n, _ = LAT_PANELS[pi]
                act.wait_ge(gemm_done, u0 + 2 * pi + 2)
                if what == "dk":
                    act.wait_ge(masks_ready, 1)
                for dst in dsts[what]:
                    pn = k.panel("act")
                    for t in range(NT):
                        ins = nc.scalar.copy(dst[:, t], G[2 * (pn % 2) + t][:, 0:n])
                    ins.then_inc(free_act, 1)

            def lat_step(step, s):
                if step == "N":
                    act.wait_ge(free_act, k.free_act)
                    act.wait_ge(qk_ready, k.norms)
                    x, nh = lat_heads(s)
                    square(x, NT * nh, lrot[:, :, 0:nh * HD])
                elif step == "T":
                    act.wait_ge(ltT_done, 1)
                    nc.scalar.copy(lkT[:, 0], A[0]).then_inc(kq_act, 1)
                    act.wait_ge(ltT_done, 3)
                    nc.scalar.copy(lqT[:, 0:2].rearrange("p a n -> p (a n)"), A[2]).then_inc(kq_act, 1)
                elif step == "S":
                    act.wait_ge(wmax_ready, s + 1)
                    for b in range(4):
                        ins = nc.scalar.activation(p_sb[:, b], A[b], ACT.Exp, bias=n_max[:, b:b + 1], accum_out=p_sum[:, b:b + 1])
                    ins.then_inc(wp_ready, 1)
                    nc.scalar.activation(sink_e[:, 0:4], sink_e[:, 0:4], ACT.Exp).then_inc(wse_ready, 1)
                elif step == "P":
                    for b in (0, 2):
                        act.wait_ge(wpT_done, 4 * s + b + 1)
                        nc.scalar.copy(laT[:, b], A[b]).then_inc(waT_act, 1)
                elif step == "V":
                    act.wait_ge(woT_done, s + 1)
                    split(act_hi[:, Y_ATTN[s]:Y_ATTN[s] + 1], lambda dst: nc.scalar.copy(dst, A[0][:, 0:SEQ]))
                elif step == "X":
                    if s == 0:
                        nc.scalar.preload_act_table(ACT.Silu)
                        act.wait_ge(free_act, k.free_act)
                        nc.scalar.activation(dz, dz, ACT.Silu).then_inc(dz_ready, 1)
                    act.wait_ge(conv_ready, s + 1)
                    nc.scalar.activation(conv_t[:, s % 2], conv_t[:, s % 2], ACT.Silu).then_inc(cs_ready, 1)
                elif step == "Y":
                    act.wait_ge(cvB_done, s + 1)
                    for t in range(NT):
                        ins = nc.scalar.copy(CONV[s][0][:, t], A[2 * (s % 2) + t])
                    ins.then_inc(cb_ready, 1)
                elif step == "L":
                    nc.scalar.preload_act_table_set("natural_log_exp_and_others")
                    act.wait_ge(gz_ready, 1)
                    nc.scalar.activation(gate_s, gate_s, ACT.Exp).then_inc(ge_ready, 1)
                    act.wait_ge(ge_ready, 1)
                    nc.scalar.activation(gate_s, gate_s, ACT.Ln, bias=1.0).then_inc(gl_ready, 1)
                    act.wait_ge(lat_in, 128)
                    nc.scalar.activation(alog_row, alog_row, ACT.Exp).then_inc(ea_ready, 1)
                    for i, x in enumerate((dk_c, dk_x, dq_x)):
                        act.wait_ge(cb_ready, (1, 3, 5)[i])
                        if i == 2:
                            act.wait_ge(l2s_ready, 1)
                        nc.scalar.activation(sq_t[i % 2], x, ACT.Square).then_inc(l2q_ready, 1)
                    act.wait_ge(gates_ready, 1)
                    nc.scalar.activation(beta, lnb_all.rearrange("p s (d h) -> p s d h", d=2), ACT.Exp).then_inc(beta_ready, 1)
                    rsqrt(48)
                    act.wait_ge(gsum_done, 1)
                    nc.scalar.activation(neg_G.rearrange("p d s h -> p (d s h)"), A[0][:, 0:64], ACT.Copy, scale=-1.0)
                    nc.scalar.activation(e_G.rearrange("p d s h -> p (d s h)"), A[0][:, 0:64], ACT.Exp)
                    nc.scalar.activation(e_tail.rearrange("p d s h -> p (d s h)"), A[0][:, 64:128], ACT.Exp)
                    nc.scalar.activation(e_last.rearrange("p c h -> p (c h)"), A[1][:, 0:64], ACT.Exp).then_inc(eg_ready, 1)
                elif step == "W":
                    for i, dst in enumerate((kT_c, kT_x, qT_x)):
                        act.wait_ge(dT_done, 2 * i + 1)
                        nc.scalar.copy(dst[:, 0:2].rearrange("p a n -> p (a n)"), KQ_BANKS[i][0]).then_inc(dT_act, 1)

            for n in range(LAT_UNITS):
                if n and n % 2 == 0:
                    lat_evac(n // 2 - 1)
                if n:
                    convert()
                for step, s in LAT_SLOTS.get(n, []):
                    lat_step(step, s)
            lat_evac(len(LAT_PANELS) - 1)
            convert()
            act.wait_ge(eg_ready, 1)
            for rd in range(4):
                lat = rd >= 2
                for c in range(4):
                    d, r = c // 2, c % 2
                    t, st = delta_tile(rd, d)
                    act.wait_ge(e_done, 4 * rd + c + 1)
                    for i in range(4):
                        h = 2 * i + r
                        ins = nc.scalar.activation(LT[:, c, i * P:i * P + P], A[c][:, i * P:i * P + P], ACT.Exp, bias=neg_G[:, d, st, h:h + 1])
                    ins.then_inc(E_ready, 1)
                if lat:
                    for c in range(4):
                        d, r = c // 2, c % 2
                        t, st = delta_tile(rd, d)
                        act.wait_ge(in_done, 4 * (rd - 2) + c + 1)
                        for i in range(4):
                            h = 2 * i + r
                            ins = nc.scalar.activation(intraT[:, d, r, i * P:i * P + P], A[c][:, i * P:i * P + P], ACT.Exp, bias=neg_G[:, d, st, h:h + 1])
                        ins.then_inc(ie_ready, 1)
                for lev in range(1, LEVELS - 1):
                    for c in range(4):
                        act.wait_ge(x_done, joined(rd, lev, c, LEVELS - 1))
                        nc.scalar.copy(X[:, c], A[c]).then_inc(X_ready, 1)
                act.wait_ge(wT_done, rd + 1)
                for r in range(2):
                    ins = nc.scalar.copy(wT[:, r], A[r])
                ins.then_inc(wT_ready, 1)
                for d in range(2):
                    act.wait_ge(uv_done, 2 * rd + d + 1)
                    for c in range(2):
                        step = c if d == 0 else 1 - c
                        ins = nc.scalar.copy(u_st[CH * c:CH * c + CH, step], A[2 + d][CH * c:CH * c + CH])
                    ins.then_inc(uv_ready, 1)
                if lat:
                    for r in range(2):
                        act.wait_ge(qdT_done, 2 * (rd - 2) + r + 1)
                        nc.scalar.copy(q_decT[:, r], G[r]).then_inc(qdT_ready, 1)
            nc.scalar.preload_act_table(ACT.Sigmoid)
            nc.scalar.activation(sig, sig, ACT.Sigmoid).then_inc(sig_ready, 1)
            nc.scalar.preload_act_table_set("natural_log_exp_and_others")
            act.wait_ge(oacc_ready, 2)
            square(o_dn, 16, sq_t[0])
            for q in range(2):
                act.wait_ge(ydT_done, q + 1)
                split(act_hi[:, 4 + 2 * q:6 + 2 * q], lambda dst: nc.scalar.copy(dst, A[q]))
            for n in range(4):
                convert()
                k.panel("dve")
            for q in range(4):
                act.wait_ge(yT_done, q + 1)
                split(h_hi[:, 2 * q:2 * q + 2], lambda dst: nc.scalar.copy(dst, A[q]))
            for _ in range(3):
                convert()
            act.wait_ge(x_ready, 4 * LAT + 1)
            squares(0)
            convert()
            k.panel("dve")
            k.panel("dve")
            act.wait_ge(x_ready, 4 * LAT + 2)
            squares(1)
            norm(LAT, 16, 8)
            um = k.u - 2

            def relu(p, u_end):
                act.wait_ge(gemm_done, u_end)
                pn = k.panel("dve")
                if p >= 1:
                    act.wait_ge(hid_ready, p)
                if p == 4:
                    act.wait_ge(x_ready, 4 * LAT + 4)
                for t in range(NT):
                    ins = nc.scalar.activation(relu_st[:, t], G[2 * (pn % 2) + t], ACT.Relu)
                ins.then_inc(relu_ready, 1)

            def split_hidden(p):
                for q in range(2):
                    act.wait_ge(hidT_done, 2 * p + q + 1)
                    kt = 4 * (p % 4) + 2 * q
                    split(act_hi[:, kt:kt + 2], lambda dst: nc.scalar.copy(dst, A[2 * (p % 2) + q]))

            for part in range(2):
                for p in range(4):
                    hp = 4 * part + p
                    if p >= 1:
                        relu(hp - 1, um + 16 * part + 2 * p)
                    convert()
                    if p >= 1:
                        split_hidden(hp - 1)
                    convert()
                for j in range(8):
                    if j == 0:
                        relu(4 * part + 3, um + 16 * part + 8)
                    convert()
                    if j == 0:
                        split_hidden(4 * part + 3)
                k.panel("dve")
                k.panel("dve")

        @block.vector
        def _(dve):
            k = Walk()
            chain = [0]

            def link(ins):
                chain[0] += 1
                ins.then_inc(dve_step, 1)
                dve.wait_ge(dve_step, chain[0])

            def convert():
                if k.u == len(units):
                    return
                slot, _, (_, _, kts, n) = k.next_load(loads, "unit")
                u = k.u
                k.u += 1
                dve.wait_ge(hi_ready, u + 1)
                if u >= 2:
                    dve.wait_ge(gemm_done, u - 1)
                nc.vector.tensor_tensor(w_lo[:, u % 2, 0:len(kts), 0:n], raw[:, slot].rearrange("p (k n) -> p k n", k=UNIT_K)[:, 0:len(kts), 0:n],
                                        w_hi[:, u % 2, 0:len(kts), 0:n].bitcast(F32), ALU.subtract).then_inc(lo_ready, 1)
                dve.wait_ge(lo_ready, u + 1)
                dve.sem_inc(raw_free, 1)

            def modulation_units():
                while k.s < len(loads) and loads[k.s][0] == "ada":
                    slot, count, (_, l, n) = k.next_load(loads, "ada")
                    b = 3 * l + n // KT
                    dve.wait_ge(landed[slot], count)
                    if n % KT == 0:
                        dve.wait_ge(bias_in[b % 2], 16 * (b // 2 + 1))
                    else:
                        dve.wait_ge(acc_done, k.a)
                    c = (KT if l == LAT else 0) + n % KT
                    nc.vector.scalar_tensor_tensor(out=acc[:, b % 2], in0=raw[:, slot], scalar=c_col[:, c:c + 1], in1=acc[:, b % 2],
                                                   op0=ALU.mult, op1=ALU.add).then_inc(acc_done, 1)
                    k.a += 1
                    if l == LAT and n < KT:
                        if n == 0:
                            dve.wait_ge(biasc_in, 16)
                        else:
                            dve.wait_ge(accc_done, n)
                        nc.vector.scalar_tensor_tensor(out=acc_c, in0=raw[:, slot], scalar=c_col[:, 2 * KT + n:2 * KT + n + 1], in1=acc_c,
                                                       op0=ALU.mult, op1=ALU.add).then_inc(accc_done, 1)
                        dve.wait_ge(accc_done, n + 1)
                    dve.wait_ge(acc_done, k.a)
                    dve.sem_inc(raw_free, 1)

            def split(dst_lo, dst_hi):
                f = k.f
                k.f += 1
                dve.wait_ge(split_hi, f + 1)
                nc.vector.tensor_tensor(dst_lo, full[:, f % 2, 0:SEQ * dst_lo.shape[1]].rearrange("p (a n) -> p a n", n=SEQ), dst_hi.bitcast(F32),
                                        ALU.subtract).then_inc(split_lo, 1)

            def rsqrt(ss, n, width, eps=EPS):
                k.rms += 1
                v, y, t = rms_v[:, 0:n], rms_y[:, 0:n], rms_t[:, 0:n]
                nc.vector.tensor_scalar(v, ss, 1.0 / width, eps, ALU.mult, ALU.add).then_inc(v_ready, 1)
                dve.wait_ge(y_ready, k.rms)
                link(nc.vector.tensor_tensor(t, y, y, ALU.mult))
                link(nc.vector.tensor_tensor(t, t, v, ALU.mult))
                link(nc.vector.tensor_scalar(t, t, -0.5, 1.5, ALU.mult, ALU.add))
                link(nc.vector.tensor_tensor(y, y, t, ALU.mult))

            def gains(l, which, scale, col):
                return nc.vector.scalar_tensor_tensor(out=gsc[:, l % 2, which:which + 8], in0=mod[:, l % 2, scale:scale + 8], scalar=1.0,
                                                      in1=cols[:, col:col + 8], op0=ALU.add, op1=ALU.mult)

            def norm(x=x_res, lo=h_lo, hi=h_hi, late=lambda: None, between=lambda: None):
                m = k.m
                k.m += 1
                dve.wait_ge(ss_ready, 2 * m + 2)
                link(nc.vector.tensor_tensor(ssum, ssq[:, :, 0], ssq[:, :, 1], ALU.add))
                rsqrt(ssum, NT, D)
                for t in range(NT):
                    nc.vector.tensor_scalar(n_st[:, t], x[:, t], rms_y[:, t:t + 1], None, ALU.mult).then_inc(n_ready, 1)
                late()
                between()
                for q in range(KT // 2):
                    split(lo[:, 2 * q:2 * q + 2], hi[:, 2 * q:2 * q + 2])

            def residual(u_end, n, gate, l):
                dve.wait_ge(gemm_done, u_end)
                dve.wait_ge(mod_out, mods(l, ("r1", "r2")[gate]))
                pn = k.panel("dve")
                sl = slice(512 * n, 512 * n + 512)
                for t in range(NT):
                    ins = nc.vector.tensor_tensor(n_st[:, t, sl], G[2 * (pn % 2) + t], gates[:, gate, sl], ALU.mult)
                ins.then_inc(free_dve, 1)
                dve.wait_ge(free_dve, k.free_dve)
                for t in range(NT):
                    ins = nc.vector.tensor_tensor(x_res[:, t, sl], x_res[:, t, sl], n_st[:, t, sl], ALU.add)
                ins.then_inc(x_ready, 1)

            def step_sb(step, g):
                n = k.group + g
                ns = k.sb + g
                if step == "T":
                    dve.wait_ge(qkT_done, 2 * n + 2)
                    nc.vector.tensor_copy(kT, A[1].rearrange("p (a n) -> p a n", a=2)).then_inc(kT_ready, 1)
                elif step == "S":
                    for o, b in enumerate((2, 0, 1)):
                        dve.wait_ge(z_copied, 3 * ns + o + 1)
                        nc.vector.scalar_tensor_tensor(out=e_sb[:, b], in0=z_sb[:, b], scalar=-1.0, in1=z_sb[:, b],
                                                       op0=ALU.mult, op1=ALU.min).then_inc(nabs_ready, 1)
                    for o, b in enumerate((2, 0, 1)):
                        dve.wait_ge(ln_ready, 3 * ns + o + 1)
                        nc.vector.scalar_tensor_tensor(out=e_sb[:, b], in0=z_sb[:, b], scalar=0.0, in1=e_sb[:, b],
                                                       op0=ALU.max, op1=ALU.add).then_inc(sp_ready, 1)
                elif step == "C":
                    for o, b in enumerate((2, 0, 1)):
                        dve.wait_ge(r_done, 3 * ns + o + 1)
                        nc.vector.tensor_tensor(aT[:, b], z_sb[:, b], A[b], ALU.subtract).then_inc(d_ready, 1)
                elif step == "V":
                    split(act_lo[:, 2 * g:2 * g + 2], act_hi[:, 2 * g:2 * g + 2])

            def step_softmax(step, g, kind):
                n = k.group + g if g != "kv" else 0
                if step == "N":
                    k.norms += 1
                    x, heads, tables = normed(kind, g)
                    per_table = heads // (tables.stop - tables.start)
                    dve.wait_ge(sq_ready, k.norms)
                    link(nc.vector.tensor_reduce(ss16[:, 0:NT * heads].rearrange("p (t h) -> p t h", t=NT),
                                                 e_sb[:, 0:NT, 0:heads * HD].rearrange("p t (h d) -> p t h d", d=HD), AX.X, ALU.add))
                    rsqrt(ss16[:, 0:NT * heads], NT * heads, HD)
                    for t in range(NT):
                        xt = x[:, t].rearrange("p (h d) -> p h d", d=HD)
                        r = rms_y[:, t * heads:(t + 1) * heads].rearrange("p (h o) -> p h o", o=1).broadcast_to([P, heads, HD])
                        ins = nc.vector.tensor_tensor(xt, xt, r, ALU.mult)
                    ins.then_inc(xn_ready, 1)
                    dve.wait_ge(xn_ready, k.norms)
                    dve.wait_ge(rope_ready, rope_layers(kind))
                    for t in range(NT):
                        ins = nc.vector.tensor_tensor(by_table(rope_st[:, t, 0:heads * HD], tables), by_table(x[:, t], tables),
                                                      for_heads(rope_t[:, 0, t, tables], per_table), ALU.mult)
                    link(ins)
                    dve.wait_ge(rot_ready, k.norms)
                    for t in range(NT):
                        c, r = rope_st[:, t, 0:heads * HD], e_sb[:, t, 0:heads * HD]
                        if g == "kv":
                            dst = qk_st[:, 1, t, 256:512].rearrange("p (h o d) -> p h o d", h=2, o=2)
                            c, r = (for_heads(y.rearrange("p (h d) -> p h d", d=HD), 2) for y in (c, r))
                        else:
                            dst = x[:, t]
                        ins = nc.vector.tensor_tensor(dst, c, r, ALU.add)
                    ins.then_inc(qk_ready, 1)
                elif step == "T":
                    if g == "kv":
                        dve.wait_ge(kvT_done, k.swa + 1)
                        nc.vector.tensor_copy(kT, A[1].rearrange("p (a n) -> p a n", a=2)).then_inc(kvT_ready, 1)
                    elif kind == "moba":
                        dve.wait_ge(qkT_done, 2 * n + 2)
                        nc.vector.tensor_copy(kT, A[1].rearrange("p (a n) -> p a n", a=2)).then_inc(kT_ready, 1)
                elif step == "S":
                    for t in range(NT):
                        dve.wait_ge(s_done, 2 * (k.sm + g) + t + 1)
                        for par in range(2):
                            nk = P * (t + 1)
                            ins = nc.vector.tensor_reduce(n_max[:, 4 * t + 2 * par:4 * t + 2 * par + 2],
                                                          A[2 - 2 * t + par][:, 0:2 * nk].rearrange("p (i n) -> p i n", i=2),
                                                          AX.X, ALU.max, negate=True)
                    if kind == "swa":
                        link(ins)
                        by_head = sinks[:, 4 * g:4 * g + 4].rearrange("p (i r) -> p r i", i=2)
                        for t in range(NT):
                            m = n_max[:, 4 * t:4 * t + 4].rearrange("p (r i) -> p r i", r=2)
                            ins = nc.vector.scalar_tensor_tensor(out=m, in0=by_head, scalar=-1.0, in1=m, op0=ALU.mult, op1=ALU.min)
                        link(ins)
                        for t in range(NT):
                            m = n_max[:, 4 * t:4 * t + 4].rearrange("p (r i) -> p r i", r=2)
                            ins = nc.vector.tensor_tensor(sink_e[:, 4 * t:4 * t + 4].rearrange("p (r i) -> p r i", r=2), by_head, m, ALU.add)
                        ins.then_inc(sink_ready, 1)
                        dve.wait_ge(sink_ready, 4 * k.swa + g + 1)
                        dve.sem_inc(max_ready, 1)
                    else:
                        ins.then_inc(max_ready, 1)
                elif step == "C":
                    dve.wait_ge(p_ready, 3 * (k.sm + g) + 3)
                    if kind == "swa":
                        dve.wait_ge(se_ready, 4 * k.swa + g + 1)
                        link(nc.vector.tensor_tensor(p_inv, p_sum, sink_e, ALU.add))
                        link(nc.vector.reciprocal(p_inv, p_inv))
                    else:
                        link(nc.vector.reciprocal(p_inv, p_sum))
                    for b in (2, 0, 1):
                        if b == 2:
                            p, r = z_sb[:, 2].rearrange("p (c n) -> p c n", c=4), p_inv[:, 0:4]
                        else:
                            p, r = z_sb[:, b].rearrange("p (c n) -> p c n", c=2), p_inv[:, 4 + 2 * b:6 + 2 * b]
                        nc.vector.tensor_tensor(p, p, over_elems(r, p.shape[-1]), ALU.mult).then_inc(pn_ready, 1)
                elif step == "V":
                    split(act_lo[:, 2 * g:2 * g + 2], act_hi[:, 2 * g:2 * g + 2])

            dve.wait_ge(const_in, 48)
            nc.vector.tensor_copy(ident_b, ident).then_inc(cast_ready, 1)
            nc.vector.tensor_copy(masks_b, consts[:, 3:6]).then_inc(cast_ready, 1)
            dve.wait_ge(c_ready, 1)
            modulation_units()
            convert()
            for l in range(DEPTH):
                kind, _, _ = mixer(l)
                c_gain = 16 * l

                def gains1():
                    dve.wait_ge(mod_out, mods(l, "c0"))
                    gains(l, 0, 8, c_gain).then_inc(gsc_ready, 1)

                def gains2():
                    dve.wait_ge(mod_out, mods(l, "c2"))
                    gains(l, 8, 24, c_gain + 8).then_inc(gsc_ready, 1)

                norm(late=gains1, between=convert)
                panels = qkv_panels(kind)
                u0 = k.u - 2
                nq = 2 * len(panels)
                for n in range(nq + 4):
                    if n % 2 == 0 and 0 < n <= nq:
                        k.panel("act")
                    if n:
                        convert()
                    if n == nq + 3:
                        residual(u0 + nq + 3, 0, 0, l)
                        residual(u0 + nq + 4, 1, 0, l)
                    else:
                        modulation_units()
                    for step, g in SLOTS[kind].get(n, []):
                        (step_sb(step, g) if kind == "sb" else step_softmax(step, g, kind))
                k.end_mixer(kind)
                norm(late=gains2, between=convert)

                def act_mul(p):
                    dve.wait_ge(silu_ready, (FF // 256) * l + p + 1)
                    pn = k.panel("dve")
                    if p >= 1:
                        dve.wait_ge(actT_done, (FF // 256) * l + p)
                    for t in range(NT):
                        ins = nc.vector.tensor_tensor(act_st[:, t], G[2 * (pn % 2) + t][:, 256:512], silu_st[:, t], ALU.mult)
                    ins.then_inc(act_ready, 1)
                    dve.wait_ge(act_ready, (FF // 256) * l + p + 1)
                    dve.sem_inc(free_dve, 1)

                for p in range(FF // 256):
                    convert()
                    if p >= 1:
                        act_mul(p - 1)
                        convert()
                        split(act_lo[:, 2 * p - 2:2 * p], act_hi[:, 2 * p - 2:2 * p])
                    modulation_units()
                p = FF // 256
                ud = k.u - 1
                for j in range(12):
                    if j < 11:
                        convert()
                        if j == 0:
                            act_mul(p - 1)
                            convert()
                            split(act_lo[:, 2 * p - 2:2 * p], act_hi[:, 2 * p - 2:2 * p])
                        modulation_units()
                    else:
                        residual(ud + 12, 1, 1, l)
                    if j == 7:
                        residual(ud + 6, 0, 1, l)

            def gains_lat():
                dve.wait_ge(mod_out, mods(LAT, "c0"))
                gains(LAT, 16, 40, 88)
                gains(LAT, 0, 8, 88).then_inc(gsc_ready, 1)

            def gains_ctx():
                dve.sem_inc(gsc_ready, 1)

            norm(late=gains_lat, between=convert)
            norm(ctx_raw, act_lo, act_hi, late=gains_ctx)
            u0 = k.u - 2

            def head_norm(step):
                k.norms += 1
                x, nh = lat_heads(step)
                dve.wait_ge(sq_ready, k.norms)
                link(nc.vector.tensor_reduce(ss16[:, 0:NT * nh].rearrange("p (t h) -> p t h", t=NT),
                                             lrot[:, :, 0:nh * HD].rearrange("p t (h d) -> p t h d", d=HD), AX.X, ALU.add))
                rsqrt(ss16[:, 0:NT * nh], NT * nh, HD)
                for t in range(NT):
                    ins = nc.vector.tensor_tensor(heads(x[:, t]), heads(x[:, t]), over_elems(rms_y[:, t * nh:(t + 1) * nh]), ALU.mult)
                ins.then_inc(xn_ready, 1)
                dve.wait_ge(xn_ready, k.norms)
                dve.wait_ge(rope2_ready, 1)

                def twice(y):
                    return y.rearrange("p (h o d) -> p h o d", h=2, o=1).broadcast_to([P, 2, 2, HD])

                def kdst(t):
                    return kdup[:, t].rearrange("p (h o d) -> p h o d", h=2, o=2)
                if step == "kc":
                    gain = rope_g[:, 1].rearrange("p (a b d) -> p a b d", a=1, b=1).broadcast_to([P, 2, 2, HD])
                    for t in range(NT):
                        ins = nc.vector.tensor_tensor(kdst(2 + t), twice(x[:, t]), gain, ALU.mult)
                else:
                    q = 0 if step == "q" else 1
                    for t in range(NT):
                        ins = nc.vector.tensor_tensor(heads(lrope_st[:, t, 0:nh * HD]), heads(x[:, t]), over_heads(rope_t[:, 0, t, q], nh), ALU.mult)
                    link(ins)
                    dve.wait_ge(rot_ready, k.norms - (1 if step == "q" else 0))
                    for t in range(NT):
                        c, r = lrope_st[:, t, 0:nh * HD], lrot[:, t, 0:nh * HD]
                        if step == "q":
                            ins = nc.vector.tensor_tensor(x[:, t], c, r, ALU.add)
                        else:
                            ins = nc.vector.tensor_tensor(kdst(t), twice(c), twice(r), ALU.add)
                ins.then_inc(qk_ready, 1)

            def delta_inputs():
                dve.wait_ge(free_act, k.free_act)
                dve.wait_ge(lat_in, 128)
                dtb = dtb_row.rearrange("p (o n) -> p o n", o=1).broadcast_to([P, 4, 16])
                nc.vector.tensor_tensor(gate_z[:, :, 0:16], dab[:, :, 0:16], dtb, ALU.add)
                link(nc.vector.tensor_scalar(gate_z[:, :, 16:32], dab[:, :, 16:32], -1.0, None, ALU.mult))
                nc.vector.scalar_tensor_tensor(out=gate_s, in0=gate_z, scalar=-1.0, in1=gate_z, op0=ALU.mult, op1=ALU.min).then_inc(gz_ready, 1)
                dve.wait_ge(gl_ready, 1)
                dve.wait_ge(ea_ready, 1)
                link(nc.vector.scalar_tensor_tensor(out=gate_s, in0=gate_z, scalar=0.0, in1=gate_s, op0=ALU.max, op1=ALU.add))
                ea = alog_row.rearrange("p (o n) -> p o n", o=1).broadcast_to([P, 4, 16])
                nc.vector.scalar_tensor_tensor(out=g_all, in0=gate_s[:, :, 0:16], scalar=-1.0, in1=ea, op0=ALU.mult, op1=ALU.mult)
                nc.vector.tensor_scalar(lnb_all, gate_s[:, :, 16:32], -1.0, None, ALU.mult).then_inc(gates_ready, 1)
                for i in range(3):
                    dve.wait_ge(l2q_ready, i + 1)
                    nc.vector.tensor_reduce(ss16[:, 16 * i:16 * i + 16].rearrange("p (t h) -> p t h", t=NT),
                                            sq_t[i % 2].rearrange("p t (h d) -> p t h d", d=HD), AX.X, ALU.add).then_inc(l2s_ready, 1)
                dve.wait_ge(l2s_ready, 3)
                link(nc.vector.tensor_scalar(ss16[:, 32:48], ss16[:, 32:48], EPS * (1.0 - 1.0 / HD), float(HD), ALU.add, ALU.mult))
                rsqrt(ss16, 48, 1.0)
                for i, x in enumerate((dk_c, dk_x, dq_x)):
                    for t in range(NT):
                        ins = nc.vector.tensor_tensor(heads(x[:, t]), heads(x[:, t]), over_elems(rms_y[:, 16 * i + 8 * t:16 * i + 8 * t + 8]), ALU.mult)
                    ins.then_inc(l2_ready, 1)
                dve.wait_ge(eg_ready, 1)
                dve.wait_ge(beta_ready, 1)
                for d in range(2):
                    nc.vector.tensor_tensor(lnb_G[:, d], lnb_all[:, :, DNH * d:DNH * d + DNH], neg_G[:, d], ALU.subtract)
                for d in range(2):
                    ins = nc.vector.tensor_tensor(beG[:, d], beta[:, :, d], e_G[:, d], ALU.mult)
                ins.then_inc(beg_ready, 1)

            def lat_step(step, s):
                if step == "N":
                    head_norm(s)
                elif step == "T":
                    dve.wait_ge(ltT_done, 2)
                    nc.vector.tensor_copy(lkT[:, 1], A[1]).then_inc(kq_dve, 1)
                    dve.wait_ge(ltT_done, 4)
                    nc.vector.tensor_copy(lqT[:, 2:4].rearrange("p a n -> p (a n)"), A[3]).then_inc(kq_dve, 1)
                elif step == "S":
                    for b in range(4):
                        dve.wait_ge(ws_done, 4 * s + b + 1)
                        ins = nc.vector.tensor_reduce(n_max[:, b:b + 1], A[b], AX.X, ALU.max, negate=True)
                    link(ins)
                    sink = sinks[:, 2 * s:2 * s + 2].rearrange("p (o r) -> p o r", o=1).broadcast_to([P, 2, 2])
                    mx = n_max[:, 0:4].rearrange("p (t r) -> p t r", t=2)
                    link(nc.vector.scalar_tensor_tensor(out=mx, in0=sink, scalar=-1.0, in1=mx, op0=ALU.mult, op1=ALU.min))
                    nc.vector.tensor_tensor(sink_e[:, 0:4].rearrange("p (t r) -> p t r", t=2), sink, mx, ALU.add).then_inc(wmax_ready, 1)
                    dve.wait_ge(wp_ready, s + 1)
                    dve.wait_ge(wse_ready, s + 1)
                    link(nc.vector.tensor_tensor(p_inv[:, 0:4], p_sum[:, 0:4], sink_e[:, 0:4], ALU.add))
                    link(nc.vector.reciprocal(p_inv[:, 0:4], p_inv[:, 0:4]))
                    for b in range(4):
                        ins = nc.vector.tensor_scalar(p_sb[:, b], p_sb[:, b], p_inv[:, b:b + 1], None, ALU.mult)
                    ins.then_inc(wn_ready, 1)
                elif step == "P":
                    for b in (1, 3):
                        dve.wait_ge(wpT_done, 4 * s + b + 1)
                        nc.vector.tensor_copy(laT[:, b], A[b]).then_inc(waT_dve, 1)
                elif step == "V":
                    split(act_lo[:, Y_ATTN[s]:Y_ATTN[s] + 1], act_hi[:, Y_ATTN[s]:Y_ATTN[s] + 1])
                elif step == "X":
                    dve.wait_ge(cvT_done, s + 1)
                    if s >= 2:
                        dve.wait_ge(cvB_done, s - 1)
                    for tap, (lo, hi) in ((1, (0, SEQ)), (0, (1, SEQ)), (2, (0, SEQ - 1))):
                        for a in range(4):
                            c = NCOL + 12 * tap + 4 * CONV[s][1] + a
                            src = A[2 * (s % 2) + a // 2][:, SEQ * (a % 2) + lo + tap - 1:SEQ * (a % 2) + hi + tap - 1]
                            y, col = conv_t[:, s % 2, a, lo:hi], cols[:, c:c + 1]
                            if tap == 1:
                                ins = nc.vector.tensor_scalar(y, src, col, None, ALU.mult)
                            else:
                                ins = nc.vector.scalar_tensor_tensor(out=y, in0=src, scalar=col, in1=y, op0=ALU.mult, op1=ALU.add)
                        if tap < 2:
                            link(ins)
                    ins.then_inc(conv_ready, 1)
                elif step == "L":
                    delta_inputs()
                elif step == "W":
                    for i, dst in enumerate((kT_c, kT_x, qT_x)):
                        dve.wait_ge(dT_done, 2 * i + 2)
                        nc.vector.tensor_copy(dst[:, 2:4].rearrange("p a n -> p (a n)"), KQ_BANKS[i][1]).then_inc(dT_dve, 1)

            for n in range(LAT_UNITS):
                if n and n % 2 == 0:
                    for _ in range(2 if LAT_PANELS[n // 2 - 1][3] else 1):
                        k.panel("act")
                if n:
                    convert()
                for step, s in LAT_SLOTS.get(n, []):
                    lat_step(step, s)
            k.panel("act")
            convert()

            def of_heads(x, n):
                return x.rearrange("p (i n) -> p i n", n=n)

            for rd in range(4):
                lat = rd >= 2
                for c in range(5):
                    if c < 4:
                        dve.wait_ge(E_ready, 4 * rd + c + 1)
                        dve.wait_ge(kk_done, 4 * rd + c + 1)
                        nc.vector.scalar_tensor_tensor(out=LT[:, c], in0=LT[:, c], scalar=-1.0, in1=G[c], op0=ALU.mult, op1=ALU.mult).then_inc(L_ready, 1)
                    if c:
                        dve.wait_ge(L_ready, 4 * rd + c)
                        x = of_heads(LT[:, c - 1], P)
                        eye = ident.rearrange("p (o n) -> p o n", o=1).broadcast_to([P, 4, P])
                        nc.vector.tensor_tensor(x, x, eye, ALU.add).then_inc(LT_ready, 1)
                if lat:
                    for c in range(4):
                        dve.wait_ge(ie_ready, 4 * (rd - 2) + c + 1)
                        dve.wait_ge(id_done, 4 * (rd - 2) + c + 1)
                        x = intraT[:, c // 2, c % 2]
                        nc.vector.tensor_tensor(x, x, G[c], ALU.mult).then_inc(intra_ready, 1)
                for c in range(4):
                    dve.wait_ge(LT_ready, 4 * rd + c + 1)
                    nc.vector.tensor_tensor(of_heads(XT[:, c], P), of_heads(LT[:, c], P), over_heads(level_mask[:, 1 - c // 2, 0], 4), ALU.mult)
                    dve.wait_ge(y_done, solved(rd, 0, c))
                    nc.vector.tensor_tensor(of_heads(X[:, c], P), of_heads(A[c], P), over_heads(level_mask[:, c // 2, 0], 4), ALU.mult).then_inc(Z_ready, 1)
                for lev in range(1, LEVELS):
                    for c in range(4):
                        dve.wait_ge(y_done, solved(rd, lev, c))
                        nc.vector.tensor_tensor(of_heads(Z[:, c], P), of_heads(A[c], P), over_heads(level_mask[:, c // 2, lev], 4), ALU.mult).then_inc(Z_ready, 1)
                    for c in range(4):
                        dve.wait_ge(xT_done, joined(rd, lev, c))
                        nc.vector.tensor_copy(XT[:, c], G[c]).then_inc(XT_ready, 1)
                for step in range(2):
                    c = 2 * rd + step
                    if c:
                        dve.wait_ge(S_ready, c)
                    else:
                        dve.wait_ge(state_zero, 1)
                    if c < 7:
                        for r in range(2):
                            decay = over_elems(e_last[:, c].rearrange("p (i r) -> p r i", r=2)[:, r])
                            ins = nc.vector.tensor_tensor(heads(state_t[:, 256 * r:256 * r + 256]), heads(state[:, 256 * r:256 * r + 256]), decay, ALU.mult)
                    dve.wait_ge(wS_done, c + 1)
                    dve.wait_ge(uv_ready, 2 * rd + 2)
                    nc.vector.tensor_tensor(u_st[:, step], u_st[:, step], A[0], ALU.subtract).then_inc(u_ready, 1)
                    if c < 7:
                        dve.wait_ge(u_ready, c + 1)
                        dve.wait_ge(su_done, c + 1)
                        nc.vector.tensor_tensor(state, state_t, A[3], ALU.add).then_inc(S_ready, 1)
                if lat:
                    dve.wait_ge(o_done, rd - 1)
                    for d in range(2):
                        t, _ = delta_tile(rd, d)
                        if rd == 2:
                            link(nc.vector.tensor_copy(o_dn[:, t], A[1 + d]))
                        else:
                            link(nc.vector.tensor_tensor(o_dn[:, t], o_dn[:, t], A[1 + d], ALU.add))
                        ins = nc.vector.tensor_tensor(o_dn[:, t], o_dn[:, t], G[d], ALU.add)
                    ins.then_inc(oacc_ready, 1)
            k.norms += 1
            dve.wait_ge(sq_ready, k.norms)
            link(nc.vector.tensor_reduce(ss16[:, 0:16].rearrange("p (t h) -> p t h", t=NT), sq_t[0].rearrange("p t (h d) -> p t h d", d=HD), AX.X, ALU.add))
            rsqrt(ss16[:, 0:16], 16, HD)
            for t in range(NT):
                ins = nc.vector.tensor_tensor(heads(o_dn[:, t]), heads(o_dn[:, t]), over_elems(rms_y[:, 8 * t:8 * t + 8]), ALU.mult)
            link(ins)
            for t in range(NT):
                ins = nc.vector.tensor_tensor(heads(o_dn[:, t]), heads(o_dn[:, t]), over_heads(dng_row, DNH), ALU.mult)
            link(ins)
            dve.wait_ge(dz_ready, 1)
            for t in range(NT):
                gate = dz[:, t].rearrange("p (i r d) -> p r i d", r=2, d=HD)
                ins = nc.vector.tensor_tensor(gate, gate, o_dn[:, t].rearrange("p (r i d) -> p r i d", r=2, d=HD), ALU.mult)
            ins.then_inc(yd_ready, 1)
            for q in range(2):
                split(act_lo[:, 4 + 2 * q:6 + 2 * q], act_hi[:, 4 + 2 * q:6 + 2 * q])
            um = u0 + LAT_UNITS
            dve.wait_ge(sig_ready, 1)
            for n in range(4):
                convert()
                dve.wait_ge(gemm_done, um + 1 + n)
                pn = k.panel("dve")
                sl = slice(512 * (n % 2), 512 * (n % 2) + 512)
                for t in range(NT):
                    ins = nc.vector.tensor_tensor(sig[:, n // 2, t, sl], sig[:, n // 2, t, sl], G[2 * (pn % 2) + t], ALU.mult)
                ins.then_inc(free_dve, 1)
                if n >= 2:
                    dve.wait_ge(free_dve, k.free_dve)
                    nc.vector.tensor_tensor(n_st[:, :, sl], sig[:, 0, :, sl], sig[:, 1, :, sl], ALU.add).then_inc(yy_ready, 1)
            for q in range(4):
                split(h_lo[:, 2 * q:2 * q + 2], h_hi[:, 2 * q:2 * q + 2])
            convert()
            convert()
            convert()
            residual(um + 7, 0, 0, LAT)
            residual(um + 8, 1, 0, LAT)

            def gains_lat2():
                dve.wait_ge(mod_out, mods(LAT, "c2"))
                gains(LAT, 8, 24, 96).then_inc(gsc_ready, 1)

            norm(late=gains_lat2, between=convert)
            um = k.u - 2

            def hidden(p):
                dve.wait_ge(relu_ready, p + 1)
                pn = k.panel("dve")
                if p >= 1:
                    dve.wait_ge(hidT_done, 2 * p)
                for t in range(NT):
                    ins = nc.vector.tensor_tensor(hid_st[:, t], G[2 * (pn % 2) + t], relu_st[:, t], ALU.mult)
                ins.then_inc(hid_ready, 1)
                dve.wait_ge(hid_ready, p + 1)
                dve.sem_inc(free_dve, 1)

            def split_hidden(p):
                for q in range(2):
                    kt = 4 * (p % 4) + 2 * q
                    split(act_lo[:, kt:kt + 2], act_hi[:, kt:kt + 2])

            for part in range(2):
                for p in range(4):
                    hp = 4 * part + p
                    if p >= 1:
                        hidden(hp - 1)
                    convert()
                    if p >= 1:
                        split_hidden(hp - 1)
                    convert()
                for j in range(8):
                    if j == 0:
                        hidden(4 * part + 3)
                    convert()
                    if j == 0:
                        split_hidden(4 * part + 3)
                    if j == 5:
                        residual(um + 16 * part + 12, 0, 1, LAT)
                residual(um + 16 * part + 16, 1, 1, LAT)

        @block.tensor
        def _(pe):
            k = Walk()

            def wait_panel_free(pn):
                if pn >= 2:
                    who, count = k.panel_free[pn - 2]
                    pe.wait_ge(free_act if who == "act" else free_dve, count)

            def unit(x_hi, x_lo, kts, banks, first, last, n=512, done=gemm_done):
                u = k.u
                k.u += 1
                pe.wait_ge(hi_ready, u + 1)
                pe.wait_ge(lo_ready, u + 1)
                for t in range(NT):
                    ts = slice(t * P, t * P + P)
                    for i, kt in enumerate(kts):
                        st = first and i == 0
                        en = last and i == len(kts) - 1
                        nc.tensor.matmul(banks[t][:, 0:n], x_hi[:, kt, ts], w_hi[:, u % 2, i, 0:n], start=st, stop=False)
                        nc.tensor.matmul(banks[t][:, 0:n], x_hi[:, kt, ts], w_lo[:, u % 2, i, 0:n], start=False, stop=False)
                        ins = nc.tensor.matmul(banks[t][:, 0:n], x_lo[:, kt, ts], w_hi[:, u % 2, i, 0:n], start=False, stop=en)
                if done is not None:
                    ins.then_inc(done, 1)

            def norm_transposes():
                m = k.m
                k.m += 1
                for t in range(NT):
                    pe.wait_ge(n_ready, 2 * m + t + 1)
                if k.sums:
                    pe.wait_ge(mod_out, k.sums)
                if k.f:
                    pe.wait_ge(split_full, k.f)
                for q in range(KT // 2):
                    for i in range(2):
                        for t in range(NT):
                            ins = nc.tensor.transpose(A[q][:, i * SEQ + t * P:i * SEQ + t * P + P],
                                                      n_st[:, t, (2 * q + i) * P:(2 * q + i + 1) * P], ident)
                    ins.then_inc(norm_T, 1)
                k.f += KT // 2

            def modulation(l, piece):
                j = int(piece[1])
                pe.wait_ge(acc_done, ADA_U * l + KT * (j + 1))
                if k.sums:
                    pe.wait_ge(mod_out, k.sums)
                if k.f:
                    pe.wait_ge(split_full, k.f)
                else:
                    pe.wait_ge(cols_ready, 1)
                src, banks = acc[:, (3 * l + j) % 2], SUM_BANKS[l, piece]
                if piece[0] == "r":
                    for i in range(2):
                        o = (0, D)[j - 1] + 512 * i
                        nc.tensor.matmul(banks[i], ones, src[:, o:o + 512], start=True, stop=True).then_inc(sums_done, 1)
                        k.sums += 1
                    return
                blocks = [(c, src, c) for c in range(2 * KT)] if j == 0 else [(c, src, c + (KT if j == 1 else 0)) for c in range(KT)]
                if l == LAT and j == 0:
                    pe.wait_ge(accc_done, KT)
                    blocks += [(2 * KT + c, acc_c, c) for c in range(2 * KT)]
                for dst, x, c in blocks:
                    ins = nc.tensor.matmul(banks[0][:, dst:dst + 1], x[:, c * P:c * P + P], ones[:, 0:1], start=True, stop=True)
                ins.then_inc(sums_done, 1)
                k.sums += 1

            def step_sb(step, g, evac):
                n = k.group + g
                ns = k.sb + g
                if step == "T":
                    pe.wait_ge(free_act, evac)
                    if ns:
                        pe.wait_ge(d_ready, 3 * ns)
                    for what in range(2):
                        for a in range(2):
                            for t in range(NT):
                                ins = nc.tensor.transpose(A[what][:, a * SEQ + t * P:a * SEQ + t * P + P],
                                                          qk_st[:, g % 2, t, 256 * what + a * P:256 * what + a * P + P], ident)
                        ins.then_inc(qkT_done, 1)
                elif step == "S":
                    pe.wait_ge(qT_ready, n + 1)
                    pe.wait_ge(kT_ready, k.kt + g + 1)
                    pe.wait_ge(cast_ready, 2)
                    if k.f:
                        pe.wait_ge(split_full, k.f)
                    for h in range(GROUP):
                        r = slice(HD * (h % 2), HD * (h % 2) + HD)
                        o = A[2 + h % 2][:, h // 2 * P:h // 2 * P + P]
                        nc.tensor.matmul(o, kT[r, h // 2, P:2 * P], qT[r, h // 2, P:2 * P], start=True, stop=False)
                        ins = nc.tensor.matmul(o, ident_b, m_sb, start=False, stop=True)
                    ins.then_inc(z_done, 1)
                    for h in range(GROUP):
                        r = slice(HD * (h % 2), HD * (h % 2) + HD)
                        o = A[h % 2][:, (h // 2) * SEQ:(h // 2) * SEQ + SEQ]
                        nc.tensor.matmul(o, kT[r, h // 2, 0:P], qT[r, h // 2, :], start=True, stop=False)
                        ins = nc.tensor.matmul(o[:, 0:P], ident_b, m_sb, start=False, stop=True)
                        if h >= 2:
                            ins.then_inc(z_done, 1)
                elif step == "C":
                    pe.wait_ge(sp_ready, 3 * ns + 1)
                    nc.tensor.matmul(A[2], tri, e_sb[:, 2], start=True, stop=True).then_inc(r_done, 1)
                    for b in range(2):
                        pe.wait_ge(sp_ready, 3 * ns + 2 + b)
                        nc.tensor.matmul(A[b], tri, e_sb[:, b], start=True, stop=False)
                        nc.tensor.matmul(A[b].rearrange("p (h n) -> p h n", h=2)[:, :, P:SEQ], ones,
                                         e_sb[:, 2, 256 * b:256 * b + 256].rearrange("p (h n) -> p h n", h=2),
                                         start=False, stop=True).then_inc(r_done, 1)
                elif step == "V":
                    weighted_values(n, g, evac, "sb")

            def weighted_values(n, g, evac, kind):
                pe.wait_ge(aT_ready, 3 * n + 3)
                pe.wait_ge(free_act, evac)
                v = v_st[:, 0 if kind == "swa" else g // 2]
                for i in range(2):
                    for par in range(2):
                        c = HD * (g // 2) if kind == "swa" else 256 * (g % 2) + HD * (2 * i + par)
                        o = A[3][HD * par:HD * par + HD, SEQ * i:SEQ * i + SEQ]
                        nc.tensor.matmul(o, v[:, 0, c:c + HD], aT[:, par, i * SEQ:i * SEQ + SEQ], start=True, stop=False)
                        ins = nc.tensor.matmul(o[:, P:SEQ], v[:, 1, c:c + HD], aT[:, 2, SEQ * par + P * i:SEQ * par + P * i + P], start=False, stop=True)
                ins.then_inc(av_done, 1)
                k.f += 1

            def step_softmax(step, g, kind, evac):
                if step == "N":
                    k.norms += 1
                    k.normed[g] = k.norms
                    return
                if g == "kv":
                    pe.wait_ge(qk_ready, k.normed["kv"])
                    for a in range(2):
                        for t in range(NT):
                            ins = nc.tensor.transpose(A[1][:, a * SEQ + t * P:a * SEQ + t * P + P],
                                                      qk_st[:, 1, t, 256 + a * P:256 + a * P + P], ident)
                    ins.then_inc(kvT_done, 1)
                    return
                n = k.group + g
                if step == "T":
                    if n:
                        pe.wait_ge(aT_ready, 3 * n)
                    pe.wait_ge(qk_ready, k.normed[2 * (g // 2) if kind == "swa" else g])
                    b, c = staged(kind, g)
                    for what in range(1 if kind == "swa" else 2):
                        for a in range(2):
                            for t in range(NT):
                                ins = nc.tensor.transpose(A[what][:, a * SEQ + t * P:a * SEQ + t * P + P],
                                                          qk_st[:, b, t, c + 256 * what + a * P:c + 256 * what + a * P + P], ident)
                        ins.then_inc(qkT_done, 2 if kind == "swa" else 1)
                elif step == "S":
                    pe.wait_ge(qT_ready, n + 1)
                    if kind == "swa":
                        pe.wait_ge(kvT_ready, k.swa + 1)
                    else:
                        pe.wait_ge(kT_ready, k.kt + g + 1)
                    if k.f:
                        pe.wait_ge(split_full, k.f)
                    for t in range(NT):
                        nk = P * (t + 1)
                        for h in range(GROUP):
                            r = slice(HD * (h % 2), HD * (h % 2) + HD)
                            o = A[2 - 2 * t + h % 2][:, h // 2 * nk:(h // 2 + 1) * nk]
                            nc.tensor.matmul(o, qT[r, h // 2, t * P:t * P + P], kT[r, g // 2 if kind == "swa" else h // 2, 0:nk],
                                             start=True, stop=False)
                            if t and kind == "swa":
                                ins = nc.tensor.matmul(o, ident_b, m_window.rearrange("p c n -> p (c n)"), start=False, stop=True)
                            else:
                                ins = nc.tensor.matmul(o[:, t * P:t * P + P], ident_b, m_causal, start=False, stop=True)
                        ins.then_inc(s_done, 1)
                elif step == "C":
                    pe.wait_ge(pn_ready, 3 * (k.sm + g) + 3)
                    for h in range(GROUP):
                        par, i = h % 2, h // 2
                        ins = nc.tensor.transpose(A[2][:, SEQ * par + P * i:SEQ * par + P * i + P], z_sb[:, par, SEQ * i + P:SEQ * i + SEQ], ident)
                    ins.then_inc(pT_done, 1)
                    for par in range(2):
                        for i in range(2):
                            nc.tensor.transpose(A[par][:, SEQ * i:SEQ * i + P], z_sb[:, 2, SEQ * par + P * i:SEQ * par + P * i + P], ident)
                            ins = nc.tensor.transpose(A[par][:, SEQ * i + P:SEQ * i + SEQ], z_sb[:, par, SEQ * i:SEQ * i + P], ident)
                        ins.then_inc(pT_done, 1)
                elif step == "V":
                    weighted_values(n, g, evac, kind)

            def attend(kind, step, g, evac):
                if kind == "sb":
                    step_sb(step, g, evac["v", g // 2] if step == "V" else evac["qk", g])
                else:
                    step_softmax(step, g, kind, evac["kv", 0] if kind == "swa" else evac.get(("v", (0 if g == "kv" else g // 2))))

            pe.wait_ge(const_in, 48)
            nc.tensor.transpose(A[0][:, 0:NCOL], cols_in, ident[0:NCOL, 0:NCOL])
            nc.tensor.transpose(A[0][:, NCOL:NCOL + 36], cols_in2, ident[0:36, 0:36]).then_inc(cols_T, 1)
            modulation(0, "c0")
            for l in range(DEPTH):
                kind, _, _ = mixer(l)
                norm_transposes()
                f_h = k.f
                panels = qkv_panels(kind)
                evac = {}
                pns = []
                f_o = {}
                for n in range(2 * len(panels)):
                    pi, h = n // 2, n % 2
                    what, g, _ = panels[pi]
                    if h == 0:
                        pns.append(k.panel("act"))
                        evac[what, g] = k.free_act
                        wait_panel_free(pns[-1])
                    pe.wait_ge(split_lo, f_h - 2 + 2 * h)
                    unit(h_hi, h_lo, range(4 * h, 4 * h + 4), G[2 * (pns[-1] % 2):2 * (pns[-1] % 2) + 2], h == 0, h == 1,
                         width(panels[pi]))
                    for step, g in SLOTS[kind].get(n, []):
                        attend(kind, step, g, evac)
                        if step == "V":
                            f_o[g] = k.f
                po = [k.panel("dve"), k.panel("dve")]
                n = 2 * len(panels)
                for h in range(2):
                    pe.wait_ge(split_lo, f_o[2 * h + 1])
                    for j in range(2):
                        if h == 0:
                            wait_panel_free(po[j])
                        unit(act_hi, act_lo, range(4 * h, 4 * h + 4), G[2 * (po[j] % 2):2 * (po[j] % 2) + 2], h == 0, h == 1)
                        for step, g in SLOTS[kind].get(n, []):
                            attend(kind, step, g, evac)
                            if step == "V":
                                f_o[g] = k.f
                        if l == 0 and n == 2 * len(panels) + 1:
                            modulation(0, "r1")
                            modulation(0, "c1")
                        n += 1
                k.end_mixer(kind)
                if l == 0:
                    modulation(0, "c2")
                    modulation(0, "r2")
                norm_transposes()
                f_h = k.f

                def act_transposes(p):
                    pe.wait_ge(act_ready, (FF // 256) * l + p + 1)
                    pe.wait_ge(split_full, k.f - 1)
                    for a in range(2):
                        for t in range(NT):
                            ins = nc.tensor.transpose(A[p % 2][:, a * SEQ + t * P:a * SEQ + t * P + P], act_st[:, t, a * P:a * P + P], ident)
                    ins.then_inc(actT_done, 1)
                    k.f += 1

                for p in range(FF // 256):
                    pn = k.panel("dve")
                    wait_panel_free(pn)
                    for h in range(2):
                        pe.wait_ge(split_lo, f_h - 2 + 2 * h)
                        unit(h_hi, h_lo, range(4 * h, 4 * h + 4), G[2 * (pn % 2):2 * (pn % 2) + 2], h == 0, h == 1)
                        if h == 0 and p >= 1:
                            act_transposes(p - 1)
                    if (l, ("up", p)) in SUMS and p < FF // 256 - 1:
                        modulation(l + 1, SUMS[l, ("up", p)])
                f_a = k.f + 1
                for j in range(2):
                    pn = k.panel("dve")
                    wait_panel_free(pn)
                    for h in range(6):
                        kts = range(4 * h, min(4 * h + 4, FFT))
                        pe.wait_ge(split_lo, f_a - FF // 256 + (kts[-1] // 2 + 1))
                        unit(act_hi, act_lo, kts, G[2 * (pn % 2):2 * (pn % 2) + 2], h == 0, h == 5)
                        if j == 0 and h == 0:
                            act_transposes(FF // 256 - 1)
                            if (l, ("up", FF // 256 - 1)) in SUMS:
                                modulation(l + 1, SUMS[l, ("up", FF // 256 - 1)])
                        if (l, ("down", 6 * j + h)) in SUMS:
                            modulation(l + 1, SUMS[l, ("down", 6 * j + h)])
                modulation(l + 1, "c2")
                modulation(l + 1, "r2")

            norm_transposes()
            norm_transposes()
            f_h = k.f

            def lat_step(step, s):
                if step == "N":
                    k.norms += 1
                elif step == "T":
                    pe.wait_ge(split_full, k.f)
                    pe.wait_ge(qk_ready, k.norms)
                    for g in range(2):
                        for t in range(4):
                            ins = nc.tensor.transpose(A[g][:, t * P:t * P + P], kdup[:, t, g * P:g * P + P], ident)
                        ins.then_inc(ltT_done, 1)
                    for b in range(2):
                        for i in range(2):
                            for t in range(NT):
                                ins = nc.tensor.transpose(A[2 + b][:, i * SEQ + t * P:i * SEQ + t * P + P], aq[:, t, (2 * b + i) * P:(2 * b + i + 1) * P], ident)
                        ins.then_inc(ltT_done, 1)
                    pe.wait_ge(kq_act, 2)
                    pe.wait_ge(kq_dve, 2)
                    pe.wait_ge(masks_ready, 1)
                elif step == "S":
                    if s:
                        pe.wait_ge(split_full, k.f)
                    for t in range(NT):
                        for r in range(2):
                            hr = slice(HD * r, HD * r + HD)
                            b = 2 * t + r
                            nc.tensor.matmul(A[b], lqT[hr, s, t * P:t * P + P], lkT[hr, s // 2], start=True, stop=False)
                            nc.tensor.matmul(A[b][:, (1 - t) * P:(2 - t) * P], ident_b, m_from if t else m_causal, start=False, stop=True).then_inc(ws_done, 1)
                elif step == "P":
                    pe.wait_ge(wn_ready, s + 1)
                    for kt in range(4):
                        for b in range(4):
                            ins = nc.tensor.transpose(A[kt][:, b * P:b * P + P], p_sb[:, b, kt * P:kt * P + P], ident)
                        ins.then_inc(wpT_done, 1)
                elif step == "V":
                    pe.wait_ge(waT_act, 2 * s + 2)
                    pe.wait_ge(waT_dve, 2 * s + 2)
                    for r in range(2):
                        for kt in range(4):
                            v = (kva_x, kva_c)[kt // 2][:, kt % 2, P + HD * (s // 2):P + HD * (s // 2) + HD]
                            p = laT[:, kt].rearrange("p (t r n) -> p r t n", t=NT, r=2)[:, r]
                            ins = nc.tensor.matmul(A[0][HD * r:HD * r + HD, 0:SEQ].rearrange("p (t n) -> p t n", t=NT), v, p,
                                                   start=kt == 0, stop=kt == 3)
                    ins.then_inc(woT_done, 1)
                    k.f += 1
                elif step == "X":
                    x = CONV[s][0]
                    pe.wait_ge(split_full, k.f)
                    pe.wait_ge(free_act, lat_free["dq" if s == 4 else "dv"])
                    if s >= 2:
                        pe.wait_ge(cb_ready, s - 1)
                    for a in range(4):
                        for t in range(NT):
                            ins = nc.tensor.transpose(A[2 * (s % 2) + a // 2][:, SEQ * (a % 2) + t * P:SEQ * (a % 2) + t * P + P], x[:, t, a * P:a * P + P], ident)
                    ins.then_inc(cvT_done, 1)
                elif step == "Y":
                    pe.wait_ge(cs_ready, s + 1)
                    for t in range(NT):
                        for a in range(4):
                            ins = nc.tensor.transpose(A[2 * (s % 2) + t][:, a * P:a * P + P], conv_t[:, s % 2, a, t * P:t * P + P], ident)
                    ins.then_inc(cvB_done, 1)
                elif step == "L":
                    pe.wait_ge(cb_ready, 5)
                    pe.wait_ge(gates_ready, 1)
                    pe.wait_ge(lat_in, 128)
                    for d in range(2):
                        for i, m_ in enumerate((tri_dir, later_dir)):
                            nc.tensor.matmul(A[0][:, 64 * i + 32 * d:64 * i + 32 * d + 32].rearrange("p (s h) -> p s h", s=4), m_[:, d],
                                             g_all[:, :, 8 * d:8 * d + 8], start=True, stop=True)
                        for rd in range(4):
                            for st in range(2):
                                c = 2 * rd + st
                                ins = nc.tensor.matmul(A[1][CH * d:CH * d + CH, 8 * c:8 * c + 8], half[:, st if d == 0 else 1 - st],
                                                       g_all[:, delta_tile(rd, d)[1], 8 * d:8 * d + 8], start=True, stop=True)
                    ins.then_inc(gsum_done, 1)
                elif step == "W":
                    pe.wait_ge(eg_ready, 1)
                    for i, x in enumerate((dk_c, dk_x, dq_x)):
                        pe.wait_ge(l2_ready, i + 1)
                        if i == 2:
                            pe.wait_ge(dT_act, 1)
                            pe.wait_ge(dT_dve, 1)
                        for b in range(2):
                            for a in range(2):
                                for t in range(NT):
                                    ins = nc.tensor.transpose(KQ_BANKS[i][b][:, a * SEQ + t * P:a * SEQ + t * P + P],
                                                              x[:, t, (2 * b + a) * P:(2 * b + a + 1) * P], ident)
                            ins.then_inc(dT_done, 1)

            lat_free = {}
            for pi, (what, _, n, both) in enumerate(LAT_PANELS):
                banks = []
                for _ in range(2 if both else 1):
                    pn = k.panel("act")
                    wait_panel_free(pn)
                    banks.append(G[2 * (pn % 2):2 * (pn % 2) + 2])
                lat_free[what] = k.free_act
                for h in range(2):
                    pe.wait_ge(split_lo, f_h - 2 + 2 * h)
                    kts = range(4 * h, 4 * h + 4)
                    unit(h_hi, h_lo, kts, banks[0], h == 0, h == 1, n, None if both else gemm_done)
                    if both:
                        k.u -= 1
                        unit(act_hi, act_lo, kts, banks[1], h == 0, h == 1, n)
                    for step, s in LAT_SLOTS.get(2 * pi + h, []):
                        lat_step(step, s)
            pe.wait_ge(free_act, k.free_act)
            pe.wait_ge(dT_act, 3)
            pe.wait_ge(dT_dve, 3)
            pe.wait_ge(eg_ready, 1)
            pe.wait_ge(beg_ready, 1)

            def decay(bank, d, st, r, mask, with_beta):
                for i in range(4):
                    h = 2 * i + r
                    o = bank[:, i * P:i * P + P]
                    if with_beta:
                        nc.tensor.matmul(o, lnb_G[:, d, st, h:h + 1].broadcast_to([P, P]), ident, start=True, stop=False)
                    else:
                        nc.tensor.matmul(o, g_all[:, st, DNH * d + h:DNH * d + h + 1].broadcast_to([P, P]), tri_dir[:, d], start=True, stop=False)
                    ins = nc.tensor.matmul(o, ident_b, mask[:, d], start=False, stop=True)
                return ins

            def dots(bank, kT_s, other, t, r):
                for i in range(4):
                    hr = slice(HD * r, HD * r + HD)
                    ins = nc.tensor.matmul(bank[:, i * P:i * P + P], kT_s[hr, i, t * P:t * P + P], other[hr, i, t * P:t * P + P], start=True, stop=True)
                return ins

            def four(bank, lhsT, rhs):
                for i in range(4):
                    sl = slice(P * i, P * i + P)
                    ins = nc.tensor.matmul(bank[:, sl], lhsT[:, sl], rhs[:, sl], start=True, stop=True)
                return ins

            for rd in range(4):
                lat = rd >= 2
                kT_s = kT_x if lat else kT_c
                if rd:
                    pe.wait_ge(S_ready, 2 * rd)
                if rd == 3:
                    pe.wait_ge(oacc_ready, 1)
                for c in range(4):
                    d, r = c // 2, c % 2
                    t, st = delta_tile(rd, d)
                    decay(A[c], d, st, r, m_strict, True).then_inc(e_done, 1)
                    dots(G[c], kT_s, kT_s, t, r).then_inc(kk_done, 1)
                if lat:
                    for c in range(4):
                        d, r = c // 2, c % 2
                        t, st = delta_tile(rd, d)
                        pe.wait_ge(E_ready, 4 * rd + c + 1)
                        decay(A[c], d, st, r, m_incl, False).then_inc(in_done, 1)
                        pe.wait_ge(LT_ready, 4 * rd + c + 1)
                        dots(G[c], kT_s, qT_x, t, r).then_inc(id_done, 1)
                for lev in range(LEVELS):
                    for c in range(4):
                        if lev == 0:
                            if lat:
                                pe.wait_ge(ie_ready, 4 * (rd - 2) + c + 1)
                            pe.wait_ge(LT_ready, 4 * rd + c + 1)
                            for i in range(4):
                                ins = nc.tensor.transpose(A[c][:, i * P:i * P + P], LT[:, c, i * P:i * P + P], ident)
                            ins.then_inc(y_done, 1)
                        else:
                            if lev == 1:
                                pe.wait_ge(Z_ready, solved(rd, 0, c))
                            else:
                                pe.wait_ge(X_ready, joined(rd, lev - 1, c, LEVELS - 1))
                            four(A[c], LT[:, c], X[:, c]).then_inc(y_done, 1)
                    for c in range(4 if lev else 0):
                        if lev == 1 and lat:
                            pe.wait_ge(intra_ready, 4 * (rd - 2) + c + 1)
                        pe.wait_ge(Z_ready, solved(rd, lev, c))
                        if lev > 1:
                            pe.wait_ge(XT_ready, joined(rd, lev - 1, c))
                        if lev < LEVELS - 1:
                            four(A[c], XT[:, c], Z[:, c]).then_inc(x_done, 1)
                        four(G[c], Z[:, c], XT[:, c]).then_inc(xT_done, 1)
                pe.wait_ge(XT_ready, joined(rd, LEVELS - 1, 3))
                pe.wait_ge(prep_ready, 2 * rd + 2)
                for d in range(2):
                    for h in range(DNH):
                        i, r = h // 2, h % 2
                        ins = nc.tensor.matmul(A[r][CH * d:CH * d + CH, i * P:i * P + P], bek[:, d, HD * h:HD * h + HD], XT[:, 2 * d + r, i * P:i * P + P],
                                               start=True, stop=True)
                ins.then_inc(wT_done, 1)
                for d in range(2):
                    for h in range(DNH):
                        i, r = h // 2, h % 2
                        ins = nc.tensor.matmul(A[2 + d][:, hcol(h):hcol(h) + HD], XT[:, 2 * d + r, i * P:i * P + P], bv[:, d, HD * h:HD * h + HD],
                                               start=True, stop=True)
                    ins.then_inc(uv_done, 1)
                if lat:
                    for r in range(2):
                        for d in range(2):
                            for i in range(4):
                                h = 2 * i + r
                                ins = nc.tensor.matmul(G[r][CH * d:CH * d + CH, i * P:i * P + P], q_dec[:, d, HD * h:HD * h + HD], ident,
                                                       start=True, stop=True)
                        ins.then_inc(qdT_done, 1)
                pe.wait_ge(wT_ready, rd + 1)
                pe.wait_ge(uv_ready, 2 * rd + 2)
                if lat:
                    pe.wait_ge(qdT_ready, 2 * (rd - 2) + 2)
                for step in range(2):
                    c = 2 * rd + step
                    if c:
                        pe.wait_ge(S_ready, c)
                    else:
                        pe.wait_ge(state_zero, 1)
                    for d in range(2):
                        ch = step if d == 0 else 1 - step
                        cs, ds = slice(CH * ch, CH * ch + CH), slice(CH * d, CH * d + CH)
                        for h in range(DNH):
                            hs = slice(hcol(h), hcol(h) + HD)
                            i, r = h // 2, h % 2
                            ins = nc.tensor.matmul(A[0][cs, hs], wT[ds, r, i * P + CH * ch:i * P + CH * ch + CH], state[ds, hs], start=True, stop=True)
                    ins.then_inc(wS_done, 1)
                    if lat:
                        for d in range(2):
                            ch = step if d == 0 else 1 - step
                            cs, ds = slice(CH * ch, CH * ch + CH), slice(CH * d, CH * d + CH)
                            for h in range(DNH):
                                hs = slice(hcol(h), hcol(h) + HD)
                                i, r = h // 2, h % 2
                                nc.tensor.matmul(A[1 + d][cs, hs], q_decT[ds, r, i * P + CH * ch:i * P + CH * ch + CH], state[ds, hs], start=True, stop=True)
                    pe.wait_ge(u_ready, c + 1)
                    for d in range(2):
                        ch = step if d == 0 else 1 - step
                        cs, ds = slice(CH * ch, CH * ch + CH), slice(CH * d, CH * d + CH)
                        if c < 7:
                            for h in range(DNH):
                                hs = slice(hcol(h), hcol(h) + HD)
                                ins = nc.tensor.matmul(A[3][ds, hs], k_tail[cs, d, HD * h:HD * h + HD], u_st[cs, step, hs], start=True, stop=True)
                    if c < 7:
                        ins.then_inc(su_done, 1)
                    if lat:
                        for d in range(2):
                            ch = step if d == 0 else 1 - step
                            cs = slice(CH * ch, CH * ch + CH)
                            for h in range(DNH):
                                hs = slice(hcol(h), hcol(h) + HD)
                                i, r = h // 2, h % 2
                                ins = nc.tensor.matmul(G[d][cs, hs], intraT[cs, d, r, i * P + CH * ch:i * P + CH * ch + CH], u_st[cs, step, hs],
                                                       start=True, stop=True)
                        if step:
                            ins.then_inc(o_done, 1)
            pe.wait_ge(yd_ready, 1)
            for q in range(2):
                for a in range(2):
                    for t in range(NT):
                        ins = nc.tensor.transpose(A[q][:, a * SEQ + t * P:a * SEQ + t * P + P], dz[:, t, (2 * q + a) * P:(2 * q + a + 1) * P], ident)
                ins.then_inc(ydT_done, 1)
            k.f += 2
            f_y = k.f
            pe.wait_ge(split_lo, f_y)
            for n in range(4):
                pn = k.panel("dve")
                wait_panel_free(pn)
                unit(act_hi, act_lo, Y_ATTN if n < 2 else range(4, 8), G[2 * (pn % 2):2 * (pn % 2) + 2], True, True)
            pe.wait_ge(split_full, f_y)
            for q in range(4):
                pe.wait_ge(yy_ready, q // 2 + 1)
                for i in range(2):
                    for t in range(NT):
                        ins = nc.tensor.transpose(A[q][:, i * SEQ + t * P:i * SEQ + t * P + P], n_st[:, t, (2 * q + i) * P:(2 * q + i + 1) * P], ident)
                ins.then_inc(yT_done, 1)
            k.f += 4
            po = [k.panel("dve"), k.panel("dve")]
            for h in range(2):
                pe.wait_ge(split_lo, k.f - 2 + 2 * h)
                for j in range(2):
                    if h == 0:
                        wait_panel_free(po[j])
                    unit(h_hi, h_lo, range(4 * h, 4 * h + 4), G[2 * (po[j] % 2):2 * (po[j] % 2) + 2], h == 0, h == 1)
            norm_transposes()
            f_h = k.f

            def hidden_transposes(p):
                pe.wait_ge(hid_ready, p + 1)
                pe.wait_ge(split_full, k.f - 2)
                for q in range(2):
                    for a in range(2):
                        for t in range(NT):
                            ins = nc.tensor.transpose(A[2 * (p % 2) + q][:, a * SEQ + t * P:a * SEQ + t * P + P],
                                                      hid_st[:, t, (2 * q + a) * P:(2 * q + a + 1) * P], ident)
                    ins.then_inc(hidT_done, 1)
                k.f += 2

            for part in range(2):
                for p in range(4):
                    pn = k.panel("dve")
                    wait_panel_free(pn)
                    for h in range(2):
                        pe.wait_ge(split_lo, f_h - 2 + 2 * h)
                        unit(h_hi, h_lo, range(4 * h, 4 * h + 4), G[2 * (pn % 2):2 * (pn % 2) + 2], h == 0, h == 1)
                        if h == 0 and p >= 1:
                            hidden_transposes(4 * part + p - 1)
                f_a = k.f + 2
                for j in range(2):
                    pn = k.panel("dve")
                    wait_panel_free(pn)
                    for h in range(4):
                        pe.wait_ge(split_lo, f_a - 8 + 2 * (h + 1))
                        unit(act_hi, act_lo, range(4 * h, 4 * h + 4), G[2 * (pn % 2):2 * (pn % 2) + 2], h == 0, h == 3)
                        if j == 0 and h == 0:
                            hidden_transposes(4 * part + 3)


def kernel(**inputs):
    import concourse.bacc as _bacc
    from concourse.bass_utils import run_bass_kernel_spmd as _run

    nc = _bacc.Bacc("TRN2", target_bir_lowering=False, num_devices=1)
    arrays = {n: np.ascontiguousarray(v) for n, v in inputs.items()}
    cols = np.concatenate([arrays.pop(n).reshape(-1, P) for n in
                           ("norm_gain", "c", "c_2", "c_ctx_2", "g_norm1_2", "g_norm2_2")])
    arrays["cols"] = cols
    arrays["cols_2"] = arrays.pop("conv_w_2").reshape(36, P)
    i = np.arange(P)
    eye = np.eye(P, dtype=np.float32)
    one = np.ones((P, P), np.float32)
    tri = (i[:, None] >= i[None, :]).astype(np.float32)
    m_sb = np.where(i[:, None] < i[None, :], 0.0, NEG).astype(np.float32)
    m_causal = np.where(i[None, :] <= i[:, None], 0.0, NEG).astype(np.float32)
    m_prev = np.where(i[None, :] > i[:, None], 0.0, NEG).astype(np.float32)
    arrays["consts"] = np.stack([eye, one, tri, m_sb, m_prev, m_causal])
    freq = (np.float32(1.0) / np.float32(10000.0) ** (np.arange(0, HD, 2, dtype=np.float32) / np.float32(HD))).astype(np.float32)
    ang = np.arange(SEQ, dtype=np.float32)[:, None] * freq[None, :]
    cos, sin = np.cos(ang), np.sin(ang)
    arrays["rope"] = np.stack([np.concatenate([cos, cos], 1), np.concatenate([-sin, sin], 1)]).astype(np.float32)
    freq = (np.float32(10000.0) ** (-np.arange(16, dtype=np.float32) / np.float32(16))).astype(np.float32)
    pos = np.arange(SEQ)
    ang = [(pos // 64).astype(np.float32)[:, None] * freq[None, :], (pos % 64).astype(np.float32)[:, None] * freq[None, :]]
    arrays["rope_2"] = np.stack([np.concatenate([f(a) for a in ang for f in (np.cos, np.cos)], 1),
                                 np.concatenate([f(a) for a in ang for f in (lambda x: -np.sin(x), np.sin)], 1)]).astype(np.float32)
    a, b = i[:, None], i[None, :]
    same = a // CH == b // CH
    half = np.concatenate([np.repeat(i[:, None] // CH == h, CH, 1) for h in range(2)], 1)
    arrays["consts_2"] = np.stack([same & (a <= b), same & (a >= b), same & (a > b), same & (a < b), half]).astype(np.float32)
    lower = [(a // (2 * s) == b // (2 * s)) & (a // s % 2 == 1) & (b // s % 2 == 0) for s in (1, 2, 4, 8, 16, 32)]
    allow = lambda m: np.where(m, 0.0, NEG)
    arrays["masks_2"] = np.stack([m | (a == b) for m in lower + [m.T for m in lower]] + [allow(same & (a < b)), allow(same & (a > b)), allow(same & (a <= b)),
                                                                 allow(same & (a >= b)), allow(b >= a)]).astype(np.float32)
    keep = ["x", "cols", "consts", "rope", "ada_w", "ada_b", "ffn_w_gate", "ffn_w_up", "ffn_w_down", "sb_w_in", "sb_w_out",
            "moba_w_in", "moba_w_out", "moba_qk_gain", "swa_w_in", "swa_w_out", "swa_qk_gain", "swa_sinks",
            "ctx_2", "w_ada_2", "b_ada_2", "w_in_2", "q_norm_g_2", "k_norm_g_2", "attn_sink_2", "cols_2", "a_log_2", "dt_bias_2",
            "dn_norm_g_2", "w_br_attn_2", "w_br_dn_2", "w_out_2", "w_mlp1_2", "w_mlp2_2", "rope_2", "consts_2", "masks_2"]
    arrays = {n: arrays[n] for n in keep}
    w = {n: nc.dram_tensor(f"in_{n}", a.shape, mybir.dt.from_np(a.dtype), kind="ExternalInput").ap() for n, a in arrays.items()}
    out = nc.dram_tensor("out_x", (1, SEQ, D), F32, kind="ExternalOutput").ap()
    build(nc, w, out)
    r = _run(nc, [{f"in_{n}": a for n, a in arrays.items()}], core_ids=[0])
    return r.results[0]["out_x"]
```
